# Optimizing a Trainium2 kernel written in Bass

```python
import jax, jax.numpy as jnp
from jax import lax
import numpy as np
import math
import jax
import jax.numpy as jnp

D_MODEL = 1024
BATCH = 1
SEQ = 256
DEPTH = 2

D_CONV_A = 512
CONV_A_WIDTH = 3
D_CONV_B = 512
CONV_B_WIDTH = 31
N_HEADS = 16
HEAD_DIM = 64
D_ATTN = N_HEADS * HEAD_DIM
BLOCK_Q = 128
N_GROUPS = 4
EXPERTS_PER_GROUP = 8
N_EXPERTS = N_GROUPS * EXPERTS_PER_GROUP
TOP_K = 2
D_EXPERT = 512
ROW_CHUNK = 256
LN_EPS = 1e-5
DEEPNORM_ALPHA = (2 * DEPTH) ** 0.25
DEEPNORM_BETA = (8 * DEPTH) ** -0.25

N_EVEN = (DEPTH + 1) // 2
N_ODD = DEPTH // 2
D_IN_EVEN = 3 * D_CONV_A + 2 * D_CONV_B
D_MIX_EVEN = D_CONV_A + D_CONV_B


def layer_norm(x, g, b):
    xf = x.astype(jnp.float32)
    mu = jnp.mean(xf, axis=-1, keepdims=True)
    var = jnp.mean(jnp.square(xf - mu), axis=-1, keepdims=True)
    y = (xf - mu) * lax.rsqrt(var + LN_EPS)
    return (y * g + b).astype(x.dtype)

def causal_depthwise_conv(x, w):
    k = w.shape[0]
    return lax.conv_general_dilated(
        x, w[:, None, :].astype(x.dtype), window_strides=(1,), padding=[(k - 1, 0)],
        dimension_numbers=("NWC", "WIO", "NWC"), feature_group_count=x.shape[-1])

def conv_mixers(x, w_in, conv_a, conv_b_w, conv_b_bias, norm_b_g, norm_b_b, w_out):
    u = jnp.einsum("bsd,de->bse", x, w_in)
    a_b, a_c, a_v, b_val, b_gate = jnp.split(
        u, [D_CONV_A, 2 * D_CONV_A, 3 * D_CONV_A, 3 * D_CONV_A + D_CONV_B], axis=-1)
    y_a = a_b * causal_depthwise_conv(a_c * a_v, conv_a)
    g = b_val * jax.nn.sigmoid(b_gate)
    g = causal_depthwise_conv(g, conv_b_w) + conv_b_bias
    y_b = jax.nn.silu(layer_norm(g, norm_b_g, norm_b_b))
    return jnp.einsum("bse,ed->bsd", jnp.concatenate([y_a, y_b], axis=-1), w_out)

def stick_breaking_attention(x, w_qkv, w_o):
    b, s, _ = x.shape
    qkv = jnp.einsum("bsd,de->bse", x, w_qkv).reshape(b, s, 3, N_HEADS, HEAD_DIM)
    q = qkv[:, :, 0].transpose(0, 2, 1, 3)
    k = qkv[:, :, 1].transpose(0, 2, 1, 3)
    v = qkv[:, :, 2].transpose(0, 2, 1, 3)
    scale = HEAD_DIM ** -0.5
    outs = []
    for blk in range(s // BLOCK_Q):
        q0 = blk * BLOCK_Q
        kv_len = q0 + BLOCK_Q
        qb = q[:, :, q0:kv_len]
        kb = k[:, :, :kv_len]
        vb = v[:, :, :kv_len]
        z = jnp.einsum("bhqd,bhkd->bhqk", qb, kb,
                       preferred_element_type=jnp.float32) * scale
        t_idx = q0 + jnp.arange(BLOCK_Q)[:, None]
        s_idx = jnp.arange(kv_len)[None, :]
        causal = s_idx < t_idx
        log_keep = jnp.where(causal, jax.nn.log_sigmoid(-z), 0.0)
        later = lax.cumsum(log_keep, axis=3, reverse=True) - log_keep
        a = jnp.where(causal, jnp.exp(jax.nn.log_sigmoid(z) + later), 0.0)
        outs.append(jnp.einsum("bhqk,bhkd->bhqd", a.astype(vb.dtype), vb))
    o = jnp.concatenate(outs, axis=2).transpose(0, 2, 1, 3).reshape(b, s, D_ATTN)
    return jnp.einsum("bse,ed->bsd", o, w_o)

def hierarchical_moe(x, rg_w, rg_b, re_w, re_b, w_up, w_down):
    b, s, d = x.shape
    h = x.reshape(-1, d)
    t = h.shape[0]
    g_logits = jnp.matmul(h, rg_w).astype(jnp.float32) + rg_b
    grp = jnp.argmax(g_logits, axis=-1)
    g_gate = jnp.take_along_axis(jax.nn.softmax(g_logits, axis=-1), grp[:, None], axis=-1)
    e_logits = (jnp.matmul(h, re_w).astype(jnp.float32) + re_b).reshape(t, N_GROUPS, EXPERTS_PER_GROUP)
    e_logits = jnp.take_along_axis(e_logits, grp[:, None, None], axis=1)[:, 0]
    top_val, top_idx = lax.top_k(e_logits, TOP_K)
    weights = (g_gate * jax.nn.softmax(top_val, axis=-1)).reshape(-1)
    ids = (grp[:, None] * EXPERTS_PER_GROUP + top_idx).reshape(-1).astype(jnp.int32)
    n_assign = t * TOP_K
    order = jnp.argsort(ids)
    sorted_ids = ids[order]
    tok = order // TOP_K
    sizes = jnp.bincount(ids, length=N_EXPERTS)
    padded = (sizes + ROW_CHUNK - 1) // ROW_CHUNK * ROW_CHUNK
    pad_end = jnp.cumsum(padded)
    pad_start = pad_end - padded
    start = jnp.cumsum(sizes) - sizes
    dest = pad_start[sorted_ids] + jnp.arange(n_assign) - start[sorted_ids]
    n_chunks = -(-n_assign // ROW_CHUNK) + N_EXPERTS
    rows = jnp.zeros((n_chunks * ROW_CHUNK, d), h.dtype).at[dest].set(h[tok])
    chunk_expert = jnp.minimum(
        jnp.searchsorted(pad_end, jnp.arange(n_chunks) * ROW_CHUNK, side="right"), N_EXPERTS - 1)

    def expert_chunk(args):
        xc, e = args
        gate, up = jnp.split(jnp.matmul(xc, w_up[e]), 2, axis=-1)
        return jnp.matmul(jax.nn.silu(gate) * up, w_down[e])

    y_rows = lax.map(expert_chunk, (rows.reshape(n_chunks, ROW_CHUNK, d), chunk_expert))
    y = y_rows.reshape(-1, d)[dest] * weights[order][:, None].astype(h.dtype)
    out = jnp.zeros((t, d), h.dtype).at[tok].add(y)
    return out.reshape(b, s, d)

def first_inputs(seed: int = 0) -> dict:
    key = jax.random.key(seed)
    ks = jax.random.split(key, 24)
    nrm = jax.random.normal
    f32 = jnp.float32
    x = nrm(ks[0], (BATCH, SEQ, D_MODEL), f32)
    even_w_in = nrm(ks[1], (N_EVEN, D_MODEL, D_IN_EVEN), f32) * D_MODEL ** -0.5
    even_conv_a = nrm(ks[2], (N_EVEN, CONV_A_WIDTH, D_CONV_A), f32) * CONV_A_WIDTH ** -0.5
    even_conv_b_w = nrm(ks[3], (N_EVEN, CONV_B_WIDTH, D_CONV_B), f32) * CONV_B_WIDTH ** -0.5
    even_conv_b_bias = nrm(ks[4], (N_EVEN, D_CONV_B), f32) * 0.02
    even_norm_b_g = 1.0 + 0.1 * nrm(ks[5], (N_EVEN, D_CONV_B), f32)
    even_norm_b_b = 0.02 * nrm(ks[6], (N_EVEN, D_CONV_B), f32)
    even_w_out = nrm(ks[7], (N_EVEN, D_MIX_EVEN, D_MODEL), f32) * (D_MIX_EVEN ** -0.5 * DEEPNORM_BETA)
    v_scale = jnp.concatenate([jnp.ones((2 * D_ATTN,), f32), jnp.full((D_ATTN,), DEEPNORM_BETA, f32)])
    odd_w_qkv = nrm(ks[8], (N_ODD, D_MODEL, 3 * D_ATTN), f32) * D_MODEL ** -0.5 * v_scale
    odd_w_o = nrm(ks[9], (N_ODD, D_ATTN, D_MODEL), f32) * (D_ATTN ** -0.5 * DEEPNORM_BETA)
    ln_mix_g = 1.0 + 0.1 * nrm(ks[10], (DEPTH, D_MODEL), f32)
    ln_mix_b = 0.02 * nrm(ks[11], (DEPTH, D_MODEL), f32)
    ln_ffn_g = 1.0 + 0.1 * nrm(ks[12], (DEPTH, D_MODEL), f32)
    ln_ffn_b = 0.02 * nrm(ks[13], (DEPTH, D_MODEL), f32)
    router_group_w = nrm(ks[14], (DEPTH, D_MODEL, N_GROUPS), f32) * D_MODEL ** -0.5
    router_group_b = 0.01 * nrm(ks[15], (DEPTH, N_GROUPS), f32)
    router_expert_w = nrm(ks[16], (DEPTH, D_MODEL, N_EXPERTS), f32) * D_MODEL ** -0.5
    router_expert_b = 0.01 * nrm(ks[17], (DEPTH, N_EXPERTS), f32)
    expert_w_up = nrm(ks[18], (DEPTH, N_EXPERTS, D_MODEL, 2 * D_EXPERT), f32) * D_MODEL ** -0.5
    expert_w_down = nrm(ks[19], (DEPTH, N_EXPERTS, D_EXPERT, D_MODEL), f32) * (D_EXPERT ** -0.5 * DEEPNORM_BETA)
    return {"x": x, "even_w_in": even_w_in, "even_conv_a": even_conv_a,
            "even_conv_b_w": even_conv_b_w, "even_conv_b_bias": even_conv_b_bias,
            "even_norm_b_g": even_norm_b_g, "even_norm_b_b": even_norm_b_b,
            "even_w_out": even_w_out, "odd_w_qkv": odd_w_qkv, "odd_w_o": odd_w_o,
            "ln_mix_g": ln_mix_g, "ln_mix_b": ln_mix_b, "ln_ffn_g": ln_ffn_g, "ln_ffn_b": ln_ffn_b,
            "router_group_w": router_group_w, "router_group_b": router_group_b,
            "router_expert_w": router_expert_w, "router_expert_b": router_expert_b,
            "expert_w_up": expert_w_up, "expert_w_down": expert_w_down}

def first_block(x, even_w_in, even_conv_a, even_conv_b_w, even_conv_b_bias, even_norm_b_g,
              even_norm_b_b, even_w_out, odd_w_qkv, odd_w_o, ln_mix_g, ln_mix_b, ln_ffn_g,
              ln_ffn_b, router_group_w, router_group_b, router_expert_w, router_expert_b,
              expert_w_up, expert_w_down):
    for layer in range(DEPTH):
        i = layer // 2
        if layer % 2 == 0:
            mix = conv_mixers(x, even_w_in[i], even_conv_a[i], even_conv_b_w[i],
                              even_conv_b_bias[i], even_norm_b_g[i], even_norm_b_b[i],
                              even_w_out[i])
        else:
            mix = stick_breaking_attention(x, odd_w_qkv[i], odd_w_o[i])
        x = layer_norm(DEEPNORM_ALPHA * x + mix, ln_mix_g[layer], ln_mix_b[layer])
        ffn = hierarchical_moe(x, router_group_w[layer], router_group_b[layer],
                               router_expert_w[layer], router_expert_b[layer],
                               expert_w_up[layer], expert_w_down[layer])
        x = layer_norm(DEEPNORM_ALPHA * x + ffn, ln_ffn_g[layer], ln_ffn_b[layer])
    return x


N_HEADS_2 = D_MODEL // HEAD_DIM
MOBA_HEADS = N_HEADS_2 // 2
DIL_HEADS = N_HEADS_2 - MOBA_HEADS
MOBA_BLOCK = 256
MOBA_TOPK = 3
MOBA_QCHUNK = 16
DIL_PAIRS = ((128, 1), (512, 4), (2048, 16))
DIL_BLOCK = 128
NSA_HEADS = N_HEADS_2
NSA_GROUPS = 4
NSA_HPG = NSA_HEADS // NSA_GROUPS
NSA_CMP_LEN = 32
NSA_CMP_STRIDE = 16
NSA_CMP_HIDDEN = 2 * HEAD_DIM
NSA_SEL_BLOCK = 64
NSA_SEL_TOPN = 16
NSA_WINDOW = 512
NSA_WIN_BLOCK = 128
NSA_QCHUNK = 32
NSA_FORCE = 1.0e6
REL_BUCKETS = 32
REL_MAX_DIST = 2048
FFN_HIDDEN = -((-8 * D_MODEL) // (3 * 256)) * 256
PLE_DIM = 256
N_EVEN_2 = (DEPTH + 1) // 2
N_ODD_2 = DEPTH // 2
RMS_EPS = 1e-6
ATTN_SCALE = HEAD_DIM ** -0.5
F32 = jnp.float32


def _rms(x, g):
    xf = x.astype(F32)
    y = xf * lax.rsqrt(jnp.mean(xf * xf, axis=-1, keepdims=True) + RMS_EPS)
    return (y * g.astype(F32)).astype(x.dtype)

def _heads(t, n):
    B, S, _ = t.shape
    return t.reshape(B, S, n, HEAD_DIM).transpose(0, 2, 1, 3)

def _rel_bucket(dist):
    n = jnp.maximum(dist, 0)
    exact = REL_BUCKETS // 2
    nf = jnp.maximum(n, 1).astype(F32)
    large = exact + (jnp.log(nf / exact) / math.log(REL_MAX_DIST / exact) * (REL_BUCKETS - exact)).astype(jnp.int32)
    return jnp.where(n < exact, n, jnp.minimum(large, REL_BUCKETS - 1))

def _masked_softmax(s, mask):
    s = jnp.where(mask, s.astype(F32), -jnp.inf)
    m = jnp.max(s, axis=-1, keepdims=True)
    m = jnp.where(jnp.isfinite(m), m, 0.0)
    e = jnp.exp(s - m)
    l = jnp.sum(e, axis=-1, keepdims=True)
    p = e / jnp.where(l > 0, l, 1.0)
    return p, (m + jnp.log(l))[..., 0]

def _moba(q, k, v, tab):
    B, H, S, hd = q.shape
    nb = -(-S // MOBA_BLOCK)
    padw = ((0, 0), (0, 0), (0, nb * MOBA_BLOCK - S), (0, 0))
    kb = jnp.pad(k, padw).reshape(B, H, nb, MOBA_BLOCK, hd)
    vb = jnp.pad(v, padw).reshape(B, H, nb, MOBA_BLOCK, hd)
    kmean = jnp.mean(kb.astype(F32), axis=3)
    own = jnp.arange(S) // MOBA_BLOCK
    gate = jnp.einsum('bhsd,bhnd->bhsn', q.astype(F32), kmean)
    gate = jnp.where(jnp.arange(nb)[None, :] < own[:, None], gate, -jnp.inf)
    n_sel = min(MOBA_TOPK, nb)
    _, sel = lax.top_k(gate, n_sel)
    sel_ok = sel < own[:, None]
    nc = S // MOBA_QCHUNK

    def to_chunks(t):
        return jnp.moveaxis(t.reshape(B, H, nc, MOBA_QCHUNK, *t.shape[3:]), 2, 0)

    b_ix = jnp.arange(B)[:, None, None, None]
    h_ix = jnp.arange(H)[None, :, None, None]
    a_blk = jnp.arange(MOBA_BLOCK)

    def chunk(args):
        c, qc, sc, okc = args
        t = c * MOBA_QCHUNK + jnp.arange(MOBA_QCHUNK)
        j = (c * MOBA_QCHUNK) // MOBA_BLOCK
        k_own = lax.dynamic_index_in_dim(kb, j, axis=2, keepdims=False)
        v_own = lax.dynamic_index_in_dim(vb, j, axis=2, keepdims=False)
        d_own = t[:, None] - (j * MOBA_BLOCK + a_blk)[None, :]
        s_own = jnp.einsum('bhqd,bhkd->bhqk', qc, k_own).astype(F32) * ATTN_SCALE + tab[:, _rel_bucket(d_own)].astype(F32)
        m_own = jnp.broadcast_to(d_own >= 0, s_own.shape)
        k_sel = kb[b_ix, h_ix, sc].reshape(B, H, MOBA_QCHUNK, n_sel * MOBA_BLOCK, hd)
        v_sel = vb[b_ix, h_ix, sc].reshape(B, H, MOBA_QCHUNK, n_sel * MOBA_BLOCK, hd)
        kpos = (sc[..., None] * MOBA_BLOCK + a_blk).reshape(B, H, MOBA_QCHUNK, n_sel * MOBA_BLOCK)
        s_sel = jnp.einsum('bhqd,bhqkd->bhqk', qc, k_sel).astype(F32) * ATTN_SCALE + tab[h_ix, _rel_bucket(t[:, None] - kpos)].astype(F32)
        m_sel = jnp.repeat(okc, MOBA_BLOCK, axis=-1)
        pr, _ = _masked_softmax(jnp.concatenate([s_own, s_sel], axis=-1), jnp.concatenate([m_own, m_sel], axis=-1))
        p_own = pr[..., :MOBA_BLOCK].astype(v.dtype)
        p_sel = pr[..., MOBA_BLOCK:].astype(v.dtype)
        return jnp.einsum('bhqk,bhkd->bhqd', p_own, v_own) + jnp.einsum('bhqk,bhqkd->bhqd', p_sel, v_sel)

    out = lax.map(chunk, (jnp.arange(nc), to_chunks(q), to_chunks(sel), to_chunks(sel_ok)))
    return jnp.moveaxis(out, 0, 2).reshape(B, H, S, hd)

def _stride_split(t, dil, L):
    B, H, S, hd = t.shape
    t = jnp.pad(t, ((0, 0), (0, 0), (0, L * dil - S), (0, 0)))
    return t.reshape(B, H, L, dil, hd).transpose(0, 1, 3, 2, 4)

def _band(t):
    prev = jnp.pad(t, ((0, 0), (0, 0), (0, 0), (1, 0), (0, 0), (0, 0)))[:, :, :, :-1]
    return jnp.concatenate([prev, t], axis=4)

def _dilated(q, k, v, tab):
    B, H, S, hd = q.shape
    blk = DIL_BLOCK
    outs, lses = [], []
    for window, dil in DIL_PAIRS:
        steps = window // dil
        L = -(-S // (dil * blk)) * blk
        nbk = L // blk
        qs = _stride_split(q, dil, L).reshape(B, H, dil, nbk, blk, hd)
        ks = _stride_split(k, dil, L).reshape(B, H, dil, nbk, blk, hd)
        vs = _stride_split(v, dil, L).reshape(B, H, dil, nbk, blk, hd)
        step = jnp.arange(blk)[:, None] + blk - jnp.arange(2 * blk)[None, :]
        key_ok = (jnp.arange(nbk)[:, None] * blk - blk + jnp.arange(2 * blk)[None, :]) >= 0
        mask = ((step >= 0) & (step <= steps))[None] & key_ok[:, None, :]
        bias = tab[:, _rel_bucket(step * dil)].astype(F32)
        s = jnp.einsum('bhrjqd,bhrjkd->bhrjqk', qs, _band(ks)).astype(F32) * ATTN_SCALE + bias[None, :, None, None]
        pr, lse = _masked_softmax(s, mask)
        o = jnp.einsum('bhrjqk,bhrjkd->bhrjqd', pr.astype(v.dtype), _band(vs))
        outs.append(o.reshape(B, H, dil, L, hd).transpose(0, 1, 3, 2, 4).reshape(B, H, L * dil, hd)[:, :, :S])
        lses.append(lse.reshape(B, H, dil, L).transpose(0, 1, 3, 2).reshape(B, H, L * dil)[:, :, :S])
    w = jax.nn.softmax(jnp.stack(lses), axis=0)
    o = jnp.einsum('nbhs,nbhsd->bhsd', w, jnp.stack(outs).astype(F32))
    return o.astype(q.dtype)

def _compress(t, pos_emb, w1, b1, w2, b2):
    B, G, S, hd = t.shape
    nc = (S - NSA_CMP_LEN) // NSA_CMP_STRIDE + 1
    idx = jnp.arange(nc)[:, None] * NSA_CMP_STRIDE + jnp.arange(NSA_CMP_LEN)[None, :]
    blocks = (t[:, :, idx] + pos_emb).reshape(B, G, nc, NSA_CMP_LEN * hd)
    return jax.nn.gelu(blocks @ w1 + b1) @ w2 + b2

def _nsa(q, kc, vc, ks, vs, kw, vw, gates, tab):
    B, H, S, hd = q.shape
    G, hpg = NSA_GROUPS, NSA_HPG
    qg = q.reshape(B, G, hpg, S, hd)
    tabg = tab.reshape(G, hpg, REL_BUCKETS)
    t = jnp.arange(S)
    nc = kc.shape[2]
    dc = t[:, None] - (jnp.arange(nc) * NSA_CMP_STRIDE + NSA_CMP_LEN - 1)[None, :]
    s = jnp.einsum('bghsd,bgcd->bghsc', qg, kc).astype(F32) * ATTN_SCALE + tabg[:, :, _rel_bucket(dc)].astype(F32)
    p_cmp, _ = _masked_softmax(s, dc >= 0)
    o_cmp = jnp.einsum('bghsc,bgcd->bghsd', p_cmp.astype(vc.dtype), vc)
    n_sel = -(-S // NSA_SEL_BLOCK)
    cstart = jnp.arange(nc) * NSA_CMP_STRIDE
    sstart = jnp.arange(n_sel) * NSA_SEL_BLOCK
    overlap = jnp.maximum(jnp.minimum(cstart[:, None] + NSA_CMP_LEN, sstart[None, :] + NSA_SEL_BLOCK) - jnp.maximum(cstart[:, None], sstart[None, :]), 0).astype(F32)
    imp = jnp.einsum('bghsc,cn->bgsn', p_cmp, overlap)
    cur = (t // NSA_SEL_BLOCK)[:, None]
    blk_id = jnp.arange(n_sel)[None, :]
    forced = (blk_id == 0) | (blk_id == cur) | (blk_id == cur - 1)
    imp = jnp.where(blk_id <= cur, imp + jnp.where(forced, NSA_FORCE, 0.0), -jnp.inf)
    n_top = min(NSA_SEL_TOPN, n_sel)
    _, sel = lax.top_k(imp, n_top)
    padw = ((0, 0), (0, 0), (0, n_sel * NSA_SEL_BLOCK - S), (0, 0))
    ksb = jnp.pad(ks, padw).reshape(B, G, n_sel, NSA_SEL_BLOCK, hd)
    vsb = jnp.pad(vs, padw).reshape(B, G, n_sel, NSA_SEL_BLOCK, hd)
    nq = S // NSA_QCHUNK
    b_ix = jnp.arange(B)[:, None, None, None]
    g_ix = jnp.arange(G)[None, :, None, None]
    h_ix = jnp.arange(hpg)[None, None, :, None, None]
    a_blk = jnp.arange(NSA_SEL_BLOCK)

    def sel_chunk(args):
        c, qc, sc = args
        tq = c * NSA_QCHUNK + jnp.arange(NSA_QCHUNK)
        kk = ksb[b_ix, g_ix, sc].reshape(B, G, NSA_QCHUNK, n_top * NSA_SEL_BLOCK, hd)
        vv = vsb[b_ix, g_ix, sc].reshape(B, G, NSA_QCHUNK, n_top * NSA_SEL_BLOCK, hd)
        kpos = (sc[..., None] * NSA_SEL_BLOCK + a_blk).reshape(B, G, NSA_QCHUNK, n_top * NSA_SEL_BLOCK)
        dist = tq[:, None] - kpos
        bias = tabg[g_ix[..., None], h_ix, _rel_bucket(dist)[:, :, None]].astype(F32)
        s = jnp.einsum('bghqd,bgqkd->bghqk', qc, kk).astype(F32) * ATTN_SCALE + bias
        pr, _ = _masked_softmax(s, (dist >= 0)[:, :, None])
        return jnp.einsum('bghqk,bgqkd->bghqd', pr.astype(vv.dtype), vv)

    qch = jnp.moveaxis(qg.reshape(B, G, hpg, nq, NSA_QCHUNK, hd), 3, 0)
    sch = jnp.moveaxis(sel.reshape(B, G, nq, NSA_QCHUNK, n_top), 2, 0)
    o_slc = jnp.moveaxis(lax.map(sel_chunk, (jnp.arange(nq), qch, sch)), 0, 3).reshape(B, G, hpg, S, hd)
    nw = S // NSA_WIN_BLOCK
    span = NSA_WINDOW + NSA_WIN_BLOCK
    kwp = jnp.pad(kw, ((0, 0), (0, 0), (NSA_WINDOW, 0), (0, 0)))
    vwp = jnp.pad(vw, ((0, 0), (0, 0), (NSA_WINDOW, 0), (0, 0)))
    kidx = jnp.arange(span)[None, :]
    dw = jnp.arange(NSA_WIN_BLOCK)[:, None] + NSA_WINDOW - kidx
    bias_w = tabg[:, :, _rel_bucket(dw)].astype(F32)

    def win_block(args):
        j, qb = args
        kb_ = lax.dynamic_slice_in_dim(kwp, j * NSA_WIN_BLOCK, span, axis=2)
        vb_ = lax.dynamic_slice_in_dim(vwp, j * NSA_WIN_BLOCK, span, axis=2)
        ok = (dw >= 0) & (dw < NSA_WINDOW) & (j * NSA_WIN_BLOCK - NSA_WINDOW + kidx >= 0)
        s = jnp.einsum('bghqd,bgkd->bghqk', qb, kb_).astype(F32) * ATTN_SCALE + bias_w
        pr, _ = _masked_softmax(s, ok)
        return jnp.einsum('bghqk,bgkd->bghqd', pr.astype(vb_.dtype), vb_)

    qwb = jnp.moveaxis(qg.reshape(B, G, hpg, nw, NSA_WIN_BLOCK, hd), 3, 0)
    o_win = jnp.moveaxis(lax.map(win_block, (jnp.arange(nw), qwb)), 0, 3).reshape(B, G, hpg, S, hd)
    o = (gates[..., 0:1] * o_cmp.reshape(B, H, S, hd) + gates[..., 1:2] * o_slc.reshape(B, H, S, hd)
         + gates[..., 2:3] * o_win.reshape(B, H, S, hd))
    return o.astype(q.dtype)

def _mixer_ab(xn, w_in, w_out, qn_a, kn_a, qn_b, kn_b, rel_bias):
    B, S, _ = xn.shape
    wa = MOBA_HEADS * HEAD_DIM
    wb = DIL_HEADS * HEAD_DIM
    qa, ka, va, qb, kb, vb = jnp.split(xn @ w_in, [wa, 2 * wa, 3 * wa, 3 * wa + wb, 3 * wa + 2 * wb], axis=-1)
    oa = _moba(_rms(_heads(qa, MOBA_HEADS), qn_a), _rms(_heads(ka, MOBA_HEADS), kn_a), _heads(va, MOBA_HEADS), rel_bias[:, :MOBA_HEADS].T)
    ob = _dilated(_rms(_heads(qb, DIL_HEADS), qn_b), _rms(_heads(kb, DIL_HEADS), kn_b), _heads(vb, DIL_HEADS), rel_bias[:, MOBA_HEADS:].T)
    o = jnp.concatenate([oa, ob], axis=1).transpose(0, 2, 1, 3).reshape(B, S, D_MODEL)
    return o @ w_out

def _mixer_nsa(xn, w_in, w_out, qn, kn_c, kn_s, kn_w, cmp_k, cmp_v, rel_bias):
    B, S, _ = xn.shape
    qw = NSA_HEADS * HEAD_DIM
    kvw = NSA_GROUPS * HEAD_DIM
    q, kc, vc, ks, vs, kw, vw, g = jnp.split(xn @ w_in, [qw + i * kvw for i in range(7)], axis=-1)
    q = _rms(_heads(q, NSA_HEADS), qn)
    kc = _rms(_compress(_heads(kc, NSA_GROUPS), *cmp_k), kn_c)
    vc = _compress(_heads(vc, NSA_GROUPS), *cmp_v)
    ks = _rms(_heads(ks, NSA_GROUPS), kn_s)
    kw = _rms(_heads(kw, NSA_GROUPS), kn_w)
    gates = jax.nn.sigmoid(g.astype(F32)).reshape(B, S, NSA_HEADS, 3).transpose(0, 2, 1, 3)
    o = _nsa(q, kc, vc, ks, _heads(vs, NSA_GROUPS), kw, _heads(vw, NSA_GROUPS), gates, rel_bias.T)
    return o.transpose(0, 2, 1, 3).reshape(B, S, D_MODEL) @ w_out

def _swiglu(x, wg, wu, wd):
    return (jax.nn.silu(x @ wg) * (x @ wu)) @ wd

def second_inputs(seed: int = 0) -> dict:
    key = jax.random.key(seed)
    keys = iter(jax.random.split(key, 40))

    def nrm(shape, scale):
        return jax.random.normal(next(keys), shape, F32) * scale

    def gain(shape):
        return 1.0 + nrm(shape, 0.02)

    D, hd, F, CH = D_MODEL, HEAD_DIM, FFN_HIDDEN, NSA_CMP_HIDDEN
    res = (2 * DEPTH) ** -0.5
    w_ab = 3 * (MOBA_HEADS + DIL_HEADS) * hd
    w_nsa = NSA_HEADS * hd + 6 * NSA_GROUPS * hd + 3 * NSA_HEADS
    cin = NSA_CMP_LEN * hd
    return {
        'x': nrm((BATCH, SEQ, D), 1.0),
        'p': nrm((DEPTH, BATCH, SEQ, PLE_DIM), 1.0),
        'rel_bias': nrm((REL_BUCKETS, N_HEADS_2), 0.5),
        'norm_mix': gain((DEPTH, D)),
        'norm_ffn': gain((DEPTH, D)),
        'norm_ple': gain((DEPTH, D)),
        'w_ffn_gate': nrm((DEPTH, D, F), D ** -0.5),
        'w_ffn_up': nrm((DEPTH, D, F), D ** -0.5),
        'w_ffn_down': nrm((DEPTH, F, D), F ** -0.5 * res),
        'w_ple_proj': nrm((DEPTH, PLE_DIM, D), PLE_DIM ** -0.5 * res),
        'w_ple_gate': nrm((DEPTH, D, D), D ** -0.5),
        'w_in_ab': nrm((N_EVEN_2, D, w_ab), D ** -0.5),
        'w_out_ab': nrm((N_EVEN_2, D, D), D ** -0.5 * res),
        'qn_moba': gain((N_EVEN_2, hd)),
        'kn_moba': gain((N_EVEN_2, hd)),
        'qn_dil': gain((N_EVEN_2, hd)),
        'kn_dil': gain((N_EVEN_2, hd)),
        'w_in_nsa': nrm((N_ODD_2, D, w_nsa), D ** -0.5),
        'w_out_nsa': nrm((N_ODD_2, D, D), D ** -0.5 * res),
        'qn_nsa': gain((N_ODD_2, hd)),
        'kn_cmp': gain((N_ODD_2, hd)),
        'kn_slc': gain((N_ODD_2, hd)),
        'kn_win': gain((N_ODD_2, hd)),
        'cmp_k_pos': nrm((N_ODD_2, NSA_CMP_LEN, hd), 0.1),
        'cmp_k_w1': nrm((N_ODD_2, cin, CH), cin ** -0.5),
        'cmp_k_b1': nrm((N_ODD_2, CH), 0.01),
        'cmp_k_w2': nrm((N_ODD_2, CH, hd), CH ** -0.5),
        'cmp_k_b2': nrm((N_ODD_2, hd), 0.01),
        'cmp_v_pos': nrm((N_ODD_2, NSA_CMP_LEN, hd), 0.1),
        'cmp_v_w1': nrm((N_ODD_2, cin, CH), cin ** -0.5),
        'cmp_v_b1': nrm((N_ODD_2, CH), 0.01),
        'cmp_v_w2': nrm((N_ODD_2, CH, hd), CH ** -0.5),
        'cmp_v_b2': nrm((N_ODD_2, hd), 0.01),
    }

def second_block(x, p, rel_bias, norm_mix, norm_ffn, norm_ple, w_ffn_gate, w_ffn_up, w_ffn_down,
              w_ple_proj, w_ple_gate, w_in_ab, w_out_ab, qn_moba, kn_moba, qn_dil, kn_dil,
              w_in_nsa, w_out_nsa, qn_nsa, kn_cmp, kn_slc, kn_win,
              cmp_k_pos, cmp_k_w1, cmp_k_b1, cmp_k_w2, cmp_k_b2,
              cmp_v_pos, cmp_v_w1, cmp_v_b1, cmp_v_w2, cmp_v_b2):
    h = x
    for i in range(DEPTH):
        e = i // 2
        xn = _rms(h, norm_mix[i])
        if i % 2 == 0:
            mix = _mixer_ab(xn, w_in_ab[e], w_out_ab[e], qn_moba[e], kn_moba[e], qn_dil[e], kn_dil[e], rel_bias)
        else:
            cmp_k = (cmp_k_pos[e], cmp_k_w1[e], cmp_k_b1[e], cmp_k_w2[e], cmp_k_b2[e])
            cmp_v = (cmp_v_pos[e], cmp_v_w1[e], cmp_v_b1[e], cmp_v_w2[e], cmp_v_b2[e])
            mix = _mixer_nsa(xn, w_in_nsa[e], w_out_nsa[e], qn_nsa[e], kn_cmp[e], kn_slc[e], kn_win[e], cmp_k, cmp_v, rel_bias)
        h = h + mix.astype(h.dtype)
        h = h + _swiglu(_rms(h, norm_ffn[i]), w_ffn_gate[i], w_ffn_up[i], w_ffn_down[i])
        gate = jax.nn.sigmoid(_rms(h, norm_ple[i]) @ w_ple_gate[i])
        h = h + gate * (p[i] @ w_ple_proj[i])
    return h


def setup_inputs(seed=0):
    out = dict(first_inputs(seed))
    for name, value in second_inputs(seed + 1).items():
        if name != "x":
            out[name + "_2"] = value
    return out


def reference(
    x, even_w_in, even_conv_a, even_conv_b_w, even_conv_b_bias, even_norm_b_g, even_norm_b_b,
    even_w_out, odd_w_qkv, odd_w_o, ln_mix_g, ln_mix_b, ln_ffn_g, ln_ffn_b, router_group_w,
    router_group_b, router_expert_w, router_expert_b, expert_w_up, expert_w_down, p_2,
    rel_bias_2, norm_mix_2, norm_ffn_2, norm_ple_2, w_ffn_gate_2, w_ffn_up_2, w_ffn_down_2,
    w_ple_proj_2, w_ple_gate_2, w_in_ab_2, w_out_ab_2, qn_moba_2, kn_moba_2, qn_dil_2, kn_dil_2,
    w_in_nsa_2, w_out_nsa_2, qn_nsa_2, kn_cmp_2, kn_slc_2, kn_win_2, cmp_k_pos_2, cmp_k_w1_2,
    cmp_k_b1_2, cmp_k_w2_2, cmp_k_b2_2, cmp_v_pos_2, cmp_v_w1_2, cmp_v_b1_2, cmp_v_w2_2,
    cmp_v_b2_2,
):
    x = first_block(
        x, even_w_in, even_conv_a, even_conv_b_w, even_conv_b_bias, even_norm_b_g,
        even_norm_b_b, even_w_out, odd_w_qkv, odd_w_o, ln_mix_g, ln_mix_b, ln_ffn_g, ln_ffn_b,
        router_group_w, router_group_b, router_expert_w, router_expert_b, expert_w_up,
        expert_w_down,
    )
    return second_block(
        x, p_2, rel_bias_2, norm_mix_2, norm_ffn_2, norm_ple_2, w_ffn_gate_2, w_ffn_up_2,
        w_ffn_down_2, w_ple_proj_2, w_ple_gate_2, w_in_ab_2, w_out_ab_2, qn_moba_2, kn_moba_2,
        qn_dil_2, kn_dil_2, w_in_nsa_2, w_out_nsa_2, qn_nsa_2, kn_cmp_2, kn_slc_2, kn_win_2,
        cmp_k_pos_2, cmp_k_w1_2, cmp_k_b1_2, cmp_k_w2_2, cmp_k_b2_2, cmp_v_pos_2, cmp_v_w1_2,
        cmp_v_b1_2, cmp_v_w2_2, cmp_v_b2_2,
    )


_drawn_inputs = setup_inputs


def setup_inputs(seed=0):
    import zlib

    import numpy as np

    out = dict(_drawn_inputs(seed))
    spreads = {}
    factors = {'even_conv_b_bias': 4.733,
     'even_norm_b_b': 8.0,
     'router_group_b': 8.0,
     'router_expert_b': 7.54,
     'norm_mix_2': 8.0,
     'norm_ffn_2': 5.122,
     'norm_ple_2': 200.0,
     'qn_moba_2': 8.0,
     'kn_moba_2': 8.0,
     'qn_dil_2': 8.0,
     'kn_dil_2': 8.0,
     'qn_nsa_2': 8.0,
     'kn_cmp_2': 88.179,
     'kn_slc_2': 8.0,
     'kn_win_2': 8.0,
     'cmp_k_pos_2': 8.0,
     'cmp_k_b1_2': 64.0,
     'cmp_k_b2_2': 170.788,
     'cmp_v_pos_2': 23.47,
     'cmp_v_b1_2': 200.0,
     'cmp_v_b2_2': 64.0}
    for name, (base, spread) in spreads.items():
        noise = np.random.default_rng([zlib.crc32(name.encode()), seed]).standard_normal(out[name].shape)
        drawn = base * np.exp(spread * noise) if base else spread * noise
        out[name] = jnp.asarray(drawn.astype(out[name].dtype))
    for name, factor in factors.items():
        out[name] = (out[name] * factor).astype(out[name].dtype)
    return out
```

```python
from contextlib import ExitStack

import numpy as np

import concourse.bass as bass
from concourse import mybir

F32 = mybir.dt.float32
I32 = mybir.dt.int32
U32 = mybir.dt.uint32
ALU = mybir.AluOpType
ACT = mybir.ActivationFunctionType
AX = mybir.AxisListType

P = 128
S = 256
D = 1024
DC = D // P
NT = S // P
DEPTH = 2
NE = 32
NG = 4
F_E = 512
NH = 16
HD = 64
FFN = 2816
FC = FFN // P
NCMP = 15
ALPHA = (2 * DEPTH) ** 0.25
LN_EPS = 1e-5
RMS_EPS = 1e-6
NEG = -1e30
BIG = 3e38

WIN = 64
NOV = S * 2 // WIN - 1
SLOTS = 2 * S
YR = NE * WIN
NRING = 6
RW = 4096

CONST_COLS = {}


def host_constants():
    p = np.arange(P)[:, None]
    j = np.arange(P)[None, :]
    parts = [
        ("ident", p == j),
        ("ones", np.ones((P, P))),
        ("before", p < j),
        ("suffix", p >= j),
        ("halves", (p // HD) == (j // HD)),
        ("strict", np.concatenate([np.where(p < j, 0.0, NEG), np.zeros((P, P)), np.where(p < j, 0.0, NEG)], 1)),
        ("slot", np.broadcast_to(np.arange(SLOTS), (P, SLOTS))),
        ("io32m", np.broadcast_to(np.arange(NE) - 64, (P, NE))),
        ("io32", np.broadcast_to(np.arange(NE), (P, NE))),
        ("io4m", np.broadcast_to(np.arange(NG) - 64, (P, NG))),
        ("io7", np.broadcast_to(np.arange(NOV), (P, NOV))),
    ]
    at = 0
    for name, a in parts:
        CONST_COLS[name] = (at, at + a.shape[1])
        at += a.shape[1]
    return np.concatenate([np.asarray(a, np.float32) for _, a in parts], 1)


def bucket_of(n):
    n = max(int(n), 0)
    if n < 16:
        return n
    return min(16 + int(np.log(np.float32(n / 16)) / np.log(2048 / 16) * 16), 31)


def host_bias_tables():
    W = 384
    a = np.zeros((33, 2, W), np.float32)
    for col in range(W - 1):
        d = col - 127
        if d < 0:
            a[32, :, col] = NEG
            continue
        a[bucket_of(d), :, col] = 1.0
        count = (d <= 128) + (d % 4 == 0) + (d % 16 == 0)
        a[32, 1, col] = np.log(count) if count else NEG
    c = np.zeros((33, NCMP, S), np.float32)
    for k in range(NCMP):
        for t in range(S):
            d = t - (16 * k + 31)
            if d >= 0:
                c[bucket_of(d), k, t] = 1.0
            else:
                c[32, k, t] = NEG
    return np.concatenate([a.reshape(33, -1), c.reshape(33, -1)], 1)


CONSTS = host_constants()
BIAS_TABLES = host_bias_tables()


class Queue:

    def __init__(self, sem):
        self.sem, self.n, self.items, self.seen = sem, 0, [], {}

    def wait(self, *toks):
        for t in toks:
            if t is None:
                continue
            if isinstance(t, list):
                self.wait(*t)
                continue
            sem, v = t
            if self.seen.get(sem.name, 0) < v:
                self.seen[sem.name] = v
                self.items.append(("wait", sem, v))

    def op(self, fn, *toks):
        self.wait(*toks)
        self.n += 1
        self.items.append(("inc", fn, self.sem, 1))
        return self.sem, self.n

    def quiet(self, fn, *toks):
        self.wait(*toks)
        self.items.append(("plain", fn))

    def dma(self, fn, counter, *toks):
        self.wait(*toks)
        self.items.append(("inc", fn, counter.sem, 16))
        return counter.next(16)

    def last(self):
        return (self.sem, self.n) if self.n else None

    def branch(self, cond):
        q = Queue(None)
        q.seen = dict(self.seen)
        self.items.append(("if", cond, q))
        return q

    def bump(self, fn, counter, *toks):
        self.wait(*toks)
        self.items.append(("inc", fn, counter.sem, 1))
        return counter.next(1)

    def play(self, e):
        for it in self.items:
            if it[0] == "wait":
                e.wait_ge(it[1], it[2])
            elif it[0] == "inc":
                it[1](e).then_inc(it[2], it[3])
            elif it[0] == "plain":
                it[1](e)
            else:
                with e.If(it[1](e)):
                    it[2].play(e)


class Counter:
    def __init__(self, sem):
        self.sem, self.n = sem, 0

    def next(self, by):
        self.n += by
        return self.sem, self.n


def bass_two_blocks_kernel(nc, I, out):
    ctx = ExitStack()
    with ctx:
        def sb(name, shape, dt=F32):
            return ctx.enter_context(nc.sbuf_tensor(name, shape, dt))

        def sem(name):
            return ctx.enter_context(nc.semaphore(name))

        CW = CONSTS.shape[1]
        cst = sb("cst", [P, CW])
        X = sb("X", [P, NT, D])
        XT = sb("XT", [P, DC, S])
        R = sb("R", [P, NT, D])
        GB = sb("GB", [P, 2, D])
        ring = sb("ring", [P, NRING, RW])
        AW = 15800
        arena = sb("arena", [P, AW])
        small = sb("small", [P, 1100])
        oi = sb("oi", [1, 64], I32)
        yi = sb("yi", [P, 2 * NT], U32)
        ps = [ctx.enter_context(nc.psum_tensor(f"ps{i}", [P, 512], F32)) for i in range(8)]

        ys = nc.dram_tensor("ys", [YR + SLOTS + WIN, D], F32, kind="Internal").ap()
        tv = nc.dram_tensor("tv", [2, NH, 384], F32, kind="Internal").ap()

        PE, DV, AC, PL = (Queue(sem(n)) for n in ("s_pe", "s_dve", "s_act", "s_pool"))
        SP = Queue(sem("s_sp"))
        c_in = Counter(sem("s_in"))
        c_ring = [Counter(sem(f"s_ring{i}")) for i in range(NRING)]
        c_gb = Counter(sem("s_gb"))
        c_rw = Counter(sem("s_rw"))
        c_y = [Counter(sem(f"s_y{i}")) for i in range(2)]
        c_yg = Counter(sem("s_yg"))
        c_tv = Counter(sem("s_tv"))
        c_bias = [Counter(sem(f"s_bias{i}")) for i in range(3)]
        c_sm = Counter(sem("s_sm"))
        c_out = Counter(sem("s_out"))
        c_ov = [{n: Counter(sem(f"s_ov_{n}{l}")) for n in ("dma", "pe", "act", "dve", "pool", "y")} for l in range(DEPTH)]

        def C(name, rows=P):
            a, b = CONST_COLS[name]
            return cst[0:rows, a:b]

        ident, ones = C("ident"), C("ones")

        class Area:

            def __init__(self):
                self.at = 0

            def take(self, *shape):
                n = int(np.prod(shape))
                v = arena[:, self.at:self.at + n]
                self.at += n
                assert self.at <= AW, self.at
                if len(shape) == 2:
                    return v.rearrange("p (a b) -> p a b", b=shape[1])
                if len(shape) == 3:
                    return v.rearrange("p (a b c) -> p a b c", b=shape[1], c=shape[2])
                return v

        sm_at = [0]

        def S_(*shape):
            n = int(np.prod(shape))
            v = small[:, sm_at[0]:sm_at[0] + n]
            sm_at[0] += n
            assert sm_at[0] <= 1100
            if len(shape) == 2:
                return v.rearrange("p (a b) -> p a b", b=shape[1])
            if len(shape) == 3:
                return v.rearrange("p (a b c) -> p a b c", b=shape[1], c=shape[2])
            return v

        def stage():
            toks = [q.last() for q in (PE, DV, AC, PL)]
            for q in (PE, DV, AC, PL):
                q.wait(toks)
            for i in range(8):
                free[i] = None
            sm_at[0] = 0
            return Area()

        free = [None] * 8

        loads = []

        def load(*pieces):
            loads.append({"pieces": pieces, "released": None})

        taken = [0]

        def next_slot():
            n = taken[0]
            taken[0] += 1
            i = n % NRING
            tok = c_ring[i].next(16 * len(loads[n]["pieces"]))
            return ring[:, i, :], tok, n

        def rows4(w, r0):
            return lambda s: s[:, 0:4096].rearrange("p (c n) -> p c n", c=4), w[r0:r0 + 512, :].rearrange("(c p) n -> p c n", p=P)

        def cols(w, c0, n=512, at=0):
            return lambda s: s[:, at:at + 8 * n].rearrange("p (c n) -> p c n", c=8), w[:, c0:c0 + n].rearrange("(c p) n -> p c n", p=P)

        def plan_loads():
            w = I["even_w_in"][0]
            for c0 in (1536, 2048, 512, 1024, 0):
                load(cols(w, c0))
            for r in (0, 512):
                load(rows4(I["even_w_out"][0], r))
            moe_loads(0)
            w = I["odd_w_qkv"][0]
            for c0 in (0, 512, 1024, 1536):
                load(cols(w, c0))
            for r in (0, 512):
                load(rows4(w[:, 2048:3072], r))
            for r in (0, 512):
                load(rows4(I["odd_w_o"][0], r))
            moe_loads(1)
            for i in range(DEPTH):
                if i == 0:
                    for c0 in range(0, 3072, 512):
                        load(cols(I["w_in_ab_2"][0], c0))
                    wo = I["w_out_ab_2"][0]
                else:
                    for c0 in range(0, 2560, 512):
                        load(cols(I["w_in_nsa_2"][0], c0))
                    for name in ("cmp_k_w1_2", "cmp_v_w1_2"):
                        src = I[name][0].rearrange("(l d) c -> d l c", d=HD)
                        load(*((lambda s, h=h: s[HD * h:HD * h + HD, :].rearrange("p (l c) -> p l c", c=P), src) for h in range(2)))
                    wo = I["w_out_nsa_2"][0]
                for r in (0, 512):
                    load(rows4(wo, r))
                for f in range(0, FFN, 256):
                    load(cols(I["w_ffn_gate_2"][i], f, 256, 0), cols(I["w_ffn_up_2"][i], f, 256, 2048))
                for r in range(0, FFN - 256, 512):
                    load(rows4(I["w_ffn_down_2"][i], r))
                load((lambda s: s[:, 0:2048].rearrange("p (c n) -> p c n", c=2),
                      I["w_ffn_down_2"][i][FFN - 256:, :].rearrange("(c p) n -> p c n", p=P)))
                for r in (0, 512):
                    load(rows4(I["w_ple_gate_2"][i], r))
                load((lambda s: s[:, 0:2048].rearrange("p (c n) -> p c n", c=2),
                      I["w_ple_proj_2"][i].rearrange("(c p) n -> p c n", p=P)),
                     (lambda s: s[:, 2048:2560].rearrange("p (c n) -> p c n", c=2),
                      I["p_2"][i].rearrange("(c p) n -> p c n", p=P)))

        moe_end = []

        def moe_loads(layer):
            for e in range(NE):
                up, dn = I["expert_w_up"][layer, e], I["expert_w_down"][layer, e]
                load(rows4(up, 0))
                load(rows4(up, 512))
                load(rows4(dn, 0))
            moe_end.append(len(loads))

        plan_loads()

        def transposed(src, toks, gain=None):
            done = []
            for b in range(4):
                bank = ps[b]
                for q in range(4):
                    dc, tt = 2 * b + q // 2, q % 2
                    o, i = bank[:, q * P:q * P + P], src[:, tt, dc * P:dc * P + P]
                    if q < 3:
                        PE.quiet(lambda e, o=o, i=i: e.transpose(o, i, ident), free[b], toks)
                    else:
                        t = PE.op(lambda e, o=o, i=i: e.transpose(o, i, ident), free[b], toks)
                if gain is None:
                    o = XT[:, 2 * b:2 * b + 2, :].rearrange("p a b -> p (a b)")
                    if b % 2:
                        k = AC.op(lambda e, o=o, bank=bank: e.activation(o, bank[:, :], ACT.Copy), t)
                    else:
                        k = DV.op(lambda e, o=o, bank=bank: e.tensor_copy(o, bank[:, :]), t)
                    free[b] = [k]
                else:
                    free[b] = []
                    for h in range(2):
                        dc = 2 * b + h
                        o, i, g = XT[:, dc, :], bank[:, h * S:h * S + S], gain[:, dc:dc + 1]
                        if b % 2:
                            k = AC.op(lambda e, o=o, i=i, g=g: e.activation(o, i, ACT.Copy, scale=g), t)
                        else:
                            k = DV.op(lambda e, o=o, i=i, g=g: e.tensor_scalar(o, i, g, None, ALU.mult), t)
                        free[b].append(k)
                done += free[b]
            return done

        def by_tokens(lhs, slots, banks, toks, chunks):
            c = 0
            for s, n_rows in slots:
                view, arrived, n = s
                PE.wait(arrived)
                w = view[:, 0:n_rows * D].rearrange("p (c n) -> p c n", c=n_rows)
                for r in range(n_rows):
                    for tt in range(NT):
                        for h in range(2):
                            b = banks[2 * tt + h]
                            if c == 0:
                                PE.wait(free[b])
                            l = lhs(c)[:, tt * P:tt * P + P]
                            fn = lambda e, b=b, l=l, r=r, h=h, c=c, w=w: e.matmul(
                                ps[b][:, :], l, w[:, r, h * 512:h * 512 + 512], start=(c == 0), stop=(c == chunks - 1))
                            if (r == n_rows - 1 and tt == 1 and h == 1) or c == chunks - 1:
                                tok = PE.op(fn, toks)
                            else:
                                PE.quiet(fn, toks)
                            if c == chunks - 1:
                                done[b] = tok
                    c += 1
                loads[n]["released"] = tok
            return [done[b] for b in banks]

        done = [None] * 8

        def residual(banks, toks, scale, dst):
            r = []
            for tt in range(NT):
                for h in range(2):
                    b = banks[2 * tt + h]
                    sl = slice(h * 512, h * 512 + 512)
                    k = DV.op(lambda e, b=b, tt=tt, sl=sl: e.scalar_tensor_tensor(
                        dst[:, tt, sl], X[:, tt, sl], float(scale), ps[b][:, :], ALU.mult, ALU.add), toks[2 * tt + h])
                    free[b] = [k]
                    r.append(k)
            return r

        gb_free = [None]

        def load_ln(g, b):
            PL.dma(lambda e: e.dma_start(GB[:, 0, :], g.partition_broadcast(P)), c_gb, gb_free[0])
            return PL.dma(lambda e: e.dma_start(GB[:, 1, :], b.partition_broadcast(P)), c_gb)

        def layer_norm(toks, gb):
            st, ag, rs, nb = S_(2 * NT, 6), S_(NT, 2), S_(NT), S_(NT)
            res = []
            for tt in range(NT):
                k = [DV.op(lambda e, tt=tt, h=h: e.bn_stats(st[:, 2 * tt + h, :], R[:, tt, h * 512:h * 512 + 512]), toks)
                     for h in range(2)]
                k = DV.op(lambda e, tt=tt: e.bn_aggr(ag[:, tt, :], st[:, 2 * tt:2 * tt + 2, :]), k)
            k = DV.op(lambda e: e.tensor_scalar(rs, ag[:, :, 1], LN_EPS, None, ALU.add), k)
            k = AC.op(lambda e: e.activation(rs, rs, ACT.Sqrt), k)
            k = DV.op(lambda e: e.reciprocal(rs, rs), k)
            k = DV.op(lambda e: e.scalar_tensor_tensor(nb, ag[:, :, 0], -1.0, rs, ALU.mult, ALU.mult), k)
            for tt in range(NT):
                t = AC.op(lambda e, tt=tt: e.activation(R[:, tt, :], R[:, tt, :], ACT.Identity, scale=rs[:, tt:tt + 1],
                                                        bias=nb[:, tt:tt + 1]), k)
                t = DV.op(lambda e, tt=tt: e.tensor_tensor(R[:, tt, :], R[:, tt, :], GB[:, 0, :], ALU.mult), t, gb)
                t = DV.op(lambda e, tt=tt: e.tensor_tensor(X[:, tt, :], R[:, tt, :], GB[:, 1, :], ALU.add), t)
                res.append(t)
            gb_free[0] = res[-1]
            return res

        def rms_to(toks):
            ss, rs = S_(NT), S_(NT)
            k = []
            for tt in range(NT):
                k.append(AC.op(lambda e, tt=tt: e.activation(R[:, tt, :], X[:, tt, :], ACT.Square, accum_out=ss[:, tt:tt + 1]), toks))
            t = DV.op(lambda e: e.tensor_scalar(rs, ss, 1.0 / D, RMS_EPS, ALU.mult, ALU.add), k)
            t = AC.op(lambda e: e.activation(rs, rs, ACT.Sqrt), t)
            t = DV.op(lambda e: e.reciprocal(rs, rs), t)
            return [DV.op(lambda e, tt=tt: e.tensor_scalar(R[:, tt, :], X[:, tt, :], rs[:, tt:tt + 1], None, ALU.mult), t)
                    for tt in range(NT)]

        k_cst = AC.dma(lambda e: e.dma_start(cst[:, :], I["consts"]), c_in)
        k_x = AC.dma(lambda e: e.dma_start(X[:, :, :], I["x"][0].rearrange("(t p) d -> p t d", p=P)), c_in)
        gains = sb("gains", [P, 6, DC])
        hg = sb("hg", [P, 8])
        cw = sb("cw", [P, 4, 37])
        for dst, src in ((gains, "gains"), (hg, "head_gains"), (cw, "conv_taps")):
            AC.dma(lambda e, dst=dst, src=src: e.dma_start(dst[:], I[src]), c_in)
        rel = sb("rel", [33, NH])
        t = DV.op(lambda e: e.memset(rel[:, :], 1.0))
        k_in = AC.dma(lambda e: e.dma_start(rel[0:32, :], I["rel_bias_2"]), c_in, t)
        btab = sb("btab", [P, NT, NCMP, NH])
        k_tab = AC.dma(lambda e: e.dma_start(arena[0:33, 0:768 + NCMP * S], I["bias_tables"]), c_in)

        for q in (PE, DV, AC, PL):
            q.wait(k_tab)

        def bias_rows():
            tvs = arena[0:NH, 14900:14900 + 768].rearrange("p (a b) -> p a b", a=2)
            for a in range(2):
                t = PE.op(lambda e, a=a: e.matmul(ps[a][0:NH, 0:384], rel[:, :], arena[0:33, 384 * a:384 * a + 384], start=True, stop=True))
                k = DV.op(lambda e, a=a: e.tensor_copy(tvs[:, a, :], ps[a][0:NH, 0:384]), t)
            PL.dma(lambda e: e.dma_start(tv.rearrange("a h c -> h a c"), tvs), c_tv, k)
            for tt in range(NT):
                for c in range(NCMP):
                    at = 768 + c * S + tt * P
                    fn = lambda e, tt=tt, c=c, at=at: e.matmul(ps[2][:, (tt * NCMP + c) * NH:(tt * NCMP + c) * NH + NH],
                                                               arena[0:33, at:at + P], rel[:, :], start=True, stop=True)
                    t = PE.op(fn)
            DV.op(lambda e: e.tensor_copy(btab[:, :, :, :].rearrange("p a b c -> p (a b c)"), ps[2][:, 0:NT * NCMP * NH]), t)

        wide = arena[:, 10000:10000 + 4 * D + 512]
        t = PL.op(lambda e: e.memset(wide, 0.0))
        PL.dma(lambda e: e.dma_start(ys[YR:, :].rearrange("r (h c) -> (r h) c", c=512).rearrange("(p k) c -> p (k c)", p=P), wide), c_tv, t)
        bias_rows()
        k_tv = (c_tv.sem, c_tv.n)

        def conv_mixer():
            A = stage()
            gp = A.take(4, 286)
            ap_ = A.take(4, 258)
            ac, ab, gc, sg, sq = A.take(4, S), A.take(4, S), A.take(4, S), A.take(4, S), A.take(4, S)
            yT = A.take(8, S)
            mean, var = A.take(S), A.take(S)
            kx = transposed(X, [k_x])
            z = [DV.op(lambda e: e.memset(gp[:, :, 0:30], 0.0)), DV.op(lambda e: e.memset(ap_[:, :, 0:2], 0.0))]

            def chan(slot, i, bank, off):
                view, arrived, n = slot
                w = view.rearrange("p (c n) -> p c n", c=8)
                o = ps[bank][:, off:off + S]
                PE.wait(arrived, kx, free[bank])
                for c in range(DC):
                    fn = lambda e, c=c: e.matmul(o, w[:, c, i * P:i * P + P], XT[:, c, :], start=(c == 0), stop=(c == DC - 1))
                    if c < DC - 1:
                        PE.quiet(fn)
                    else:
                        t = PE.op(fn)
                loads[n]["released"] = t
                return o, t

            sv, sgt = next_slot(), next_slot()
            kg = []
            for i in range(4):
                b0, b1 = 4 + 2 * (i % 2), 5 + 2 * (i % 2)
                ov, tv_ = chan(sv, i, b0, 0)
                og, tg = chan(sgt, i, b1, 0)
                t = AC.op(lambda e, i=i, og=og: e.activation(sg[:, i, :], og, ACT.Sigmoid), tg)
                free[b1] = [t]
                t = DV.op(lambda e, i=i, ov=ov: e.tensor_tensor(gp[:, i, 30:286], ov, sg[:, i, :], ALU.mult), t, tv_)
                free[b0] = [t]
                kg.append(t)
            s_c, s_v, s_b = next_slot(), next_slot(), next_slot()
            kc_, kb_ = [], []
            for i in range(4):
                o, t = chan(s_c, i, i % 4, 0)
                k = AC.op(lambda e, i=i, o=o: e.activation(ac[:, i, :], o, ACT.Copy), t)
                free[i % 4] = [k]
                kc_.append(k)

            def conv_b(i, Q):
                t = Q.op(lambda e: e.tensor_scalar(gc[:, i, :], gp[:, i, 0:S], cw[:, i, 0:1], cw[:, i, 34:35], ALU.mult, ALU.add), kg[i], z)
                yield t
                for k in range(1, 31):
                    t = Q.op(lambda e, k=k: e.scalar_tensor_tensor(gc[:, i, :], gp[:, i, k:k + S], cw[:, i, k:k + 1], gc[:, i, :],
                                                                   ALU.mult, ALU.add), t)
                    yield t

            for four in zip(*(conv_b(i, DV) for i in range(4))):
                pass
            ends = list(four)
            ka = []
            for i in range(4):
                o, t = chan(s_v, i, 4 + i % 4, 0)
                k = DV.op(lambda e, i=i, o=o: e.tensor_tensor(ap_[:, i, 2:258], o, ac[:, i, :], ALU.mult), t, kc_[i])
                free[4 + i % 4] = [k]
                ka.append(k)
            for i in range(4):
                o, t = chan(s_b, i, i % 4, 0)
                k = AC.op(lambda e, i=i, o=o: e.activation(ab[:, i, :], o, ACT.Copy), t)
                free[i % 4] = [k]
                kb_.append(k)
            t = ka
            for tap in range(3):
                t2 = []
                for i in range(4):
                    if tap == 0:
                        t2.append(DV.op(lambda e, i=i: e.tensor_scalar(yT[:, i, :], ap_[:, i, 0:S], cw[:, i, 31:32], None, ALU.mult), ka[i], z))
                    else:
                        t2.append(DV.op(lambda e, i=i, tap=tap: e.scalar_tensor_tensor(
                            yT[:, i, :], ap_[:, i, tap:tap + S], cw[:, i, 31 + tap:32 + tap], yT[:, i, :], ALU.mult, ALU.add), t[i]))
                t = t2
            ky = DV.op(lambda e: e.tensor_tensor(yT[:, 0:4, :], yT[:, 0:4, :], ab, ALU.mult), t, kb_)

            def sums(src, toks, bank):
                PE.wait(toks, free[bank])
                for i in range(4):
                    fn = lambda e, i=i: e.matmul(ps[bank][:, 0:S], ones, src[:, i, :], start=(i == 0), stop=(i == 3))
                    if i < 3:
                        PE.quiet(fn)
                    else:
                        return PE.op(fn)

            t = sums(gc, ends, 4)
            t = DV.op(lambda e: e.tensor_scalar(mean, ps[4][:, 0:S], 1.0 / 512, None, ALU.mult), t)
            t = DV.op(lambda e: e.tensor_tensor(gc, gc, mean.unsqueeze(1).to_broadcast([P, 4, S]), ALU.subtract), t)
            kd = t
            t = AC.op(lambda e: e.activation(sq, gc, ACT.Square), t)
            t = sums(sq, [t], 5)
            t = DV.op(lambda e: e.tensor_scalar(var, ps[5][:, 0:S], 1.0 / 512, LN_EPS, ALU.mult, ALU.add), t)
            t = AC.op(lambda e: e.activation(var, var, ACT.Sqrt), t)
            t = DV.op(lambda e: e.reciprocal(var, var), t)
            t = DV.op(lambda e: e.tensor_tensor(gc, gc, var.unsqueeze(1).to_broadcast([P, 4, S]), ALU.mult), t, kd)
            ks = [AC.op(lambda e, i=i: e.activation(yT[:, 4 + i, :], gc[:, i, :], ACT.Silu, scale=cw[:, i, 35:36], bias=cw[:, i, 36:37]), t)
                  for i in range(4)]
            free[4], free[5] = [kd], [t]
            for b in range(4):
                PE.wait(free[b])
            k = by_tokens(lambda c: yT[:, c, :], [(next_slot(), 4), (next_slot(), 4)], [0, 1, 2, 3], [ky] + ks, 8)
            DV.wait(k_tv)
            return residual([0, 1, 2, 3], k, ALPHA, R)

        def moe(layer, toks):
            A = stage()
            kx = transposed(X, toks)
            rw = A.take(DC, 36)
            rb = A.take(36)
            XsT = A.take(DC, SLOTS + WIN)
            Yg = XsT.rearrange("p c s -> p (c s)")[:, 0:2 * NT * D].rearrange("p (a b) -> p a b", b=D)
            xe = [A.take(DC, WIN) for _ in range(2)]
            sil = [A.take(F_E) for _ in range(2)]
            hh = [A.take(F_E) for _ in range(2)]
            hT = [A.take(4, WIN) for _ in range(2)]
            ysb = [A.take(D) for _ in range(2)]
            Pm = A.take(NT, SLOTS)
            wov = A.take(D)
            PL.dma(lambda e: e.dma_start(rw, I["router_w"][layer].rearrange("(c p) n -> p c n", p=P)), c_rw)
            k_rw = PL.dma(lambda e: e.dma_start(rb, I["router_b"][layer].partition_broadcast(P)), c_rw)
            kz = DV.op(lambda e: e.memset(XsT[:, :, SLOTS:SLOTS + WIN], 0.0))

            lp = ps[4][:, 0:72].rearrange("p (a b) -> p a b", b=36)
            for tt in range(NT):
                for c in range(DC):
                    fn = lambda e, tt=tt, c=c: e.matmul(lp[:, tt, :], XT[:, c, tt * P:tt * P + P], rw[:, c, :], start=(c == 0), stop=(c == DC - 1))
                    if tt == 1 and c == DC - 1:
                        t = PE.op(fn, kx, k_rw)
                    else:
                        PE.quiet(fn, kx, k_rw)
            lg = S_(NT, 36)
            bc = lambda v, *s: v.to_broadcast([P, *s])
            k_lg = t = DV.op(lambda e: e.tensor_tensor(lg, lp, bc(rb.unsqueeze(1), NT, 36), ALU.add), t, k_rw)

            def V(fn, *toks):
                return DV.op(fn, *toks)

            gm, gd, ge, gs = S_(NT), S_(NT, NG), S_(NT, NG), S_(NT)
            goh, gt, gi = S_(NT, NG), S_(NT, NG), S_(NT)
            gl = lg[:, :, 0:NG]
            t = V(lambda e: e.tensor_reduce(gm, gl, AX.X, ALU.max), t)
            t = kgd = V(lambda e: e.tensor_tensor(gd, gl, bc(gm.unsqueeze(2), NT, NG), ALU.subtract), t)
            ka = AC.op(lambda e: e.activation(ge, gd, ACT.Exp), t)
            t = V(lambda e: e.tensor_tensor(gt, gl, bc(gm.unsqueeze(2), NT, NG), ALU.is_equal), t)
            t = V(lambda e: e.tensor_tensor(gt, gt, bc(C("io4m").unsqueeze(1), NT, NG), ALU.mult), t)
            t = V(lambda e: e.tensor_reduce(gi, gt, AX.X, ALU.min), t)
            t = V(lambda e: e.tensor_tensor(goh, bc(C("io4m").unsqueeze(1), NT, NG), bc(gi.unsqueeze(2), NT, NG), ALU.is_equal), t)
            mneg, ml = S_(NT, NG), S_(NT, NE)
            ml4 = ml.rearrange("p t (g e) -> p t g e", g=NG)
            el4 = lg[:, :, NG:36].rearrange("p t (g e) -> p t g e", g=NG)
            t1 = V(lambda e: e.tensor_scalar(mneg, goh, -1.0, BIG, ALU.add, ALU.mult), t)
            t = V(lambda e: e.tensor_tensor(ml4, el4, bc(goh.unsqueeze(3), NT, NG, 8), ALU.mult), t)
            t = V(lambda e: e.tensor_tensor(ml4, ml4, bc(mneg.unsqueeze(3), NT, NG, 8), ALU.add), t, t1)
            oh = [S_(NT, NE) for _ in range(2)]
            mx = [S_(NT) for _ in range(2)]
            ix = [S_(NT) for _ in range(2)]
            eq = S_(NT, NE)
            io = bc(C("io32m").unsqueeze(1), NT, NE)
            for k in range(2):
                t = V(lambda e, k=k: e.tensor_reduce(mx[k], ml, AX.X, ALU.max), t)
                t = V(lambda e, k=k: e.tensor_tensor(eq, ml, bc(mx[k].unsqueeze(2), NT, NE), ALU.is_equal), t)
                t = V(lambda e, k=k: e.tensor_tensor(eq, eq, io, ALU.mult), t)
                t = V(lambda e, k=k: e.tensor_reduce(ix[k], eq, AX.X, ALU.min), t)
                t = V(lambda e, k=k: e.tensor_tensor(oh[k], io, bc(ix[k].unsqueeze(2), NT, NE), ALU.is_equal), t)
                if k == 0:
                    t = V(lambda e: e.scalar_tensor_tensor(ml, oh[0], -BIG, ml, ALU.mult, ALU.add), t)
            M = S_(NT, NE)
            t = kM = V(lambda e: e.tensor_tensor(M, oh[0], oh[1], ALU.add), t)
            before = C("before")
            rk, sz, szT = ps[5][:, 0:64], ps[5][:, 64:96], ps[6][0:NE, 0:P]
            PE.quiet(lambda e: e.matmul(rk[:, 0:NE], before, M[:, 0, :], start=True, stop=True), kM)
            PE.quiet(lambda e: e.matmul(rk[:, NE:64], ones, M[:, 0, :], start=True, stop=False))
            PE.quiet(lambda e: e.matmul(rk[:, NE:64], before, M[:, 1, :], start=False, stop=True))
            for tt in range(NT):
                PE.quiet(lambda e, tt=tt: e.matmul(sz, ones, M[:, tt, :], start=(tt == 0), stop=(tt == 1)))
            for tt in range(NT):
                fn = lambda e, tt=tt: e.matmul(szT, M[:, tt, :], ones, start=(tt == 0), stop=(tt == 1))
                if tt:
                    kr = PE.op(fn)
                else:
                    PE.quiet(fn)
            w2, wt = S_(NT), S_(2, NT)
            t = V(lambda e: e.tensor_tensor(w2, mx[1], mx[0], ALU.subtract), t)
            ka2 = AC.op(lambda e: e.activation(w2, w2, ACT.Exp), t)
            t = V(lambda e: e.tensor_reduce(gs, ge, AX.X, ALU.add), ka)
            t2 = V(lambda e: e.tensor_scalar(wt[:, 0, :], w2, 1.0, None, ALU.add), ka2)
            t = V(lambda e: e.tensor_tensor(gs, gs, wt[:, 0, :], ALU.mult), t, t2)
            t = V(lambda e: e.reciprocal(wt[:, 0, :], gs), t)
            k_wt = V(lambda e: e.tensor_tensor(wt[:, 1, :], wt[:, 0, :], w2, ALU.mult), t)
            szs, exT, st, cx, size, ext = S_(P), S_(P), S_(NE), S_(NE), S_(NE), S_(NE)
            szs, exT = szs[0:NE, :], exT[0:NE, :]
            t = ksz = V(lambda e: e.tensor_copy(szs, szT), kr)

            def windows(o, i, toks):
                t = V(lambda e: e.tensor_scalar(o, i, float(WIN), None, ALU.is_gt), toks)
                for j in range(2, S // WIN):
                    t = V(lambda e, j=j: e.scalar_tensor_tensor(o, i, float(WIN * j), o, ALU.is_gt, ALU.add), t)
                return t

            t = windows(exT, szs, t)
            PE.quiet(lambda e: e.matmul(ps[6][:, 128:160], szs, before[0:NE, 0:NE], start=True, stop=True), ksz)
            kp = PE.op(lambda e: e.matmul(ps[6][:, 160:192], exT, before[0:NE, 0:NE], start=True, stop=True), t)
            t0 = V(lambda e: e.tensor_copy(size, sz))
            k_st = V(lambda e: e.tensor_copy(st, ps[6][:, 128:160]), kp)
            k_cx = V(lambda e: e.tensor_copy(cx, ps[6][:, 160:192]))
            k_ext = windows(ext, size, t0)
            rank, pos, pk, rr, far = S_(NT, NE), S_(NT, NE), S_(2, NT), S_(2, NT), S_(2, NT)
            t = V(lambda e: e.tensor_copy(rank, rk.rearrange("p (t e) -> p t e", t=NT)))
            tp = V(lambda e: e.tensor_tensor(pos, rank, bc(st.unsqueeze(1), NT, NE), ALU.add), t, k_st)
            tq = []
            for k in range(2):
                a = V(lambda e, k=k: e.tensor_tensor(eq, oh[k], pos, ALU.mult), tp, tq[-1:])
                b = V(lambda e, k=k: e.tensor_reduce(pk[:, k, :], eq, AX.X, ALU.add), a)
                a = V(lambda e, k=k: e.tensor_tensor(eq, oh[k], rank, ALU.mult), b)
                tq.append(V(lambda e, k=k: e.tensor_reduce(rr[:, k, :], eq, AX.X, ALU.add), a))
            k_pm = []
            for tt in range(NT):
                a = V(lambda e, tt=tt: e.tensor_scalar(Pm[:, tt, :], C("slot"), pk[:, 0, tt:tt + 1], None, ALU.is_equal), tq)
                k_pm.append(V(lambda e, tt=tt: e.scalar_tensor_tensor(Pm[:, tt, :], C("slot"), pk[:, 1, tt:tt + 1], Pm[:, tt, :],
                                                                      ALU.is_equal, ALU.add), a))
            k_xs = []
            for c in range(DC):
                b = c % 4
                PE.wait(free[b], k_pm)
                PE.quiet(lambda e, b=b, c=c: e.matmul(ps[b][:, :], X[:, 0, c * P:c * P + P], Pm[:, 0, :], start=True, stop=False))
                t = PE.op(lambda e, b=b, c=c: e.matmul(ps[b][:, :], X[:, 1, c * P:c * P + P], Pm[:, 1, :], start=False, stop=True))
                if c % 2:
                    k = AC.op(lambda e, b=b, c=c: e.activation(XsT[:, c, 0:SLOTS], ps[b][:, :], ACT.Copy), t)
                else:
                    k = DV.op(lambda e, b=b, c=c: e.tensor_copy(XsT[:, c, 0:SLOTS], ps[b][:, :]), t)
                free[b] = [k]
                k_xs.append(k)
            t = V(lambda e: e.tensor_copy(oi[:, 0:NE], st[0:1, :]), k_st)
            k_oi = t
            er = S_(2, NT)
            for k in range(2):
                a = V(lambda e, k=k: e.tensor_scalar(er[:, k, :], ix[k], 64.0, float(WIN), ALU.add, ALU.mult))
                tq.append(a)
            a = V(lambda e: e.tensor_tensor(er, er, rr, ALU.add), tq)
            b = V(lambda e: e.tensor_scalar(far, rr, float(WIN), None, ALU.is_ge), tq)
            c_ = V(lambda e: e.tensor_tensor(pk, pk, er, ALU.subtract), a, k_pm)
            c_ = V(lambda e: e.tensor_scalar(pk, pk, float(YR), None, ALU.add), c_)
            c_ = V(lambda e: e.tensor_tensor(pk, pk, far, ALU.mult), c_, b)
            c_ = V(lambda e: e.tensor_tensor(er, er, pk, ALU.add), c_)
            k_yi = V(lambda e: e.tensor_copy(yi[:, :].rearrange("p (a b) -> p a b", b=NT), er), c_)
            o1, o2, o3 = A.take(NOV, NE), A.take(NOV, NE), A.take(NOV, NE)
            o1, o2, o3 = o1[0:1, :, :], o2[0:1, :, :], o3[0:1, :, :]
            ofl = S_(2 * NOV + 1)[0:1, :]
            b1 = lambda v: v.to_broadcast([1, NOV, NE])
            a = V(lambda e: e.tensor_tensor(o1, b1(C("io7", 1).unsqueeze(2)), b1(cx[0:1, :].unsqueeze(1)), ALU.subtract), k_cx)
            b = V(lambda e: e.tensor_tensor(o2, o1, b1(ext[0:1, :].unsqueeze(1)), ALU.is_lt), a, k_ext)
            a = V(lambda e: e.scalar_tensor_tensor(o2, o1, 0.0, o2, ALU.is_ge, ALU.mult), b)
            b = V(lambda e: e.scalar_tensor_tensor(o1, o1, float(WIN), b1(st[0:1, :].unsqueeze(1)), ALU.mult, ALU.add), a)
            b = V(lambda e: e.tensor_scalar(o1, o1, float(WIN - SLOTS), None, ALU.add), b)
            b = V(lambda e: e.tensor_tensor(o1, o1, o2, ALU.mult), b)
            b = V(lambda e: e.tensor_reduce(ofl[:, 0:NOV], o1, AX.X, ALU.add), b)
            b = V(lambda e: e.tensor_scalar(ofl[:, 0:NOV], ofl[:, 0:NOV], float(SLOTS), None, ALU.add), b)
            a = V(lambda e: e.tensor_tensor(o3, o2, b1(C("io32", 1).unsqueeze(1)), ALU.mult), a)
            a = V(lambda e: e.tensor_reduce(ofl[:, NOV:2 * NOV], o3, AX.X, ALU.add), a)
            c_ = V(lambda e: e.tensor_reduce(ofl[:, 2 * NOV:2 * NOV + 1], ext[0:1, :], AX.X, ALU.add), k_ext)
            k_ofl = V(lambda e: e.tensor_copy(oi[:, NE:NE + 2 * NOV + 1], ofl), a, b, c_, k_oi)
            k_al = [AC.op(lambda e, tt=tt: e.activation(R[:, tt, :], X[:, tt, :], ACT.Copy, scale=float(ALPHA))) for tt in range(NT)]

            U = [[0, 1], [2, 3]]
            TB, YB = 4, [5, 6]
            PE.wait(k_st, k_cx)
            up_done, mult_done, copied, evac = {}, {}, {}, {}
            y_done = [None, None]
            xe_done = {}

            def gather(e_):
                ap = oi[0:1, e_:e_ + 1]
                PL.wait(k_oi, k_xs, kz, up_done.get(e_ - 2))

                def fn(e):
                    r = e.value_load(ap, min_val=0, max_val=SLOTS)
                    return e.tensor_copy(xe[e_ % 2], XsT[:, :, bass.ds(r, WIN)])
                xe_done[e_] = PL.op(fn)

            def up_half(e_, slot, half):
                view, arrived, n = slot
                w = view.rearrange("p (c n) -> p c n", c=4)
                u = U[e_ % 2]
                PE.wait(xe_done[e_], arrived)
                for c in range(4):
                    for h in range(2):
                        if half == 0 and c == 0:
                            PE.wait(free[u[h]])
                        fn = lambda e, c=c, h=h: e.matmul(ps[u[h]][0:WIN, :], xe[e_ % 2][:, 4 * half + c, :], w[:, c, h * 512:h * 512 + 512],
                                                          start=(half == 0 and c == 0), stop=(half == 1 and c == 3))
                        if c == 3 and h == 1:
                            t = PE.op(fn)
                        else:
                            PE.quiet(fn)
                loads[n]["released"] = t
                return t

            def gate(e_):
                u = U[e_ % 2]
                t = AC.op(lambda e: e.activation(sil[e_ % 2][0:WIN, :], ps[u[0]][0:WIN, :], ACT.Silu), up_done[e_], mult_done.get(e_ - 2))
                mult_done[e_] = DV.op(lambda e: e.tensor_tensor(hh[e_ % 2][0:WIN, :], sil[e_ % 2][0:WIN, :], ps[u[1]][0:WIN, :], ALU.mult),
                                      t, turned.get(e_ - 2))
                free[u[0]] = [t]
                free[u[1]] = [mult_done[e_]]

            turned = {}

            def turn(e_):
                tb = ps[TB][:, 0:256].rearrange("p (c n) -> p c n", c=4)
                PE.wait(mult_done[e_], free[TB])
                for f in range(4):
                    fn = lambda e, f=f: e.transpose(tb[:, f, :], hh[e_ % 2][0:WIN, f * P:f * P + P], ident[0:WIN, 0:WIN])
                    if f < 3:
                        PE.quiet(fn)
                    else:
                        turned[e_] = PE.op(fn)
                copied[e_] = DV.op(lambda e: e.tensor_copy(hT[e_ % 2], tb), turned[e_], down_done.get(e_ - 2))
                free[TB] = [copied[e_]]

            down_done = {}

            def down(e_, slot):
                view, arrived, n = slot
                w = view.rearrange("p (c n) -> p c n", c=4)
                PE.wait(copied[e_], arrived)
                for f in range(4):
                    for h in range(2):
                        if f == 0:
                            PE.wait(free[YB[h]])
                        fn = lambda e, f=f, h=h: e.matmul(ps[YB[h]][0:WIN, :], hT[e_ % 2][:, f, :], w[:, f, h * 512:h * 512 + 512],
                                                          start=(f == 0), stop=(f == 3))
                        if f == 3 and h == 1:
                            t = PE.op(fn)
                        else:
                            PE.quiet(fn)
                loads[n]["released"] = t
                down_done[e_] = t
                for h in range(2):
                    k = AC.op(lambda e, h=h: e.activation(ysb[e_ % 2][0:WIN, h * 512:h * 512 + 512], ps[YB[h]][0:WIN, :], ACT.Copy),
                              t, y_done[e_ % 2])
                    free[YB[h]] = [k]
                y_done[e_ % 2] = AC.dma(lambda e: e.dma_start(ys[e_ * WIN:e_ * WIN + WIN, :], ysb[e_ % 2][0:WIN, :]), c_y[e_ % 2], k)

            free[TB] = [k_lg]
            free[5] = free[6] = [k_st, k_cx, tp]
            held = None
            gather(0)
            for e_ in range(NE + 1):
                if e_ < NE:
                    s1, s2, s3 = next_slot(), next_slot(), next_slot()
                    up_half(e_, s1, 0)
                if e_ >= 1:
                    turn(e_ - 1)
                if e_ < NE:
                    up_done[e_] = up_half(e_, s2, 1)
                    if e_ + 1 < NE:
                        gather(e_ + 1)
                    gate(e_)
                if e_ >= 1:
                    down(e_ - 1, held)
                held = s3

            ov = c_ov[layer]
            n_ap = oi[0:1, NE + 2 * NOV:NE + 2 * NOV + 1]
            some = lambda e: e.value_load(n_ap, min_val=0, max_val=NOV) > 0
            for q in (PE, AC, DV, PL):
                q.wait(k_ofl)
            bp, ba, bv, bg = (q.branch(some) for q in (PE, AC, DV, PL))
            bs = Queue(None)
            xo, so, ho, to, yo = xe[0], sil[0], hh[0], hT[0], ysb[0]
            first = [q.last() for q in (PE, AC, DV, PL)] + [t for t in y_done]
            for q in (bp, ba, bv, bg, bs):
                q.wait(first, k_ofl)
            t_y = t_dn = None
            t_pe = None
            for k in range(NOV):
                sap, eap = oi[0:1, NE + k:NE + k + 1], oi[0:1, NE + NOV + k:NE + NOV + k + 1]

                def pick(e, sap=sap):
                    r = e.value_load(sap, min_val=0, max_val=SLOTS)
                    return e.tensor_copy(xo, XsT[:, :, bass.ds(r, WIN)])
                tx = bg.bump(pick, ov["pool"], t_pe)

                def piece(c, t_free):
                    def fn(e, c=c, eap=eap):
                        r = e.value_load(eap, min_val=0, max_val=NE - 1)
                        w = I["expert_w_up"][layer] if c < DC else I["expert_w_down"][layer]
                        r0 = (c if c < DC else c - DC) * P
                        src = w[bass.ds(r, 1), r0:r0 + P, :].rearrange("o p n -> p (o n)")
                        return e.dma_start(wov, src)
                    return bs.dma(fn, ov["dma"], t_free)

                for c in range(DC):
                    td = piece(c, t_pe)
                    for h in range(2):
                        fn = lambda e, c=c, h=h: e.matmul(ps[h][0:WIN, :], xo[:, c, :], wov[:, h * 512:h * 512 + 512], start=(c == 0), stop=(c == DC - 1))
                        t_pe = bp.bump(fn, ov["pe"], td, tx)
                ta = ba.bump(lambda e: e.activation(so[0:WIN, :], ps[0][0:WIN, :], ACT.Silu), ov["act"], t_pe)
                tm = bv.bump(lambda e: e.tensor_tensor(ho[0:WIN, :], so[0:WIN, :], ps[1][0:WIN, :], ALU.mult), ov["dve"], ta)
                tb = ps[TB][:, 0:256].rearrange("p (c n) -> p c n", c=4)
                for f in range(4):
                    tt_ = bp.bump(lambda e, f=f: e.transpose(tb[:, f, :], ho[0:WIN, f * P:f * P + P], ident[0:WIN, 0:WIN]), ov["pe"], tm)
                tc = bv.bump(lambda e: e.tensor_copy(to, tb), ov["dve"], tt_)
                for f in range(4):
                    td = piece(DC + f, t_pe)
                    for h in range(2):
                        fn = lambda e, f=f, h=h: e.matmul(ps[YB[h]][0:WIN, :], to[:, f, :], wov[:, h * 512:h * 512 + 512], start=(f == 0), stop=(f == 3))
                        t_pe = bp.bump(fn, ov["pe"], td, tc)
                for h in range(2):
                    te = ba.bump(lambda e, h=h: e.activation(yo[0:WIN, h * 512:h * 512 + 512], ps[YB[h]][0:WIN, :], ACT.Copy), ov["act"], t_pe, t_y)

                def put(e, sap=sap):
                    r = e.value_load(sap, min_val=0, max_val=SLOTS)
                    return e.dma_start(ys[bass.ds(r + YR, WIN), :], yo[0:WIN, :])
                t_y = ba.dma(put, ov["y"], te)
                bp.wait(te)
            for q in (bp, ba, bv, bg):
                q.wait(t_y)
            sp_branch[layer] = (k_ofl, some, bs)

            for j in range(2 * NT):
                k_yg = PL.dma(lambda e, j=j: e.indirect_dma_start(
                    Yg[:, j, :], None, ys, bass.IndirectOffsetOnAxis(ap=yi[:, j:j + 1], axis=0)), c_yg,
                    k_yi, y_done, PE.last(), DV.last(), AC.last())
            r = []
            for tt in range(NT):
                t = DV.op(lambda e, tt=tt: e.scalar_tensor_tensor(R[:, tt, :], Yg[:, tt, :], wt[:, 0, tt:tt + 1], R[:, tt, :], ALU.mult, ALU.add),
                          k_yg, k_wt, k_al)
                r.append(DV.op(lambda e, tt=tt: e.scalar_tensor_tensor(R[:, tt, :], Yg[:, NT + tt, :], wt[:, 1, tt:tt + 1], R[:, tt, :],
                                                                       ALU.mult, ALU.add), t))
            return r

        sp_branch = {}

        def stick(toks):
            A = stage()
            kx = transposed(X, toks)
            qT, kT, oT = A.take(8, S), A.take(8, S), A.take(8, S)
            zb = [A.take(2, 384) for _ in range(2)]
            tb = [A.take(2, 384) for _ in range(2)]
            V = R
            k_q = {}
            for j in range(4):
                slot = next_slot()
                view, arrived, n = slot
                w = view.rearrange("p (c n) -> p c n", c=8)
                PE.wait(arrived, kx)
                for i in range(4):
                    b = 4 + i % 4
                    o = ps[b][:, 0:S]
                    for c in range(DC):
                        fn = lambda e, c=c, i=i, o=o, w=w: e.matmul(o, w[:, c, i * P:i * P + P], XT[:, c, :], start=(c == 0), stop=(c == DC - 1))
                        if c < DC - 1:
                            PE.quiet(fn, free[b])
                        else:
                            t = PE.op(fn)
                    if j < 2:
                        k = AC.op(lambda e, i=i, j=j, o=o: e.activation(qT[:, 4 * j + i, :], o, ACT.Copy, scale=float(HD ** -0.5)), t)
                    else:
                        k = DV.op(lambda e, i=i, j=j, o=o: e.tensor_copy(kT[:, 4 * (j - 2) + i, :], o), t)
                    free[b] = [k]
                    k_q[j, i] = k
                loads[n]["released"] = t
            k = by_tokens(lambda c: XT[:, c, :], [(next_slot(), 4), (next_slot(), 4)], [0, 1, 2, 3], [], 8)
            kv = []
            for tt in range(NT):
                for h in range(2):
                    b = 2 * tt + h
                    o = V[:, tt, h * 512:h * 512 + 512]
                    if h:
                        t = AC.op(lambda e, b=b, o=o: e.activation(o, ps[b][:, :], ACT.Copy), k[b])
                    else:
                        t = DV.op(lambda e, b=b, o=o: e.tensor_copy(o, ps[b][:, :]), k[b])
                    free[b] = [t]
                    kv.append(t)
            strict, suffix = C("strict"), C("suffix")
            zk, o_free, done_a, ko = {}, {}, {}, []

            def score(p):
                u = p % 2
                for h in range(2):
                    b, r = 2 * u + h, slice(HD * h, HD * h + HD)
                    PE.wait(free[b], k_q[p // 4, p % 4], k_q[2 + p // 4, p % 4])
                    PE.quiet(lambda e, b=b, r=r: e.matmul(ps[b][:, 0:S], kT[r, p, 0:P], qT[r, p, :], start=True, stop=True))
                    t = PE.op(lambda e, b=b, r=r: e.matmul(ps[b][:, S:384], kT[r, p, P:S], qT[r, p, P:S], start=True, stop=True))
                    k = DV.op(lambda e, b=b, u=u, h=h: e.tensor_tensor(zb[u][:, h, :], ps[b][:, 0:384], strict, ALU.add), t, done_a.get(p - 2))
                    free[b] = [k]
                t = AC.op(lambda e: e.activation(tb[u], zb[u], ACT.Abs), k, zk.get(("inc", p - 2)))
                t = AC.op(lambda e: e.activation(tb[u], tb[u], ACT.Exp, scale=-1.0), t)
                t = AC.op(lambda e: e.activation(tb[u], tb[u], ACT.Ln, bias=1.0), t)
                zk[p] = DV.op(lambda e: e.scalar_tensor_tensor(tb[u], zb[u], 0.0, tb[u], ALU.max, ALU.add), t)

            def attend(p):
                u = p % 2
                for h in range(2):
                    b = 4 + h
                    PE.wait(zk[p], free[b])
                    PE.quiet(lambda e, b=b, h=h: e.matmul(ps[b][:, 0:384], suffix, tb[u][:, h, :], start=True, stop=False))
                    t = PE.op(lambda e, b=b, h=h: e.matmul(ps[b][:, P:S], ones, tb[u][:, h, S:384], start=False, stop=True))
                    k = DV.op(lambda e, b=b, h=h: e.tensor_tensor(zb[u][:, h, :], zb[u][:, h, :], ps[b][:, 0:384], ALU.subtract), t)
                    free[b] = [k]
                zk["inc", p] = t
                ta = AC.op(lambda e: e.activation(zb[u], zb[u], ACT.Exp), k)
                b = 6 + p % 2
                PE.wait(ta, kv, free[b])
                for h in range(2):
                    hh = 2 * p + h
                    r = slice(HD * h, HD * h + HD)
                    PE.quiet(lambda e, h=h, r=r, hh=hh, b=b: e.matmul(ps[b][r, 0:S], V[:, 0, hh * HD:hh * HD + HD], zb[u][:, h, 0:S], start=True, stop=False))
                    t = PE.op(lambda e, h=h, r=r, hh=hh, b=b: e.matmul(ps[b][r, P:S], V[:, 1, hh * HD:hh * HD + HD], zb[u][:, h, S:384], start=False, stop=True))
                done_a[p] = t
                k = AC.op(lambda e, b=b: e.activation(oT[:, p, :], ps[b][:, 0:S], ACT.Copy), t)
                free[b] = [k]
                ko.append(k)

            for p in range(9):
                if p < 8:
                    score(p)
                if p >= 1:
                    attend(p - 1)
            k = by_tokens(lambda c: oT[:, c, :], [(next_slot(), 4), (next_slot(), 4)], [0, 1, 2, 3], ko, 8)
            DV.wait(t)
            return residual([0, 1, 2, 3], k, ALPHA, R)

        def head_norm(slot, width, gain, scale, dst, banks, tbanks, work, toks):
            view, arrived, n = slot
            w = view.rearrange("p (c n) -> p c n", c=8)
            nh = width // HD
            ss, res = S_(NT, nh), []
            if scale != 1.0:
                g2 = S_(1)
                kg = DV.op(lambda e: e.tensor_scalar(g2, gain, float(scale), None, ALU.mult), toks)
            else:
                g2, kg = gain, None
            for tt in range(NT):
                b = banks[tt]
                for c in range(DC):
                    fn = lambda e, b=b, tt=tt, c=c: e.matmul(ps[b][:, 0:width], XT[:, c, tt * P:tt * P + P], w[:, c, 0:width], start=(c == 0), stop=(c == DC - 1))
                    if c < DC - 1:
                        PE.quiet(fn, arrived, toks, free[b])
                    else:
                        t = PE.op(fn)
                wk = work[tt]
                k = AC.op(lambda e, b=b, wk=wk: e.activation(wk[:, 0:width], ps[b][:, 0:width], ACT.Square), t, wfree.get(id(wk)))
                k = DV.op(lambda e, tt=tt, wk=wk: e.tensor_reduce(ss[:, tt, :], wk[:, 0:width].rearrange("p (h d) -> p h d", d=HD), AX.X, ALU.add), k)
                k = DV.op(lambda e, tt=tt: e.tensor_scalar(ss[:, tt, :], ss[:, tt, :], 1.0 / HD, RMS_EPS, ALU.mult, ALU.add), k)
                k = AC.op(lambda e, tt=tt: e.activation(ss[:, tt, :], ss[:, tt, :], ACT.Sqrt), k)
                k = DV.op(lambda e, tt=tt: e.reciprocal(ss[:, tt, :], ss[:, tt, :]), k)
                k = DV.op(lambda e, tt=tt, b=b, wk=wk: e.tensor_tensor(
                    wk[:, 0:width].rearrange("p (h d) -> p h d", d=HD), ps[b][:, 0:width].rearrange("p (h d) -> p h d", d=HD),
                    ss[:, tt, :].unsqueeze(2).to_broadcast([P, nh, HD]), ALU.mult), k)
                free[b] = [k]
                tb_ = tbanks[tt]
                for i in range(width // P):
                    fn = lambda e, i=i, tb_=tb_, wk=wk: e.transpose(ps[tb_][:, i * P:i * P + P], wk[:, i * P:i * P + P], ident)
                    t2 = PE.op(fn, k, free[tb_])
                wfree[id(wk)] = t2
                m = width // P
                o = dst[:, :, tt * P:tt * P + P]
                i_ = ps[tb_][:, 0:width].rearrange("p (i t) -> p i t", t=P)
                k = AC.op(lambda e, o=o, i_=i_: e.activation(o, i_, ACT.Copy, scale=g2), t2, kg)
                free[tb_] = [k]
                res.append(k)
            loads[n]["released"] = t
            return res

        wfree = {}

        def tokens_of(slot, c0, width, dst, banks, toks, release):
            view, arrived, n = slot
            w = view.rearrange("p (c n) -> p c n", c=8)
            res = []
            for tt in range(NT):
                b = banks[tt]
                for c in range(DC):
                    fn = lambda e, b=b, tt=tt, c=c: e.matmul(ps[b][:, 0:width], XT[:, c, tt * P:tt * P + P], w[:, c, c0:c0 + width], start=(c == 0), stop=(c == DC - 1))
                    if c < DC - 1:
                        PE.quiet(fn, arrived, toks, free[b])
                    else:
                        t = PE.op(fn)
                o = dst(tt)
                k = DV.op(lambda e, b=b, o=o: e.tensor_copy(o, ps[b][:, 0:width]), t)
                free[b] = [k]
                res.append(k)
            if release:
                loads[n]["released"] = t
            return res

        def bias_loader(bias, db, heads, which):
            used = {}
            tok = {}

            def fetch(p):
                a, kind = heads(p), which(p)
                b = bias[p % 3]
                base = (kind * NH + a) * 384
                PL.wait(used.get(p - 3))
                for lo, n in ((0, P), (P, S)):
                    src = bass.AP(tv.tensor, base, [[1, P], [db * 384, 2], [1, n]])
                    tok[p] = PL.dma(lambda e, b=b, lo=lo, n=n, src=src: e.dma_start(b[:, :, lo:lo + n], src), c_bias[p % 3])
            return fetch, tok, used

        def soft_scores(qT, kT, p, kp, h, bank, bias_h, k_bias, toks, scr, stats, scr_free, gate=None):
            r = slice(HD * h, HD * h + HD)
            sbuf, mx, sm = scr, stats[0], stats[1]
            b = bank
            PE.quiet(lambda e: e.matmul(ps[b][:, S:384], qT[r, p, 0:P], kT[r, kp, 0:P], start=True, stop=True), free[b], toks)
            t = PE.op(lambda e: e.matmul(ps[b][:, 0:S], qT[r, p, P:S], kT[r, kp, :], start=True, stop=True))
            k = DV.op(lambda e: e.tensor_tensor(sbuf, ps[b][:, 0:384], bias_h[:, ::-1], ALU.add), t, k_bias, scr_free)
            free[b] = [k]
            used = k
            k1 = DV.op(lambda e: e.tensor_reduce(mx[:, 1:2], sbuf[:, 0:S], AX.X, ALU.max, negate=True), k)
            k0 = DV.op(lambda e: e.tensor_reduce(mx[:, 0:1], sbuf[:, S:384], AX.X, ALU.max, negate=True), k)
            a1 = AC.op(lambda e: e.activation(sbuf[:, 0:S], sbuf[:, 0:S], ACT.Exp, bias=mx[:, 1:2], accum_out=sm[:, 1:2]), k1)
            a0 = AC.op(lambda e: e.activation(sbuf[:, S:384], sbuf[:, S:384], ACT.Exp, bias=mx[:, 0:1], accum_out=sm[:, 0:1]), k0)
            k = DV.op(lambda e: e.reciprocal(sm, sm), a1, a0)
            if gate is not None:
                k = DV.op(lambda e: e.tensor_tensor(sm, sm, gate, ALU.mult), k)
            k1 = DV.op(lambda e: e.tensor_scalar(sbuf[:, 0:S], sbuf[:, 0:S], sm[:, 1:2], None, ALU.mult), k)
            k0 = DV.op(lambda e: e.tensor_scalar(sbuf[:, S:384], sbuf[:, S:384], sm[:, 0:1], None, ALU.mult), k)
            return used, [k1, k0]

        def soft_turn(sbuf, toks, bank, pT, pT_free):
            b = bank
            PE.wait(toks, free[b])
            PE.quiet(lambda e: e.transpose(ps[b][:, 0:P], sbuf[:, S:384], ident))
            PE.quiet(lambda e: e.transpose(ps[b][:, P:S], sbuf[:, 0:P], ident))
            t = PE.op(lambda e: e.transpose(ps[b][:, S:384], sbuf[:, P:S], ident))
            k = AC.op(lambda e: e.activation(pT, ps[b][:, 0:384], ACT.Copy), t, pT_free)
            free[b] = [k]
            return t, k

        def out_and_residual(oT, toks):
            k = by_tokens(lambda c: oT[:, c, :], [(next_slot(), 4), (next_slot(), 4)], [0, 1, 2, 3], toks, 8)
            return residual([0, 1, 2, 3], k, 1.0, X)

        def mixer_ab(toks):
            A = stage()
            kr = rms_to(toks)
            kx = transposed(R, kr, gains[:, 0, :])
            qT, kT, oT = A.take(8, S), A.take(8, S), A.take(8, S)
            V = R
            work = [A.take(512) for _ in range(2)]
            bias = [A.take(2, 384) for _ in range(3)]
            scr = [A.take(384) for _ in range(4)]
            pT = [A.take(384) for _ in range(4)]
            stats = [(S_(2), S_(2)) for _ in range(4)]
            fetch, k_bias, b_used = bias_loader(bias, 1, lambda p: 2 * p, lambda p: 0 if p < 4 else 1)
            for p in range(3):
                fetch(p)
            kq, kk, kv = {}, {}, {}
            for a in range(2):
                kq[a] = head_norm(next_slot(), 512, hg[:, 2 * a:2 * a + 1], HD ** -0.5, qT[:, 4 * a:4 * a + 4, :], (4, 5), (6, 7), work, kx)
                kk[a] = head_norm(next_slot(), 512, hg[:, 2 * a + 1:2 * a + 2], 1.0, kT[:, 4 * a:4 * a + 4, :], (4, 5), (6, 7), work, kx)
                kv[a] = tokens_of(next_slot(), 0, 512, lambda tt, a=a: V[:, tt, 512 * a:512 * a + 512], (0, 1), kx, True)
            ko = []
            pend = {}
            scr_free, pT_free, o_k = {}, {}, {}

            def first(h):
                p = h // 2
                used, k = soft_scores(qT, kT, p, p, h % 2, h % 4, bias[p % 3][:, h % 2, :], k_bias[p], kq[p // 4] + kk[p // 4],
                                      scr[h % 4], stats[h % 4], scr_free.get(h - 4))
                if h % 2:
                    b_used[p] = used
                    if p + 3 < 8:
                        fetch(p + 3)
                pend[h] = k

            def second(h):
                p = h // 2
                scr_free[h], k = soft_turn(scr[h % 4], pend[h], 4 + h % 2, pT[h % 4], pT_free.get(h - 4))
                b = 6 + p % 2
                r = slice(HD * (h % 2), HD * (h % 2) + HD)
                PE.wait(k, kv[p // 4], free[b] if h % 2 == 0 else None)
                PE.quiet(lambda e: e.matmul(ps[b][r, 0:S], V[:, 0, h * HD:h * HD + HD], pT[h % 4][:, 0:S], start=True, stop=False))
                t = PE.op(lambda e: e.matmul(ps[b][r, P:S], V[:, 1, h * HD:h * HD + HD], pT[h % 4][:, S:384], start=False, stop=True))
                pT_free[h] = t
                if h % 2:
                    k = AC.op(lambda e: e.activation(oT[:, p, :], ps[b][:, 0:S], ACT.Copy), t)
                    free[b] = [k]
                    ko.append(k)

            for h in range(NH + 2):
                if h < NH:
                    first(h)
                if h >= 2:
                    second(h - 2)
            return out_and_residual(oT, ko)

        def mixer_nsa(toks):
            A = stage()
            kr = rms_to(toks)
            kx = transposed(R, kr, gains[:, 3, :])
            qT, oT = A.take(8, S), A.take(8, S)
            kvc, ksT, kwT = A.take(4, S), A.take(2, S), A.take(2, S)
            Vs, Vw = A.take(NT, S), A.take(NT, S)
            work = [A.take(512) for _ in range(2)]
            bias = [A.take(2, 384) for _ in range(3)]
            scr = [A.take(384) for _ in range(4)]
            pT = [A.take(384) for _ in range(4)]
            gw = A.take(DC, 48)
            cmp_ = A.take(227)
            w2, posT, cb = cmp_[:, 0:192], cmp_[:, 192:224], S_(8)
            b2b = A.take(HD)
            hidk, hidv = A.take(60), A.take(60)
            hidr = A.take(4, P)
            kcT = A.take(60)
            sq60, rs60 = A.take(60), A.take(60)
            vcr = A.take(4, HD)
            pc = GB[:, 0, :].rearrange("p (a b) -> p a b", b=32)
            cs = A.take(NT * NH, NCMP)
            pcT = GB[:, 1, :].rearrange("p (a b) -> p a b", b=S)
            gt = S_(NT, 48)
            stats = [(S_(2), S_(2)) for _ in range(4)]
            fetch, k_bias, b_used = bias_loader(bias, 4, lambda i: (i // 4) * 8 + i % 4, lambda i: 0)
            for p in range(3):
                fetch(p)
            PL.dma(lambda e: e.dma_start(gw, I["w_in_nsa_2"][0][:, 2560:2608].rearrange("(c p) n -> p c n", p=P)), c_sm)
            PL.dma(lambda e: e.dma_start(cmp_, I["cmp_small"]), c_sm)
            k_sm = PL.dma(lambda e: e.dma_start(b2b, I["cmp_v_b2_2"][0].partition_broadcast(P)), c_sm)

            kq = []
            for a in range(2):
                kq.append(head_norm(next_slot(), 512, hg[:, 4:5], HD ** -0.5, qT[:, 4 * a:4 * a + 4, :], (4, 5), (6, 7), work, kx))
            view, arrived, n = next_slot()
            w = view.rearrange("p (c n) -> p c n", c=8)
            k_kvc = []
            for i in range(4):
                b = i
                for c in range(DC):
                    fn = lambda e, b=b, i=i, c=c, w=w: e.matmul(ps[b][:, 0:S], w[:, c, i * P:i * P + P], XT[:, c, :], start=(c == 0), stop=(c == DC - 1))
                    if c < DC - 1:
                        PE.quiet(fn, arrived, free[b])
                    else:
                        t = PE.op(fn)
                k = DV.op(lambda e, b=b, i=i: e.tensor_copy(kvc[:, i, :], ps[b][:, 0:S]), t)
                free[b] = [k]
                k_kvc.append(k)
            loads[n]["released"] = t
            s = next_slot()
            ks = head_norm(s, 256, hg[:, 6:7], 1.0, ksT, (4, 5), (6, 7), work, kx)
            kvs = tokens_of(s, 256, 256, lambda tt: Vs[:, tt, :], (0, 1), kx, True)
            s = next_slot()
            kw = head_norm(s, 256, hg[:, 7:8], 1.0, kwT, (4, 5), (6, 7), work, kx)
            kvw = tokens_of(s, 256, 256, lambda tt: Vw[:, tt, :], (0, 1), kx, True)
            k_cb = DV.op(lambda e: e.tensor_copy(cb[:, 0:3], cmp_[:, 224:227]), k_sm)
            gp_ = ps[2][:, 0:96].rearrange("p (t n) -> p t n", t=NT)
            for tt in range(NT):
                for c in range(DC):
                    fn = lambda e, tt=tt, c=c: e.matmul(gp_[:, tt, :], XT[:, c, tt * P:tt * P + P], gw[:, c, :], start=(c == 0), stop=(c == DC - 1))
                    t = PE.op(fn, free[2], k_sm)
            k_gt = AC.op(lambda e: e.activation(gt, gp_, ACT.Sigmoid), t)
            free[2] = [k_gt]
            hid_k = []
            for j in range(2):
                view, arrived, n = next_slot()
                w1 = view.rearrange("p (l c) -> p l c", c=P)
                hb, bb = (((3, 4), 2), ((1, 5), 0))[j]
                bp_ = ps[bb][:, 128:129]
                for l in range(32):
                    r = slice(HD * j, HD * j + HD)
                    t = PE.op(lambda e, l=l, r=r, w1=w1, bp_=bp_: e.matmul(bp_, w1[r, l, :], posT[r, l:l + 1], start=(l == 0), stop=(l == 31)),
                              arrived, free[bb], k_sm) if l in (0, 31) else PE.quiet(
                        lambda e, l=l, r=r, w1=w1, bp_=bp_: e.matmul(bp_, w1[r, l, :], posT[r, l:l + 1], start=(l == 0), stop=(l == 31)))
                kb = DV.op(lambda e, j=j, bp_=bp_: e.tensor_tensor(cb[:, 4 + j:5 + j], bp_, cb[:, j:j + 1], ALU.add), t, k_cb)
                hid, hk = (hidk, hidv)[j], []
                for par in range(2):
                    r, b = slice(HD * par, HD * par + HD), hb[par]
                    for l in range(32):
                        rhs = kvc[r, 2 * j:2 * j + 2, l:l + 225:16]
                        o = ps[b][:, 0:30].rearrange("p (a b) -> p a b", a=2)
                        fn = lambda e, l=l, r=r, w1=w1, rhs=rhs, o=o: e.matmul(o, w1[r, l, :], rhs, start=(l == 0), stop=(l == 31))
                        if l == 31:
                            t = PE.op(fn)
                        else:
                            PE.quiet(fn, k_kvc, free[b])
                    hk.append(AC.op(lambda e, j=j, b=b, hid=hid, par=par: e.activation(
                        hid[:, 30 * par:30 * par + 30], ps[b][:, 0:30], ACT.Gelu_apprx_tanh, bias=cb[:, 4 + j:5 + j]), t, kb))
                    free[b] = [hk[-1]]
                loads[n]["released"] = t
                hid_k.append(hk)
                free[bb] = [kb]
            t = PE.op(lambda e: e.matmul(ps[0][:, 0:60], w2[:, 0:P], hidk, start=True, stop=True), hid_k[0], free[0], k_sm)
            t = kraw = AC.op(lambda e: e.activation(kcT, ps[0][:, 0:60], ACT.Identity, bias=cb[:, 2:3]), t)
            t = AC.op(lambda e: e.activation(sq60, kcT, ACT.Square), t)
            t = PE.op(lambda e: e.matmul(ps[0][:, 64:124], C("halves"), sq60, start=True, stop=True), t)
            t = DV.op(lambda e: e.tensor_scalar(rs60, ps[0][:, 64:124], 1.0 / HD, RMS_EPS, ALU.mult, ALU.add), t)
            t = AC.op(lambda e: e.activation(rs60, rs60, ACT.Sqrt), t)
            t = DV.op(lambda e: e.reciprocal(rs60, rs60), t)
            k_kc = DV.op(lambda e: e.scalar_tensor_tensor(kcT, kcT, hg[:, 5:6], rs60, ALU.mult, ALU.mult), t, kraw)
            free[0] = [t]
            t0 = DV.op(lambda e: e.memset(hidr, 0.0))
            h4 = hidr.rearrange("p g (i c) -> p g i c", i=4)[:, :, :, 0:NCMP]
            t = DV.op(lambda e: e.tensor_copy(h4, hidv.rearrange("p (g c) -> p g c", c=NCMP).unsqueeze(2).to_broadcast([P, 4, 4, NCMP])), t0, hid_k[1])
            vp = ps[1][:, 0:256].rearrange("p (g d) -> p g d", d=HD)
            for g in range(4):
                t2 = PE.op(lambda e, g=g: e.matmul(vp[:, g, :], hidr[:, g, :], w2[:, 128:192], start=True, stop=True), t, free[1])
            k_vc = DV.op(lambda e: e.tensor_tensor(vcr, vp, b2b.unsqueeze(1).to_broadcast([P, 4, HD]), ALU.add), t2, k_sm)
            free[1] = [k_vc]
            cp = [ps[2 + par][:, 0:NT * NH * NCMP].rearrange("p (a c) -> p a c", c=NCMP) for par in range(2)]
            for tt in range(NT):
                for h in range(NH):
                    g = h // 4
                    par, i, gi = g % 2, (g // 2) * 4 + h % 4, (g % 2) * 2 + g // 2
                    r = slice(HD * par, HD * par + HD)
                    t = PE.op(lambda e, tt=tt, h=h, par=par, r=r, i=i, gi=gi: e.matmul(
                        cp[par][:, tt * NH + h, :], qT[r, i, tt * P:tt * P + P], kcT[r, gi * NCMP:gi * NCMP + NCMP], start=True, stop=True),
                        free[2], free[3], k_kc, kq)
            cm, cl = S_(NT * NH), S_(NT * NH)
            b3 = lambda v: v.unsqueeze(2).to_broadcast([P, NT * NH, NCMP])
            k = []
            by_par = lambda v, tt, par: v[:, tt * NH:tt * NH + NH, :].rearrange("p (a b j) c -> p a b j c", b=2, j=4)[:, :, par, :, :]
            for tt in range(NT):
                for par in range(2):
                    bt = btab[:, tt, :, :].rearrange("p c (a b j) -> p a b j c", b=2, j=4)[:, :, par, :, :]
                    k.append(DV.op(lambda e, tt=tt, par=par, bt=bt: e.tensor_tensor(by_par(cs, tt, par), by_par(cp[par], tt, par), bt, ALU.add), t))
            free[2] = free[3] = k
            t = DV.op(lambda e: e.tensor_reduce(cm, cs, AX.X, ALU.max), k)
            t = DV.op(lambda e: e.tensor_scalar(cm, cm, NEG / 10, None, ALU.max), t)
            t = DV.op(lambda e: e.tensor_tensor(cs, cs, b3(cm), ALU.subtract), t)
            t = AC.op(lambda e: e.activation(cs, cs, ACT.Exp), t)
            t = DV.op(lambda e: e.tensor_reduce(cl, cs, AX.X, ALU.add), t)
            t = DV.op(lambda e: e.tensor_scalar(cl, cl, 1e-30, None, ALU.max), t)
            t = DV.op(lambda e: e.reciprocal(cl, cl), t)
            g3 = gt.rearrange("p t (h b) -> p t h b", b=3)
            t = DV.op(lambda e: e.tensor_tensor(cl.rearrange("p (t h) -> p t h", t=NT), cl.rearrange("p (t h) -> p t h", t=NT), g3[:, :, :, 0], ALU.mult), t, k_gt)
            t0 = DV.op(lambda e: e.memset(pc, 0.0))
            kpc = DV.op(lambda e: e.tensor_tensor(pc[:, :, 0:NCMP], cs, b3(cl), ALU.mult), t, t0)
            k_pc = []
            for g in range(4):
                b = g % 2
                for tt in range(NT):
                    i_ = pc[:, tt * NH + 4 * g:tt * NH + 4 * g + 4, :].rearrange("p a b -> p (a b)")
                    t = PE.op(lambda e, b=b, tt=tt, i_=i_: e.transpose(ps[b][:, tt * P:tt * P + P], i_, ident), kpc, free[b])
                k = DV.op(lambda e, b=b, g=g: e.tensor_copy(pcT[:, g, :], ps[b][:, 0:S]), t)
                free[b] = [k]
                k_pc.append(k)

            ko, pend = [], {}
            scr_free, pT_free = {}, {}
            jobs = [(i, par, br) for i in range(8) for par in range(2) for br in range(2)]

            def first(n):
                i, par, br = jobs[n]
                h = (i // 4) * 8 + par * 4 + i % 4
                kt, ktok = ((ksT, ks), (kwT, kw))[br]
                used, k = soft_scores(qT, kt, i, i // 4, par, n % 4, bias[i % 3][:, par, :], k_bias[i], kq[i // 4] + ktok,
                                      scr[n % 4], stats[n % 4], scr_free.get(n - 4), g3[:, :, h, 1 + br])
                if par and br:
                    b_used[i] = used
                    if i + 3 < 8:
                        fetch(i + 3)
                pend[n] = k

            def second(n):
                i, par, br = jobs[n]
                g = (i // 4) * 2 + par
                scr_free[n], k = soft_turn(scr[n % 4], pend[n], 4 + n % 2, pT[n % 4], pT_free.get(n - 4))
                b = 6 + i % 2
                r = slice(HD * par, HD * par + HD)
                vv, vt = ((Vs, kvs), (Vw, kvw))[br]
                PE.wait(vt, free[b] if par == 0 and br == 0 else None)
                if br == 0:
                    hi = i % 4
                    gi = par * 2 + i // 4
                    q = slice(32 * hi, 32 * hi + 32)
                    PE.quiet(lambda e: e.matmul(ps[b][r, 0:S], vcr[q, gi, :], pcT[q, g, :], start=True, stop=False), k_pc, k_vc)
                PE.quiet(lambda e: e.matmul(ps[b][r, 0:S], vv[:, 0, g * HD:g * HD + HD], pT[n % 4][:, 0:S], start=False, stop=False), k)
                t = PE.op(lambda e: e.matmul(ps[b][r, P:S], vv[:, 1, g * HD:g * HD + HD], pT[n % 4][:, S:384], start=False, stop=(br == 1)))
                pT_free[n] = t
                if par and br:
                    k = AC.op(lambda e: e.activation(oT[:, i, :], ps[b][:, 0:S], ACT.Copy), t)
                    free[b] = [k]
                    ko.append(k)

            for n in range(len(jobs) + 2):
                if n < len(jobs):
                    first(n)
                if n >= 2:
                    second(n - 2)
            return out_and_residual(oT, ko)

        def swiglu(layer, toks):
            A = stage()
            kr = rms_to(toks)
            kx = transposed(R, kr, gains[:, 3 * layer + 1, :])
            hT = A.take(FC, S)
            sil = [A.take(512) for _ in range(2)]
            kh = []
            for j in range(FC // 2):
                view, arrived, n = next_slot()
                bb = (4 + 2 * (j % 2), 5 + 2 * (j % 2))
                PE.wait(arrived, kx)
                tk = []
                for m in range(2):
                    w = view[:, 2048 * m:2048 * m + 2048].rearrange("p (c n) -> p c n", c=8)
                    for i in range(2):
                        o = ps[bb[m]][:, i * S:i * S + S]
                        for c in range(DC):
                            fn = lambda e, c=c, i=i, o=o, w=w: e.matmul(o, w[:, c, i * P:i * P + P], XT[:, c, :], start=(c == 0), stop=(c == DC - 1))
                            if c == DC - 1 and i == 1:
                                t = PE.op(fn)
                            else:
                                PE.quiet(fn, free[bb[m]])
                    tk.append(t)
                loads[n]["released"] = t
                a = AC.op(lambda e, j=j, bb=bb: e.activation(sil[j % 2], ps[bb[0]][:, :], ACT.Silu), tk[0], kh[j - 2] if j >= 2 else None)
                k = DV.op(lambda e, j=j, bb=bb: e.tensor_tensor(hT[:, 2 * j:2 * j + 2, :].rearrange("p a b -> p (a b)"), sil[j % 2], ps[bb[1]][:, :], ALU.mult), a, tk[1])
                free[bb[0]], free[bb[1]] = [a], [k]
                kh.append(k)
            slots = [(next_slot(), 4) for _ in range(5)] + [(next_slot(), 2)]
            k = by_tokens(lambda c: hT[:, c, :], slots, [0, 1, 2, 3], kh, FC)
            return residual([0, 1, 2, 3], k, 1.0, X)

        def ple(layer, toks):
            A = stage()
            kr = rms_to(toks)
            kx = transposed(R, kr, gains[:, 3 * layer + 2, :])
            G = A.take(NT, D)
            k = by_tokens(lambda c: XT[:, c, :], [(next_slot(), 4), (next_slot(), 4)], [4, 5, 6, 7], kx, 8)
            ka = []
            for tt in range(NT):
                for h in range(2):
                    b = 4 + 2 * tt + h
                    ka.append(AC.op(lambda e, tt=tt, h=h, b=b: e.activation(G[:, tt, h * 512:h * 512 + 512], ps[b][:, :], ACT.Sigmoid), k[2 * tt + h]))
                    free[b] = [ka[-1]]
            slot = next_slot()
            pT = slot[0][:, 2048:2560].rearrange("p (c n) -> p c n", c=2)
            k = by_tokens(lambda c: pT[:, c, :], [(slot, 2)], [0, 1, 2, 3], [], 2)
            r = []
            for tt in range(NT):
                for h in range(2):
                    b = 2 * tt + h
                    sl = slice(h * 512, h * 512 + 512)
                    t = DV.op(lambda e, tt=tt, b=b, sl=sl: e.tensor_tensor(G[:, tt, sl], G[:, tt, sl], ps[b][:, :], ALU.mult), ka[b], k[b])
                    free[b] = [t]
                    r.append(DV.op(lambda e, tt=tt, sl=sl: e.tensor_tensor(X[:, tt, sl], X[:, tt, sl], G[:, tt, sl], ALU.add), t))
            return r

        gb = load_ln(I["ln_mix_g"][0], I["ln_mix_b"][0])
        t = conv_mixer()
        t = layer_norm(t, gb)
        gb = load_ln(I["ln_ffn_g"][0], I["ln_ffn_b"][0])
        t = moe(0, t)
        t = layer_norm(t, gb)
        gb = load_ln(I["ln_mix_g"][1], I["ln_mix_b"][1])
        t = stick(t)
        t = layer_norm(t, gb)
        gb = load_ln(I["ln_ffn_g"][1], I["ln_ffn_b"][1])
        t = moe(1, t)
        t = layer_norm(t, gb)
        for layer in range(DEPTH):
            t = mixer_ab(t) if layer == 0 else mixer_nsa(t)
            t = swiglu(layer, t)
            t = ple(layer, t)
        assert taken[0] == len(loads)

        for n, l in enumerate(loads):
            for layer in range(DEPTH):
                if n == moe_end[layer]:
                    put_branch(SP, sp_branch[layer])
            i = n % NRING
            if n >= NRING:
                SP.wait(loads[n - NRING]["released"])
            for view, src in l["pieces"]:
                SP.items.append(("inc", lambda e, i=i, view=view, src=src: e.dma_start(view(ring[:, i, :]), src), c_ring[i].sem, 16))
        SP.dma(lambda e: e.dma_start(out[0].rearrange("(t p) d -> p t d", p=P), X[:, :, :]), c_out, t)
        SP.wait((c_out.sem, 16))

        block = ctx.enter_context(nc.Block())
        block.sync(lambda e: SP.play(e))
        block.scalar(lambda e: AC.play(e))
        block.vector(lambda e: DV.play(e))
        block.gpsimd(lambda e: PL.play(e))
        block.tensor(lambda e: PE.play(e))


def put_branch(q, what):
    ready, cond, body = what
    q.wait(ready)
    q.items.append(("if", cond, body))


_PLAIN = ["x", "even_w_in", "even_w_out", "odd_w_qkv", "odd_w_o", "ln_mix_g", "ln_mix_b", "ln_ffn_g", "ln_ffn_b",
          "expert_w_up", "expert_w_down", "rel_bias_2",
          "w_ffn_gate_2", "w_ffn_up_2", "w_ffn_down_2", "w_ple_proj_2", "w_ple_gate_2", "w_in_ab_2", "w_out_ab_2",
          "cmp_k_w1_2", "cmp_v_w1_2", "cmp_v_b2_2"]
_HEAD_GAINS = ["qn_moba_2", "kn_moba_2", "qn_dil_2", "kn_dil_2", "qn_nsa_2", "kn_cmp_2", "kn_slc_2", "kn_win_2"]


def kernel(**inputs):
    import numpy as _np
    import concourse.bacc as _bacc
    from concourse import mybir as _mybir
    from concourse.bass_utils import run_bass_kernel_spmd as _run

    a = {n: _np.ascontiguousarray(inputs[n]) for n in _PLAIN}
    asis = {n: _np.asarray(inputs[n]) for n in inputs}
    chan = lambda v: _np.asarray(v).reshape(-1, 128).T
    twice = lambda v: _np.concatenate([v, v], axis=0)
    a["conv_taps"] = _np.ascontiguousarray(_np.concatenate(
        [asis["even_conv_b_w"][0].reshape(31, 4, 128).transpose(2, 1, 0), asis["even_conv_a"][0].reshape(3, 4, 128).transpose(2, 1, 0)]
        + [chan(asis[n][0])[:, :, None] for n in ("even_conv_b_bias", "even_norm_b_g", "even_norm_b_b")], axis=2))
    a["gains"] = _np.ascontiguousarray(_np.stack(
        [chan(asis[n][i]) for i in range(2) for n in ("norm_mix_2", "norm_ffn_2", "norm_ple_2")], axis=1))
    a["head_gains"] = _np.ascontiguousarray(_np.stack([twice(asis[n][0]) for n in _HEAD_GAINS], axis=1))
    a["cmp_small"] = _np.ascontiguousarray(_np.concatenate(
        [asis["cmp_k_w2_2"][0], asis["cmp_k_w2_2"][0], asis["cmp_v_w2_2"][0],
         _np.concatenate([asis["cmp_k_pos_2"][0].T, asis["cmp_v_pos_2"][0].T], axis=0),
         asis["cmp_k_b1_2"][0][:, None], asis["cmp_v_b1_2"][0][:, None], twice(asis["cmp_k_b2_2"][0])[:, None]], axis=1))
    a["router_w"] = _np.concatenate([asis["router_group_w"], asis["router_expert_w"]], axis=2)
    a["router_b"] = _np.concatenate([asis["router_group_b"], asis["router_expert_b"]], axis=1)
    a["p_2"] = _np.ascontiguousarray(asis["p_2"][:, 0].transpose(0, 2, 1))
    w = asis["w_in_nsa_2"]
    q = w[:, :, :1024].reshape(1, 1024, 2, 2, 4, 64).transpose(0, 1, 2, 4, 3, 5).reshape(1, 1024, 1024)
    a["w_in_nsa_2"] = _np.concatenate([q, w[:, :, 1024:]], axis=2)
    a["w_out_nsa_2"] = _np.ascontiguousarray(
        asis["w_out_nsa_2"].reshape(1, 2, 2, 4, 64, 1024).transpose(0, 1, 3, 2, 4, 5).reshape(1, 1024, 1024))
    a["consts"] = CONSTS
    a["bias_tables"] = BIAS_TABLES

    nc = _bacc.Bacc("TRN2", target_bir_lowering=False, num_devices=1)
    arrays, aps = {}, {}
    for n, v in a.items():
        arrays[f"in_{n}"] = v
        aps[n] = nc.dram_tensor(f"in_{n}", v.shape, _mybir.dt.from_np(v.dtype), kind="ExternalInput").ap()
    out = nc.dram_tensor("out_0", (1, 256, 1024), _mybir.dt.float32, kind="ExternalOutput").ap()
    bass_two_blocks_kernel(nc, aps, out)
    r = _run(nc, [arrays], core_ids=[0])
    return r.results[0]["out_0"]
```

```python
from contextlib import ExitStack

import numpy as np

import concourse.bass as bass
from concourse import mybir

F32 = mybir.dt.float32
I32 = mybir.dt.int32
U32 = mybir.dt.uint32
F32R = mybir.dt.float32r
ALU = mybir.AluOpType
ACT = mybir.ActivationFunctionType
AX = mybir.AxisListType

P = 128
S = 256
D = 1024
DC = D // P
NT = S // P
DEPTH = 2
NE = 32
NG = 4
F_E = 512
NH = 16
HD = 64
FFN = 2816
FC = FFN // P
NCMP = 15
ALPHA = (2 * DEPTH) ** 0.25
LN_EPS = 1e-5
RMS_EPS = 1e-6
NEG = -1e30
BIG = 3e38

WIN = 64
NOV = S * 2 // WIN - 1
SLOTS = 2 * S
YR = NE * WIN
NRING = 6
RW = 2048
NB = 4
PC = 1024

CONST_COLS = {}


def host_constants():
    p = np.arange(P)[:, None]
    j = np.arange(P)[None, :]
    parts = [
        ("ident", p == j),
        ("ones", np.ones((P, P))),
        ("before", p < j),
        ("suffix", p >= j),
        ("halves", (p // HD) == (j // HD)),
        ("fold", (p % WIN) == np.arange(WIN)[None, :]),
        ("strict", np.concatenate([np.where(p < j, 0.0, NEG), np.zeros((P, P)), np.where(p < j, 0.0, NEG)], 1)),
        ("slot", np.broadcast_to(np.arange(SLOTS), (P, SLOTS))),
        ("io32m", np.broadcast_to(np.arange(NE) - 64, (P, NE))),
        ("io32", np.broadcast_to(np.arange(NE), (P, NE))),
        ("io4m", np.broadcast_to(np.arange(NG) - 64, (P, NG))),
        ("io7", np.broadcast_to(np.arange(NOV), (P, NOV))),
    ]
    at = 0
    for name, a in parts:
        CONST_COLS[name] = (at, at + a.shape[1])
        at += a.shape[1]
    return np.concatenate([np.asarray(a, np.float32) for _, a in parts], 1)


def bucket_of(n):
    n = max(int(n), 0)
    if n < 16:
        return n
    return min(16 + int(np.log(np.float32(n / 16)) / np.log(2048 / 16) * 16), 31)


def host_bias_tables():
    W = 384
    a = np.zeros((33, 2, W), np.float32)
    for col in range(W - 1):
        d = col - 127
        if d < 0:
            a[32, :, col] = NEG
            continue
        a[bucket_of(d), :, col] = 1.0
        count = (d <= 128) + (d % 4 == 0) + (d % 16 == 0)
        a[32, 1, col] = np.log(count) if count else NEG
    c = np.zeros((33, NCMP, S), np.float32)
    for k in range(NCMP):
        for t in range(S):
            d = t - (16 * k + 31)
            if d >= 0:
                c[bucket_of(d), k, t] = 1.0
            else:
                c[32, k, t] = NEG
    return np.concatenate([a.reshape(33, -1), c.reshape(33, -1)], 1)


CONSTS = host_constants()
BIAS_TABLES = host_bias_tables()


class Queue:

    def __init__(self, sem):
        self.sem, self.n, self.items, self.seen = sem, 0, [], {}

    def wait(self, *toks):
        for t in toks:
            if t is None:
                continue
            if isinstance(t, list):
                self.wait(*t)
                continue
            sem, v = t
            if self.seen.get(sem.name, 0) < v:
                self.seen[sem.name] = v
                self.items.append(("wait", sem, v))

    def op(self, fn, *toks):
        self.wait(*toks)
        self.n += 1
        self.items.append(("inc", fn, self.sem, 1))
        return self.sem, self.n

    def quiet(self, fn, *toks):
        self.wait(*toks)
        self.items.append(("plain", fn))

    def dma(self, fn, counter, *toks):
        self.wait(*toks)
        self.items.append(("inc", fn, counter.sem, 16))
        return counter.next(16)

    def last(self):
        return (self.sem, self.n) if self.n else None

    def branch(self, cond):
        q = Queue(None)
        q.seen = dict(self.seen)
        self.items.append(("if", cond, q))
        return q

    def bump(self, fn, counter, *toks):
        self.wait(*toks)
        self.items.append(("inc", fn, counter.sem, 1))
        return counter.next(1)

    def play(self, e):
        for it in self.items:
            if it[0] == "wait":
                e.wait_ge(it[1], it[2])
            elif it[0] == "inc":
                it[1](e).then_inc(it[2], it[3])
            elif it[0] == "plain":
                it[1](e)
            else:
                with e.If(it[1](e)):
                    it[2].play(e)


class Counter:
    def __init__(self, sem):
        self.sem, self.n = sem, 0

    def next(self, by):
        self.n += by
        return self.sem, self.n


def bass_two_blocks_kernel(nc, I, out):
    ctx = ExitStack()
    with ctx:
        def sb(name, shape, dt=F32):
            return ctx.enter_context(nc.sbuf_tensor(name, shape, dt))

        def sem(name):
            return ctx.enter_context(nc.semaphore(name))

        CW = CONSTS.shape[1]
        cst = sb("cst", [P, CW])
        X = sb("X", [P, NT, D])
        XH = sb("XH", [P, DC, S], F32R)
        XL = sb("XL", [P, DC, S], F32R)
        R = sb("R", [P, NT, D])
        GB = sb("GB", [P, 2, D])
        ring = sb("ring", [P, NRING, RW])
        whi = sb("whi", [P, NB, PC], F32R)
        wlo = sb("wlo", [P, NB, PC], F32R)
        AW = 12800
        arena = sb("arena", [P, AW])
        ARW = 5120
        arena_r = sb("arena_r", [P, ARW], F32R)
        small = sb("small", [P, 1100])
        oi = sb("oi", [1, 64], I32)
        yi = sb("yi", [P, 2 * NT], U32)
        ps = [ctx.enter_context(nc.psum_tensor(f"ps{i}", [P, 512], F32)) for i in range(8)]

        ys = nc.dram_tensor("ys", [YR + SLOTS + WIN, D], F32, kind="Internal").ap()
        tv = nc.dram_tensor("tv", [2, NH, 384], F32, kind="Internal").ap()

        PE, DV, AC, PL = (Queue(sem(n)) for n in ("s_pe", "s_dve", "s_act", "s_pool"))
        SP = Queue(sem("s_sp"))
        c_in = Counter(sem("s_in"))
        c_ring = [Counter(sem(f"s_ring{i}")) for i in range(NRING)]
        c_gb = Counter(sem("s_gb"))
        c_rw = Counter(sem("s_rw"))
        c_y = [Counter(sem(f"s_y{i}")) for i in range(2)]
        c_yg = Counter(sem("s_yg"))
        c_tv = Counter(sem("s_tv"))
        c_bias = [Counter(sem(f"s_bias{i}")) for i in range(3)]
        c_sm = Counter(sem("s_sm"))
        c_out = Counter(sem("s_out"))
        c_ov = [{n: Counter(sem(f"s_ov_{n}{l}")) for n in ("dma", "pe", "act", "dve", "pool", "y")} for l in range(DEPTH)]

        def C(name, rows=P):
            a, b = CONST_COLS[name]
            return cst[0:rows, a:b]

        ident, ones = C("ident"), C("ones")

        def shaped(v, shape):
            if len(shape) == 2:
                return v.rearrange("p (a b) -> p a b", b=shape[1])
            if len(shape) == 3:
                return v.rearrange("p (a b c) -> p a b c", b=shape[1], c=shape[2])
            return v

        class Area:

            def __init__(self):
                self.at = self.at_r = 0

            def take(self, *shape):
                v = arena[:, self.at:self.at + int(np.prod(shape))]
                self.at += int(np.prod(shape))
                assert self.at <= AW, self.at
                return shaped(v, shape)

            def take_r(self, *shape):
                v = arena_r[:, self.at_r:self.at_r + int(np.prod(shape))]
                self.at_r += int(np.prod(shape))
                assert self.at_r <= ARW, self.at_r
                return shaped(v, shape)

        sm_at = [0]

        def S_(*shape):
            n = int(np.prod(shape))
            v = small[:, sm_at[0]:sm_at[0] + n]
            sm_at[0] += n
            assert sm_at[0] <= 1100
            return shaped(v, shape)

        def stage():
            toks = [q.last() for q in (PE, DV, AC, PL)]
            for q in (PE, DV, AC, PL):
                q.wait(toks)
            for i in range(8):
                free[i] = None
            sm_at[0] = 0
            return Area()

        free = [None] * 8

        loads = []

        pieces = []

        def load(*parts, split=True):
            n = len(loads)
            loads.append({"parts": parts, "released": None, "arrived": [c_ring[n % NRING].next(16) for _ in parts][-1]})
            if split:
                pieces.extend((n, h) for h in range(RW // PC))
            else:
                raw.append(n)

        taken, prepared, next_raw = [0], [0], [0]
        piece_free = {}

        def arrived(n):
            return loads[n]["arrived"]

        def prepare(k):
            n, h = pieces[k]
            src = ring[:, n % NRING, h * PC:h * PC + PC]
            hi, lo = whi[:, k % NB, :], wlo[:, k % NB, :]
            t = AC.op(lambda e: e.activation(hi, src, ACT.Copy), arrived(n), piece_free.get(k - NB))
            t = DV.op(lambda e: e.tensor_tensor(lo, src, hi.bitcast(F32), ALU.subtract), t)
            loads[n]["released"] = t
            ready[k] = t

        ready = {}

        raw = []

        def raw_slots(n):
            next_raw[0] += n
            return raw[next_raw[0] - n:next_raw[0]]

        def next_piece():
            k = taken[0]
            taken[0] += 1
            while prepared[0] < min(k + NB, len(pieces)):
                prepare(prepared[0])
                prepared[0] += 1
            return whi[:, k % NB, :], wlo[:, k % NB, :], ready[k], k

        def rows2(w, r0):
            return lambda s: s.rearrange("p (c n) -> p c n", c=2), w[r0:r0 + 256, :].rearrange("(c p) n -> p c n", p=P)

        def rows(w, r0, n):
            for r in range(r0, r0 + n, 256):
                load(rows2(w, r))

        def cols(w, c0):
            for r in (0, 512):
                load((lambda s: s.rearrange("p (c n) -> p c n", c=4), w[r:r + 512, c0:c0 + 512].rearrange("(c p) n -> p c n", p=P)))

        def cols256(w, c0):
            load((lambda s: s.rearrange("p (c n) -> p c n", c=8), w[:, c0:c0 + 256].rearrange("(c p) n -> p c n", p=P)))

        def plan_loads():
            w = I["even_w_in"][0]
            for i in range(2):
                cols256(w, 1536 + 256 * i)
                cols256(w, 2048 + 256 * i)
            for c0 in (512, 1024, 0):
                for i in range(2):
                    cols256(w, c0 + 256 * i)
            rows(I["even_w_out"][0], 0, 1024)
            moe_loads(0)
            w = I["odd_w_qkv"][0]
            for c0 in range(0, 2048, 256):
                cols256(w, c0)
            rows(w[:, 2048:3072], 0, 1024)
            rows(I["odd_w_o"][0], 0, 1024)
            moe_loads(1)
            for i in range(DEPTH):
                if i == 0:
                    for c0 in range(0, 3072, 512):
                        cols(I["w_in_ab_2"][0], c0)
                    wo = I["w_out_ab_2"][0]
                else:
                    w = I["w_in_nsa_2"][0]
                    for c0 in (0, 512):
                        cols(w, c0)
                    for c0 in (1024, 1280):
                        cols256(w, c0)
                    for c0 in (1536, 2048):
                        cols(w, c0)
                    for name in ("cmp_k_w1_2", "cmp_v_w1_2"):
                        src = I[name][0].rearrange("(l d) c -> d l c", d=HD)
                        for l in (0, 16):
                            load(*((lambda s, h=h: s[HD * h:HD * h + HD, :].rearrange("p (l c) -> p l c", c=P), src[:, l:l + 16, :]) for h in range(2)), split=False)
                    wo = I["w_out_nsa_2"][0]
                rows(wo, 0, 1024)
                for j in range(FC // 2 + 1):
                    if j < FC // 2:
                        cols256(I["w_ffn_gate_2"][i], 256 * j)
                        cols256(I["w_ffn_up_2"][i], 256 * j)
                    if j:
                        rows(I["w_ffn_down_2"][i], 256 * (j - 1), 256)
                rows(I["w_ple_gate_2"][i], 0, 1024)
                rows(I["w_ple_proj_2"][i], 0, 256)

        moe_end = []

        def moe_loads(layer):
            for e in range(NE + 1):
                if e < NE:
                    rows(I["expert_w_up"][layer, e], 0, 1024)
                if e:
                    rows(I["expert_w_down"][layer, e - 1], 0, 512)
            moe_end.append(len(loads))

        plan_loads()

        def transposed(src, toks, gain=None):
            done = []
            for b in range(4):
                bank = ps[b]
                for q in range(4):
                    dc, tt = 2 * b + q // 2, q % 2
                    o, i = bank[:, q * P:q * P + P], src[:, tt, dc * P:dc * P + P]
                    fn = lambda e, o=o, i=i: e.transpose(o, i, ident)
                    if q < 3:
                        PE.quiet(fn, free[b], toks)
                    else:
                        t = PE.op(fn, free[b], toks)
                if gain is None:
                    oh, ol = (v[:, 2 * b:2 * b + 2, :].rearrange("p a b -> p (a b)") for v in (XH, XL))
                    k = AC.op(lambda e, oh=oh, bank=bank: e.activation(oh, bank[:, :], ACT.Copy), t)
                    k = DV.op(lambda e, oh=oh, ol=ol, bank=bank: e.tensor_tensor(ol, bank[:, :], oh.bitcast(F32), ALU.subtract), k)
                else:
                    ks = []
                    for h in range(2):
                        dc = 2 * b + h
                        i, g = bank[:, h * S:h * S + S], gain[:, dc:dc + 1]
                        ks.append(AC.op(lambda e, dc=dc, i=i, g=g: e.activation(XH[:, dc, :], i, ACT.Copy, scale=g), t))
                    for h in range(2):
                        dc = 2 * b + h
                        i, g = bank[:, h * S:h * S + S], gain[:, dc:dc + 1]
                        k = DV.op(lambda e, dc=dc, i=i, g=g: e.scalar_tensor_tensor(
                            XL[:, dc, :], i, g, XH[:, dc, :].bitcast(F32), ALU.mult, ALU.subtract), ks)
                free[b] = [k]
                done.append(k)
            return done

        def part(src, hi, lo, toks):
            t = AC.op(lambda e: e.activation(hi, src, ACT.Copy), toks)
            return DV.op(lambda e: e.tensor_tensor(lo, src, hi.bitcast(F32), ALU.subtract), t)

        def by_tokens(lhs, n_chunks, banks, toks, chunks, c0=0):
            for c in range(c0, c0 + n_chunks):
                wh, wl, tok, k = next_piece()
                PE.wait(tok)
                lh, ll = lhs(c)
                for tt in range(NT):
                    for l, w, first, last in ((lh, wl, True, False), (lh, wh, False, False), (ll, wh, False, True)):
                        for h in range(2):
                            b = banks[2 * tt + h]
                            if c == 0:
                                PE.wait(free[b])
                            fn = lambda e, b=b, l=l[:, tt * P:tt * P + P], w=w[:, h * 512:h * 512 + 512], a=c == 0 and first, z=c == chunks - 1 and last: e.matmul(
                                ps[b][:, :], l, w, start=a, stop=z)
                            if last and ((tt == 1 and h == 1) or c == chunks - 1):
                                t = done[b] = PE.op(fn, toks)
                            else:
                                PE.quiet(fn, toks)
                piece_free[k] = t
            return [done[b] for b in banks]

        def by_channels(n_out, banks, toks, first=()):
            for hf in range(2):
                wh, wl, tok, k = next_piece()
                PE.wait(tok, toks)
                wh, wl = (v.rearrange("p (c n) -> p c n", c=4) for v in (wh, wl))
                for i in range(n_out):
                    PE.wait(free[banks[i]])
                    o, cs_ = ps[banks[i]][:, 0:S], slice(i * P, i * P + P)
                    for c in range(4):
                        x = 4 * hf + c
                        PE.quiet(lambda e, o=o, cs_=cs_, c=c, x=x, wl=wl: e.matmul(o, wl[:, c, cs_], XH[:, x, :], start=(x == 0), stop=False))
                        PE.quiet(lambda e, o=o, cs_=cs_, c=c, x=x, wh=wh: e.matmul(o, wh[:, c, cs_], XL[:, x, :], start=False, stop=False))
                        fn = lambda e, o=o, cs_=cs_, c=c, x=x, wh=wh: e.matmul(o, wh[:, c, cs_], XH[:, x, :], start=False, stop=(x == 7))
                        if c == 3:
                            t = PE.op(fn)
                        else:
                            PE.quiet(fn)
                        if x == 7:
                            done[banks[i]] = t
                piece_free[k] = t
            return [done[b] for b in banks]

        def by_token_cols(groups, toks):
            for q in range(4):
                wh, wl, tok, k = next_piece()
                PE.wait(tok, toks)
                wh, wl = (v.rearrange("p (c n) -> p c n", c=2) for v in (wh, wl))
                for tt in range(NT):
                    for c0, n, banks in groups:
                        PE.wait(free[banks[tt]] if q == 0 else None)
                    for c in range(2):
                        x, rows_ = 2 * q + c, slice(tt * P, tt * P + P)
                        for l, w, first, last in ((XH, wl, True, False), (XH, wh, False, False), (XL, wh, False, True)):
                            for c0, n, banks in groups:
                                b = banks[tt]
                                fn = lambda e, b=b, l=l[:, x, rows_], w=w[:, c, c0:c0 + n], n=n, a=x == 0 and first, z=x == 7 and last: e.matmul(
                                    ps[b][:, 0:n], l, w, start=a, stop=z)
                                if last and (c == 1):
                                    t = done[b] = PE.op(fn)
                                else:
                                    PE.quiet(fn)
                piece_free[k] = t
            return [[done[b] for b in banks] for _, _, banks in groups]

        done = [None] * 8

        def residual(banks, toks, scale, dst):
            r = []
            for tt in range(NT):
                for h in range(2):
                    b = banks[2 * tt + h]
                    sl = slice(h * 512, h * 512 + 512)
                    k = DV.op(lambda e, b=b, tt=tt, sl=sl: e.scalar_tensor_tensor(
                        dst[:, tt, sl], X[:, tt, sl], float(scale), ps[b][:, :], ALU.mult, ALU.add), toks[2 * tt + h])
                    free[b] = [k]
                    r.append(k)
            return r

        gb_free = [None]

        def load_ln(g, b):
            PL.dma(lambda e: e.dma_start(GB[:, 0, :], g.partition_broadcast(P)), c_gb, gb_free[0])
            return PL.dma(lambda e: e.dma_start(GB[:, 1, :], b.partition_broadcast(P)), c_gb)

        def layer_norm(toks, gb):
            st, ag, rs, nb = S_(2 * NT, 6), S_(NT, 2), S_(NT), S_(NT)
            res = []
            for tt in range(NT):
                k = [DV.op(lambda e, tt=tt, h=h: e.bn_stats(st[:, 2 * tt + h, :], R[:, tt, h * 512:h * 512 + 512]), toks)
                     for h in range(2)]
                k = DV.op(lambda e, tt=tt: e.bn_aggr(ag[:, tt, :], st[:, 2 * tt:2 * tt + 2, :]), k)
            k = DV.op(lambda e: e.tensor_scalar(rs, ag[:, :, 1], LN_EPS, None, ALU.add), k)
            k = AC.op(lambda e: e.activation(rs, rs, ACT.Sqrt), k)
            k = DV.op(lambda e: e.reciprocal(rs, rs), k)
            k = DV.op(lambda e: e.scalar_tensor_tensor(nb, ag[:, :, 0], -1.0, rs, ALU.mult, ALU.mult), k)
            for tt in range(NT):
                t = AC.op(lambda e, tt=tt: e.activation(R[:, tt, :], R[:, tt, :], ACT.Identity, scale=rs[:, tt:tt + 1],
                                                        bias=nb[:, tt:tt + 1]), k)
                t = DV.op(lambda e, tt=tt: e.tensor_tensor(R[:, tt, :], R[:, tt, :], GB[:, 0, :], ALU.mult), t, gb)
                t = DV.op(lambda e, tt=tt: e.tensor_tensor(X[:, tt, :], R[:, tt, :], GB[:, 1, :], ALU.add), t)
                res.append(t)
            gb_free[0] = res[-1]
            return res

        def rms_to(toks):
            ss, rs = S_(NT), S_(NT)
            k = []
            for tt in range(NT):
                k.append(AC.op(lambda e, tt=tt: e.activation(R[:, tt, :], X[:, tt, :], ACT.Square, accum_out=ss[:, tt:tt + 1]), toks))
            t = DV.op(lambda e: e.tensor_scalar(rs, ss, 1.0 / D, RMS_EPS, ALU.mult, ALU.add), k)
            t = AC.op(lambda e: e.activation(rs, rs, ACT.Sqrt), t)
            t = DV.op(lambda e: e.reciprocal(rs, rs), t)
            return [DV.op(lambda e, tt=tt: e.tensor_scalar(R[:, tt, :], X[:, tt, :], rs[:, tt:tt + 1], None, ALU.mult), t)
                    for tt in range(NT)]

        k_cst = AC.dma(lambda e: e.dma_start(cst[:, :], I["consts"]), c_in)
        k_x = AC.dma(lambda e: e.dma_start(X[:, :, :], I["x"][0].rearrange("(t p) d -> p t d", p=P)), c_in)
        gains = sb("gains", [P, 6, DC])
        hg = sb("hg", [P, 8])
        cw = sb("cw", [P, 4, 37])
        for dst, src in ((gains, "gains"), (hg, "head_gains"), (cw, "conv_taps")):
            AC.dma(lambda e, dst=dst, src=src: e.dma_start(dst[:], I[src]), c_in)
        rel = sb("rel", [33, NH])
        t = DV.op(lambda e: e.memset(rel[:, :], 1.0))
        k_in = AC.dma(lambda e: e.dma_start(rel[0:32, :], I["rel_bias_2"]), c_in, t)
        btab = sb("btab", [P, NT, NCMP, NH])
        k_tab = AC.dma(lambda e: e.dma_start(arena[0:33, 0:768 + NCMP * S], I["bias_tables"]), c_in)

        for q in (PE, DV, AC, PL):
            q.wait(k_tab)

        def bias_rows():
            tvs = arena[0:NH, 12032:12800].rearrange("p (a b) -> p a b", a=2)
            for a in range(2):
                t = PE.op(lambda e, a=a: e.matmul(ps[a][0:NH, 0:384], rel[:, :], arena[0:33, 384 * a:384 * a + 384], start=True, stop=True))
                k = DV.op(lambda e, a=a: e.tensor_copy(tvs[:, a, :], ps[a][0:NH, 0:384]), t)
            PL.dma(lambda e: e.dma_start(tv.rearrange("a h c -> h a c"), tvs), c_tv, k)
            for tt in range(NT):
                for c in range(NCMP):
                    at = 768 + c * S + tt * P
                    fn = lambda e, tt=tt, c=c, at=at: e.matmul(ps[2][:, (tt * NCMP + c) * NH:(tt * NCMP + c) * NH + NH],
                                                               arena[0:33, at:at + P], rel[:, :], start=True, stop=True)
                    t = PE.op(fn)
            DV.op(lambda e: e.tensor_copy(btab[:, :, :, :].rearrange("p a b c -> p (a b c)"), ps[2][:, 0:NT * NCMP * NH]), t)

        zeros = arena[:, 11500:12012]
        t = PL.op(lambda e: e.memset(zeros, 0.0))
        rest = ys[YR:, :].rearrange("r (h c) -> (r h) c", c=512)
        for r in range(0, 2 * (SLOTS + WIN), P):
            PL.dma(lambda e, r=r: e.dma_start(rest[r:r + P, :], zeros), c_tv, t)
        bias_rows()
        k_tv = (c_tv.sem, c_tv.n)

        def conv_mixer():
            A = stage()
            gp = A.take(4, 286)
            ap_ = A.take(4, 258)
            ac, ab, gc, sg, sq = A.take(4, S), A.take(4, S), A.take(4, S), A.take(4, S), A.take(4, S)
            ya, yb = sg, sq
            yh, yl = A.take_r(8, S), A.take_r(8, S)
            mean, var = A.take(S), A.take(S)
            kx = transposed(X, [k_x])
            z = [DV.op(lambda e: e.memset(gp[:, :, 0:30], 0.0)), DV.op(lambda e: e.memset(ap_[:, :, 0:2], 0.0))]

            kg = []
            for j in range(2):
                tv_ = by_channels(2, (4, 5), kx)
                tg = by_channels(2, (6, 7), kx)
                for h in range(2):
                    i = 2 * j + h
                    t = AC.op(lambda e, i=i, h=h: e.activation(sg[:, i, :], ps[6 + h][:, 0:S], ACT.Sigmoid), tg[h])
                    free[6 + h] = [t]
                    t = DV.op(lambda e, i=i, h=h: e.tensor_tensor(gp[:, i, 30:286], ps[4 + h][:, 0:S], sg[:, i, :], ALU.mult), t, tv_[h])
                    free[4 + h] = [t]
                    kg.append(t)

            def conv_b(i, Q):
                t = Q.op(lambda e: e.tensor_scalar(gc[:, i, :], gp[:, i, 0:S], cw[:, i, 0:1], cw[:, i, 34:35], ALU.mult, ALU.add), kg[i], z)
                yield t
                for k in range(1, 31):
                    t = Q.op(lambda e, k=k: e.scalar_tensor_tensor(gc[:, i, :], gp[:, i, k:k + S], cw[:, i, k:k + 1], gc[:, i, :],
                                                                   ALU.mult, ALU.add), t)
                    yield t

            taps = zip(*(conv_b(i, DV) for i in range(4)))

            def some_taps(n):
                for _, four in zip(range(n), taps):
                    ends[:] = list(four)

            ends = [None] * 4
            kc_, kb_, ka = [], [], []
            some_taps(5)
            for j in range(2):
                t = by_channels(2, (2 * j, 2 * j + 1), kx)
                for h in range(2):
                    i = 2 * j + h
                    k = AC.op(lambda e, i=i: e.activation(ac[:, i, :], ps[i][:, 0:S], ACT.Copy), t[h])
                    free[i] = [k]
                    kc_.append(k)
                some_taps(5)
            for j in range(2):
                t = by_channels(2, (4 + 2 * j, 5 + 2 * j), kx)
                for h in range(2):
                    i = 2 * j + h
                    k = DV.op(lambda e, i=i: e.tensor_tensor(ap_[:, i, 2:258], ps[4 + i][:, 0:S], ac[:, i, :], ALU.mult), t[h], kc_[i])
                    free[4 + i] = [k]
                    ka.append(k)
                some_taps(5)
            for j in range(2):
                t = by_channels(2, (2 * j, 2 * j + 1), kx)
                for h in range(2):
                    i = 2 * j + h
                    k = AC.op(lambda e, i=i: e.activation(ab[:, i, :], ps[i][:, 0:S], ACT.Copy), t[h])
                    free[i] = [k]
                    kb_.append(k)
                some_taps(5)
            some_taps(31)
            t = ka
            for tap in range(3):
                t2 = []
                for i in range(4):
                    if tap == 0:
                        t2.append(DV.op(lambda e, i=i: e.tensor_scalar(ya[:, i, :], ap_[:, i, 0:S], cw[:, i, 31:32], None, ALU.mult), ka[i], z))
                    else:
                        t2.append(DV.op(lambda e, i=i, tap=tap: e.scalar_tensor_tensor(
                            ya[:, i, :], ap_[:, i, tap:tap + S], cw[:, i, 31 + tap:32 + tap], ya[:, i, :], ALU.mult, ALU.add), t[i]))
                t = t2
            ky = DV.op(lambda e: e.tensor_tensor(ya, ya, ab, ALU.mult), t, kb_)
            ky = part(ya, yh[:, 0:4, :], yl[:, 0:4, :], ky)

            def sums(src, toks, bank):
                PE.wait(toks, free[bank])
                for i in range(4):
                    fn = lambda e, i=i: e.matmul(ps[bank][:, 0:S], ones, src[:, i, :], start=(i == 0), stop=(i == 3))
                    if i < 3:
                        PE.quiet(fn)
                    else:
                        return PE.op(fn)

            t = sums(gc, ends, 4)
            t = DV.op(lambda e: e.tensor_scalar(mean, ps[4][:, 0:S], 1.0 / 512, None, ALU.mult), t)
            t = DV.op(lambda e: e.tensor_tensor(gc, gc, mean.unsqueeze(1).to_broadcast([P, 4, S]), ALU.subtract), t)
            kd = t
            t = AC.op(lambda e: e.activation(sq, gc, ACT.Square), t)
            t = sums(sq, [t], 5)
            t = DV.op(lambda e: e.tensor_scalar(var, ps[5][:, 0:S], 1.0 / 512, LN_EPS, ALU.mult, ALU.add), t)
            t = AC.op(lambda e: e.activation(var, var, ACT.Sqrt), t)
            t = DV.op(lambda e: e.reciprocal(var, var), t)
            t = DV.op(lambda e: e.tensor_tensor(gc, gc, var.unsqueeze(1).to_broadcast([P, 4, S]), ALU.mult), t, kd)
            ks = [AC.op(lambda e, i=i: e.activation(yb[:, i, :], gc[:, i, :], ACT.Silu, scale=cw[:, i, 35:36], bias=cw[:, i, 36:37]), t)
                  for i in range(4)]
            free[4], free[5] = [kd], [t]
            ks = part(yb, yh[:, 4:8, :], yl[:, 4:8, :], ks)
            k = by_tokens(lambda c: (yh[:, c, :], yl[:, c, :]), 8, [0, 1, 2, 3], [ky, ks], 8)
            DV.wait(k_tv)
            return residual([0, 1, 2, 3], k, ALPHA, R)

        def moe(layer, toks):
            A = stage()
            kx = transposed(X, toks)
            rw = A.take(DC, 36)
            rb = A.take(36)
            XsT = A.take(DC, SLOTS + WIN)
            Yg = XsT.rearrange("p c s -> p (c s)")[:, 0:2 * NT * D].rearrange("p (a b) -> p a b", b=D)
            xh, xl = A.take_r(NT, D), A.take_r(NT, D)
            Pm = A.take_r(NT, SLOTS)
            r_ = lambda at, *shape: shaped(arena_r[:, at:at + int(np.prod(shape))], shape)
            xe = [r_(1024 * i, DC, P) for i in range(2)]
            hT = [r_(2048 + 512 * i, 4, P) for i in range(2)]
            usb = [A.take(2 * F_E) for _ in range(2)]
            sil = [A.take(4, WIN) for _ in range(2)]
            hh = [A.take(4, WIN) for _ in range(2)]
            low = [A.take(512) for _ in range(2)]
            ysb = [A.take(D) for _ in range(2)]
            wov = A.take(D)
            kxh = AC.op(lambda e: e.activation(xh, X[:, :, :], ACT.Copy), toks)
            kxl = PL.op(lambda e: e.tensor_tensor(xl, X[:, :, :], xh.bitcast(F32), ALU.subtract), kxh)
            PL.dma(lambda e: e.dma_start(rw, I["router_w"][layer].rearrange("(c p) n -> p c n", p=P)), c_rw)
            k_rw = PL.dma(lambda e: e.dma_start(rb, I["router_b"][layer].partition_broadcast(P)), c_rw)
            kz = DV.op(lambda e: e.memset(XsT[:, :, SLOTS:SLOTS + WIN], 0.0))

            lp = ps[4][:, 0:72].rearrange("p (a b) -> p a b", b=36)
            for tt in range(NT):
                for c in range(DC):
                    for x in (XL, XH):
                        fn = lambda e, tt=tt, c=c, x=x: e.matmul(lp[:, tt, :], x[:, c, tt * P:tt * P + P].bitcast(F32), rw[:, c, :],
                                                                 start=(c == 0 and x is XL), stop=(c == DC - 1 and x is XH))
                        if tt == 1 and c == DC - 1 and x is XH:
                            t = PE.op(fn, kx, k_rw)
                        else:
                            PE.quiet(fn, kx, k_rw)
            lg = S_(NT, 36)
            bc = lambda v, *s: v.to_broadcast([P, *s])
            k_lg = t = DV.op(lambda e: e.tensor_tensor(lg, lp, bc(rb.unsqueeze(1), NT, 36), ALU.add), t, k_rw)

            def V(fn, *toks):
                return DV.op(fn, *toks)

            gm, gd, ge, gs = S_(NT), S_(NT, NG), S_(NT, NG), S_(NT)
            goh, gt, gi = S_(NT, NG), S_(NT, NG), S_(NT)
            gl = lg[:, :, 0:NG]
            t = V(lambda e: e.tensor_reduce(gm, gl, AX.X, ALU.max), t)
            t = kgd = V(lambda e: e.tensor_tensor(gd, gl, bc(gm.unsqueeze(2), NT, NG), ALU.subtract), t)
            ka = AC.op(lambda e: e.activation(ge, gd, ACT.Exp), t)
            t = V(lambda e: e.tensor_tensor(gt, gl, bc(gm.unsqueeze(2), NT, NG), ALU.is_equal), t)
            t = V(lambda e: e.tensor_tensor(gt, gt, bc(C("io4m").unsqueeze(1), NT, NG), ALU.mult), t)
            t = V(lambda e: e.tensor_reduce(gi, gt, AX.X, ALU.min), t)
            t = V(lambda e: e.tensor_tensor(goh, bc(C("io4m").unsqueeze(1), NT, NG), bc(gi.unsqueeze(2), NT, NG), ALU.is_equal), t)
            mneg, ml = S_(NT, NG), S_(NT, NE)
            ml4 = ml.rearrange("p t (g e) -> p t g e", g=NG)
            el4 = lg[:, :, NG:36].rearrange("p t (g e) -> p t g e", g=NG)
            t1 = V(lambda e: e.tensor_scalar(mneg, goh, -1.0, BIG, ALU.add, ALU.mult), t)
            t = V(lambda e: e.tensor_tensor(ml4, el4, bc(goh.unsqueeze(3), NT, NG, 8), ALU.mult), t)
            t = V(lambda e: e.tensor_tensor(ml4, ml4, bc(mneg.unsqueeze(3), NT, NG, 8), ALU.add), t, t1)
            oh = [S_(NT, NE) for _ in range(2)]
            mx = [S_(NT) for _ in range(2)]
            ix = [S_(NT) for _ in range(2)]
            eq = S_(NT, NE)
            io = bc(C("io32m").unsqueeze(1), NT, NE)
            for k in range(2):
                t = V(lambda e, k=k: e.tensor_reduce(mx[k], ml, AX.X, ALU.max), t)
                t = V(lambda e, k=k: e.tensor_tensor(eq, ml, bc(mx[k].unsqueeze(2), NT, NE), ALU.is_equal), t)
                t = V(lambda e, k=k: e.tensor_tensor(eq, eq, io, ALU.mult), t)
                t = V(lambda e, k=k: e.tensor_reduce(ix[k], eq, AX.X, ALU.min), t)
                t = V(lambda e, k=k: e.tensor_tensor(oh[k], io, bc(ix[k].unsqueeze(2), NT, NE), ALU.is_equal), t)
                if k == 0:
                    t = V(lambda e: e.scalar_tensor_tensor(ml, oh[0], -BIG, ml, ALU.mult, ALU.add), t)
            M = S_(NT, NE)
            t = kM = V(lambda e: e.tensor_tensor(M, oh[0], oh[1], ALU.add), t)
            before = C("before")
            rk, sz, szT = ps[5][:, 0:64], ps[5][:, 64:96], ps[6][0:NE, 0:P]
            PE.quiet(lambda e: e.matmul(rk[:, 0:NE], before, M[:, 0, :], start=True, stop=True), kM)
            PE.quiet(lambda e: e.matmul(rk[:, NE:64], ones, M[:, 0, :], start=True, stop=False))
            PE.quiet(lambda e: e.matmul(rk[:, NE:64], before, M[:, 1, :], start=False, stop=True))
            for tt in range(NT):
                PE.quiet(lambda e, tt=tt: e.matmul(sz, ones, M[:, tt, :], start=(tt == 0), stop=(tt == 1)))
            for tt in range(NT):
                fn = lambda e, tt=tt: e.matmul(szT, M[:, tt, :], ones, start=(tt == 0), stop=(tt == 1))
                if tt:
                    kr = PE.op(fn)
                else:
                    PE.quiet(fn)
            w2, wt = S_(NT), S_(2, NT)
            t = V(lambda e: e.tensor_tensor(w2, mx[1], mx[0], ALU.subtract), t)
            ka2 = AC.op(lambda e: e.activation(w2, w2, ACT.Exp), t)
            t = V(lambda e: e.tensor_reduce(gs, ge, AX.X, ALU.add), ka)
            t2 = V(lambda e: e.tensor_scalar(wt[:, 0, :], w2, 1.0, None, ALU.add), ka2)
            t = V(lambda e: e.tensor_tensor(gs, gs, wt[:, 0, :], ALU.mult), t, t2)
            t = V(lambda e: e.reciprocal(wt[:, 0, :], gs), t)
            k_wt = V(lambda e: e.tensor_tensor(wt[:, 1, :], wt[:, 0, :], w2, ALU.mult), t)
            szs, exT, st, cx, size, ext = S_(P), S_(P), S_(NE), S_(NE), S_(NE), S_(NE)
            szs, exT = szs[0:NE, :], exT[0:NE, :]
            t = ksz = V(lambda e: e.tensor_copy(szs, szT), kr)

            def windows(o, i, toks):
                t = V(lambda e: e.tensor_scalar(o, i, float(WIN), None, ALU.is_gt), toks)
                for j in range(2, S // WIN):
                    t = V(lambda e, j=j: e.scalar_tensor_tensor(o, i, float(WIN * j), o, ALU.is_gt, ALU.add), t)
                return t

            t = windows(exT, szs, t)
            PE.quiet(lambda e: e.matmul(ps[6][:, 128:160], szs, before[0:NE, 0:NE], start=True, stop=True), ksz)
            kp = PE.op(lambda e: e.matmul(ps[6][:, 160:192], exT, before[0:NE, 0:NE], start=True, stop=True), t)
            t0 = V(lambda e: e.tensor_copy(size, sz))
            k_st = V(lambda e: e.tensor_copy(st, ps[6][:, 128:160]), kp)
            k_cx = V(lambda e: e.tensor_copy(cx, ps[6][:, 160:192]))
            k_ext = windows(ext, size, t0)
            rank, pos, pk, rr, far = S_(NT, NE), S_(NT, NE), S_(2, NT), S_(2, NT), S_(2, NT)
            t = V(lambda e: e.tensor_copy(rank, rk.rearrange("p (t e) -> p t e", t=NT)))
            tp = V(lambda e: e.tensor_tensor(pos, rank, bc(st.unsqueeze(1), NT, NE), ALU.add), t, k_st)
            tq = []
            for k in range(2):
                a = V(lambda e, k=k: e.tensor_tensor(eq, oh[k], pos, ALU.mult), tp, tq[-1:])
                b = V(lambda e, k=k: e.tensor_reduce(pk[:, k, :], eq, AX.X, ALU.add), a)
                a = V(lambda e, k=k: e.tensor_tensor(eq, oh[k], rank, ALU.mult), b)
                tq.append(V(lambda e, k=k: e.tensor_reduce(rr[:, k, :], eq, AX.X, ALU.add), a))
            k_pm = []
            for tt in range(NT):
                a = V(lambda e, tt=tt: e.tensor_scalar(Pm[:, tt, :], C("slot"), pk[:, 0, tt:tt + 1], None, ALU.is_equal), tq)
                k_pm.append(V(lambda e, tt=tt: e.scalar_tensor_tensor(Pm[:, tt, :], C("slot"), pk[:, 1, tt:tt + 1], Pm[:, tt, :].bitcast(F32),
                                                                      ALU.is_equal, ALU.add), a))
            k_xs = []
            for c in range(DC):
                b = c % 4
                PE.wait(free[b], k_pm, kxh, kxl)
                for i, (x, tt) in enumerate(((xl, 0), (xl, 1), (xh, 0), (xh, 1))):
                    fn = lambda e, b=b, c=c, x=x, tt=tt, i=i: e.matmul(ps[b][:, :], x[:, tt, c * P:c * P + P], Pm[:, tt, :], start=(i == 0), stop=(i == 3))
                    if i < 3:
                        PE.quiet(fn)
                    else:
                        t = PE.op(fn)
                if c % 2:
                    k = AC.op(lambda e, b=b, c=c: e.activation(XsT[:, c, 0:SLOTS], ps[b][:, :], ACT.Copy), t)
                else:
                    k = DV.op(lambda e, b=b, c=c: e.tensor_copy(XsT[:, c, 0:SLOTS], ps[b][:, :]), t)
                free[b] = [k]
                k_xs.append(k)
            t = V(lambda e: e.tensor_copy(oi[:, 0:NE], st[0:1, :]), k_st)
            k_oi = t
            er = S_(2, NT)
            for k in range(2):
                a = V(lambda e, k=k: e.tensor_scalar(er[:, k, :], ix[k], 64.0, float(WIN), ALU.add, ALU.mult))
                tq.append(a)
            a = V(lambda e: e.tensor_tensor(er, er, rr, ALU.add), tq)
            b = V(lambda e: e.tensor_scalar(far, rr, float(WIN), None, ALU.is_ge), tq)
            c_ = V(lambda e: e.tensor_tensor(pk, pk, er, ALU.subtract), a, k_pm)
            c_ = V(lambda e: e.tensor_scalar(pk, pk, float(YR), None, ALU.add), c_)
            c_ = V(lambda e: e.tensor_tensor(pk, pk, far, ALU.mult), c_, b)
            c_ = V(lambda e: e.tensor_tensor(er, er, pk, ALU.add), c_)
            k_yi = V(lambda e: e.tensor_copy(yi[:, :].rearrange("p (a b) -> p a b", b=NT), er), c_)
            o1, o2, o3 = A.take(NOV, NE), A.take(NOV, NE), A.take(NOV, NE)
            o1, o2, o3 = o1[0:1, :, :], o2[0:1, :, :], o3[0:1, :, :]
            ofl = S_(2 * NOV + 1)[0:1, :]
            b1 = lambda v: v.to_broadcast([1, NOV, NE])
            a = V(lambda e: e.tensor_tensor(o1, b1(C("io7", 1).unsqueeze(2)), b1(cx[0:1, :].unsqueeze(1)), ALU.subtract), k_cx)
            b = V(lambda e: e.tensor_tensor(o2, o1, b1(ext[0:1, :].unsqueeze(1)), ALU.is_lt), a, k_ext)
            a = V(lambda e: e.scalar_tensor_tensor(o2, o1, 0.0, o2, ALU.is_ge, ALU.mult), b)
            b = V(lambda e: e.scalar_tensor_tensor(o1, o1, float(WIN), b1(st[0:1, :].unsqueeze(1)), ALU.mult, ALU.add), a)
            b = V(lambda e: e.tensor_scalar(o1, o1, float(WIN - SLOTS), None, ALU.add), b)
            b = V(lambda e: e.tensor_tensor(o1, o1, o2, ALU.mult), b)
            b = V(lambda e: e.tensor_reduce(ofl[:, 0:NOV], o1, AX.X, ALU.add), b)
            b = V(lambda e: e.tensor_scalar(ofl[:, 0:NOV], ofl[:, 0:NOV], float(SLOTS), None, ALU.add), b)
            a = V(lambda e: e.tensor_tensor(o3, o2, b1(C("io32", 1).unsqueeze(1)), ALU.mult), a)
            a = V(lambda e: e.tensor_reduce(ofl[:, NOV:2 * NOV], o3, AX.X, ALU.add), a)
            c_ = V(lambda e: e.tensor_reduce(ofl[:, 2 * NOV:2 * NOV + 1], ext[0:1, :], AX.X, ALU.add), k_ext)
            k_ofl = V(lambda e: e.tensor_copy(oi[:, NE:NE + 2 * NOV + 1], ofl), a, b, c_, k_oi)
            k_al = [AC.op(lambda e, tt=tt: e.activation(R[:, tt, :], X[:, tt, :], ACT.Copy, scale=float(ALPHA))) for tt in range(NT)]

            U = [[0, 1], [2, 3]]
            TB, YB = 4, [5, 6]
            PE.wait(k_st, k_cx)
            up_done = {}
            y_done = [None, None]
            xe_done = {}

            def gather(e_):
                ap = oi[0:1, e_:e_ + 1]
                PL.wait(k_oi, k_xs, kz, up_done.get(e_ - 2))
                hi, lo = xe[e_ % 2][:, :, 0:WIN], xe[e_ % 2][:, :, WIN:P]

                def fn(e):
                    r = e.value_load(ap, min_val=0, max_val=SLOTS)
                    return e.tensor_copy(hi, XsT[:, :, bass.ds(r, WIN)])

                def fn2(e):
                    r = e.value_load(ap, min_val=0, max_val=SLOTS)
                    return e.tensor_tensor(lo, XsT[:, :, bass.ds(r, WIN)], hi.bitcast(F32), ALU.subtract)
                t = PL.op(fn)
                xe_done[e_] = PL.op(fn2, t)

            def up(e_, chunks):
                u = U[e_ % 2]
                PE.wait(xe_done[e_])
                for c in chunks:
                    wh, wl, tok, k = next_piece()
                    PE.wait(tok)
                    if c == 0:
                        PE.wait(free[u[0]], free[u[1]])
                    for w, last in ((wl, False), (wh, True)):
                        for h in range(2):
                            fn = lambda e, c=c, h=h, w=w, last=last: e.matmul(ps[u[h]][:, :], xe[e_ % 2][:, c, :], w[:, h * 512:h * 512 + 512],
                                                                              start=(c == 0 and not last), stop=(c == DC - 1 and last))
                            if last and h:
                                piece_free[k] = up_done[e_] = PE.op(fn)
                            else:
                                PE.quiet(fn)

            def up_out(e_):
                for h in range(2):
                    u = U[e_ % 2][h]
                    t = usb_done[e_] = AC.op(lambda e, u=u, h=h: e.activation(usb[e_ % 2][:, h * F_E:h * F_E + F_E], ps[u][:, :], ACT.Copy), up_done[e_], turned.get(e_ - 2))
                    free[u] = [t]

            usb_done, turned, split_done, sil_done, down_done = {}, {}, {}, {}, {}

            def turn(e_):
                i = e_ % 2
                tb = ps[TB].rearrange("p (m c n) -> p m c n", m=2, c=4)
                PE.wait(usb_done[e_], free[TB])
                for m in range(2):
                    for f in range(4):
                        at = m * F_E + f * P
                        fn = lambda e, m=m, f=f, at=at: e.matmul(tb[:, m, f, :], usb[i][:, at:at + P], C("fold"), start=True, stop=True)
                        if m and f == 3:
                            turned[e_] = PE.op(fn)
                        else:
                            PE.quiet(fn)
                t = AC.op(lambda e: e.activation(sil[i], tb[:, 0, :, :], ACT.Silu), turned[e_], sil_done.get(e_ - 2))
                t = sil_done[e_] = DV.op(lambda e: e.tensor_tensor(hh[i], sil[i], tb[:, 1, :, :], ALU.mult), t, split_done.get(e_ - 2))
                free[TB] = [t]
                split_done[e_] = part(hh[i], hT[i][:, :, 0:WIN], hT[i][:, :, WIN:P], [t, down_done.get(e_ - 2)])

            def down(e_):
                i = e_ % 2
                PE.wait(split_done[e_])
                for f in range(4):
                    wh, wl, tok, k = next_piece()
                    PE.wait(tok)
                    if f == 0:
                        PE.wait(free[YB[0]], free[YB[1]])
                    for w, last in ((wl, False), (wh, True)):
                        for h in range(2):
                            fn = lambda e, f=f, h=h, w=w, last=last: e.matmul(ps[YB[h]][:, :], hT[i][:, f, :], w[:, h * 512:h * 512 + 512],
                                                                              start=(f == 0 and not last), stop=(f == 3 and last))
                            if last and h:
                                piece_free[k] = t = PE.op(fn)
                            else:
                                PE.quiet(fn)
                down_done[e_] = t
                ks = []
                for h in range(2):
                    k = AC.op(lambda e, h=h: e.activation(low[h][0:WIN, :], ps[YB[h]][WIN:P, :], ACT.Copy), t, low_free[h])
                    k = low_free[h] = DV.op(lambda e, h=h: e.tensor_tensor(ysb[i][0:WIN, h * 512:h * 512 + 512], low[h][0:WIN, :], ps[YB[h]][0:WIN, :], ALU.add), k, y_done[i])
                    free[YB[h]] = [k]
                    ks.append(k)
                y_done[i] = PL.dma(lambda e: e.dma_start(ys[e_ * WIN:e_ * WIN + WIN, :], ysb[i][0:WIN, :]), c_y[i], ks)

            low_free = [None, None]
            free[TB] = [k_lg]
            free[5] = free[6] = [k_st, k_cx, tp]
            gather(0)
            for e_ in range(NE + 1):
                if e_ + 1 < NE:
                    gather(e_ + 1)
                if e_ < NE:
                    up(e_, range(0, 4))
                if e_ >= 1:
                    turn(e_ - 1)
                if e_ < NE:
                    up(e_, range(4, 8))
                    up_out(e_)
                if e_ >= 1:
                    down(e_ - 1)

            ov = c_ov[layer]
            n_ap = oi[0:1, NE + 2 * NOV:NE + 2 * NOV + 1]
            some = lambda e: e.value_load(n_ap, min_val=0, max_val=NOV) > 0
            for q in (PE, AC, DV, PL):
                q.wait(k_ofl)
            bp, ba, bv, bg = (q.branch(some) for q in (PE, AC, DV, PL))
            bs = Queue(None)
            xo, so = usb[0][:, 0:512].rearrange("p (c n) -> p c n", c=DC), usb[0][:, 512:1024]
            ho, to, yo = usb[1][:, 0:512], usb[1][:, 512:768].rearrange("p (c n) -> p c n", c=4), ysb[0]
            first = [q.last() for q in (PE, AC, DV, PL)] + [t for t in y_done]
            for q in (bp, ba, bv, bg, bs):
                q.wait(first, k_ofl)
            t_y = t_dn = None
            t_pe = None
            for k in range(NOV):
                sap, eap = oi[0:1, NE + k:NE + k + 1], oi[0:1, NE + NOV + k:NE + NOV + k + 1]

                def pick(e, sap=sap):
                    r = e.value_load(sap, min_val=0, max_val=SLOTS)
                    return e.tensor_copy(xo, XsT[:, :, bass.ds(r, WIN)])
                tx = bg.bump(pick, ov["pool"], t_pe)

                def piece(c, t_free):
                    def fn(e, c=c, eap=eap):
                        r = e.value_load(eap, min_val=0, max_val=NE - 1)
                        w = I["expert_w_up"][layer] if c < DC else I["expert_w_down"][layer]
                        r0 = (c if c < DC else c - DC) * P
                        src = w[bass.ds(r, 1), r0:r0 + P, :].rearrange("o p n -> p (o n)")
                        return e.dma_start(wov, src)
                    return bs.dma(fn, ov["dma"], t_free)

                for c in range(DC):
                    td = piece(c, t_pe)
                    for h in range(2):
                        fn = lambda e, c=c, h=h: e.matmul(ps[h][0:WIN, :], xo[:, c, :], wov[:, h * 512:h * 512 + 512], start=(c == 0), stop=(c == DC - 1))
                        t_pe = bp.bump(fn, ov["pe"], td, tx)
                ta = ba.bump(lambda e: e.activation(so[0:WIN, :], ps[0][0:WIN, :], ACT.Silu), ov["act"], t_pe)
                tm = bv.bump(lambda e: e.tensor_tensor(ho[0:WIN, :], so[0:WIN, :], ps[1][0:WIN, :], ALU.mult), ov["dve"], ta)
                tb = ps[TB][:, 0:256].rearrange("p (c n) -> p c n", c=4)
                for f in range(4):
                    tt_ = bp.bump(lambda e, f=f: e.transpose(tb[:, f, :], ho[0:WIN, f * P:f * P + P], ident[0:WIN, 0:WIN]), ov["pe"], tm)
                tc = bv.bump(lambda e: e.tensor_copy(to, tb), ov["dve"], tt_)
                for f in range(4):
                    td = piece(DC + f, t_pe)
                    for h in range(2):
                        fn = lambda e, f=f, h=h: e.matmul(ps[YB[h]][0:WIN, :], to[:, f, :], wov[:, h * 512:h * 512 + 512], start=(f == 0), stop=(f == 3))
                        t_pe = bp.bump(fn, ov["pe"], td, tc)
                for h in range(2):
                    te = ba.bump(lambda e, h=h: e.activation(yo[0:WIN, h * 512:h * 512 + 512], ps[YB[h]][0:WIN, :], ACT.Copy), ov["act"], t_pe, t_y)

                def put(e, sap=sap):
                    r = e.value_load(sap, min_val=0, max_val=SLOTS)
                    return e.dma_start(ys[bass.ds(r + YR, WIN), :], yo[0:WIN, :])
                t_y = ba.dma(put, ov["y"], te)
                bp.wait(te)
            for q in (bp, ba, bv, bg):
                q.wait(t_y)
            sp_branch[layer] = (k_ofl, some, bs)

            for j in range(2 * NT):
                k_yg = PL.dma(lambda e, j=j: e.indirect_dma_start(
                    Yg[:, j, :], None, ys, bass.IndirectOffsetOnAxis(ap=yi[:, j:j + 1], axis=0)), c_yg,
                    k_yi, y_done, PE.last(), DV.last(), AC.last())
            r = []
            for tt in range(NT):
                t = DV.op(lambda e, tt=tt: e.scalar_tensor_tensor(R[:, tt, :], Yg[:, tt, :], wt[:, 0, tt:tt + 1], R[:, tt, :], ALU.mult, ALU.add),
                          k_yg, k_wt, k_al)
                r.append(DV.op(lambda e, tt=tt: e.scalar_tensor_tensor(R[:, tt, :], Yg[:, NT + tt, :], wt[:, 1, tt:tt + 1], R[:, tt, :],
                                                                       ALU.mult, ALU.add), t))
            return r

        sp_branch = {}

        def stick(toks):
            A = stage()
            kx = transposed(X, toks)
            qT, kT, oh, ol = A.take(8, S), A.take(8, S), A.take_r(8, S), A.take_r(8, S)
            zb = [A.take(2, 384) for _ in range(2)]
            tb = [A.take(2, 384) for _ in range(2)]
            V = R
            k_q = {}
            for j in range(8):
                b = (4 + 2 * (j % 2), 5 + 2 * (j % 2))
                ts = by_channels(2, b, kx)
                for h in range(2):
                    i = 2 * (j % 4) + h
                    o = ps[b[h]][:, 0:S]
                    if j < 4:
                        k = AC.op(lambda e, i=i, o=o: e.activation(qT[:, i, :], o, ACT.Copy, scale=float(HD ** -0.5)), ts[h])
                    else:
                        k = DV.op(lambda e, i=i, o=o: e.tensor_copy(kT[:, i, :], o), ts[h])
                    free[b[h]] = [k]
                    k_q[j // 4, i] = k
            k = by_tokens(lambda c: (XH[:, c, :], XL[:, c, :]), 8, [0, 1, 2, 3], [], 8)
            k = dict(zip(range(4), k))
            kv = []
            for tt in range(NT):
                for h in range(2):
                    b = 2 * tt + h
                    o = V[:, tt, h * 512:h * 512 + 512]
                    if h:
                        t = AC.op(lambda e, b=b, o=o: e.activation(o, ps[b][:, :], ACT.Copy), k[b])
                    else:
                        t = DV.op(lambda e, b=b, o=o: e.tensor_copy(o, ps[b][:, :]), k[b])
                    free[b] = [t]
                    kv.append(t)
            strict, suffix = C("strict"), C("suffix")
            zk, o_free, done_a, ko = {}, {}, {}, []

            def score(p):
                u = p % 2
                for h in range(2):
                    b, r = 2 * u + h, slice(HD * h, HD * h + HD)
                    PE.wait(free[b], k_q[0, p], k_q[1, p])
                    PE.quiet(lambda e, b=b, r=r: e.matmul(ps[b][:, 0:S], kT[r, p, 0:P], qT[r, p, :], start=True, stop=True))
                    t = PE.op(lambda e, b=b, r=r: e.matmul(ps[b][:, S:384], kT[r, p, P:S], qT[r, p, P:S], start=True, stop=True))
                    k = DV.op(lambda e, b=b, u=u, h=h: e.tensor_tensor(zb[u][:, h, :], ps[b][:, 0:384], strict, ALU.add), t, done_a.get(p - 2))
                    free[b] = [k]
                t = AC.op(lambda e: e.activation(tb[u], zb[u], ACT.Abs), k, zk.get(("inc", p - 2)))
                t = AC.op(lambda e: e.activation(tb[u], tb[u], ACT.Exp, scale=-1.0), t)
                t = AC.op(lambda e: e.activation(tb[u], tb[u], ACT.Ln, bias=1.0), t)
                zk[p] = DV.op(lambda e: e.scalar_tensor_tensor(tb[u], zb[u], 0.0, tb[u], ALU.max, ALU.add), t)

            def attend(p):
                u = p % 2
                for h in range(2):
                    b = 4 + h
                    PE.wait(zk[p], free[b])
                    PE.quiet(lambda e, b=b, h=h: e.matmul(ps[b][:, 0:384], suffix, tb[u][:, h, :], start=True, stop=False))
                    t = PE.op(lambda e, b=b, h=h: e.matmul(ps[b][:, P:S], ones, tb[u][:, h, S:384], start=False, stop=True))
                    k = DV.op(lambda e, b=b, h=h: e.tensor_tensor(zb[u][:, h, :], zb[u][:, h, :], ps[b][:, 0:384], ALU.subtract), t)
                    free[b] = [k]
                zk["inc", p] = t
                ta = AC.op(lambda e: e.activation(zb[u], zb[u], ACT.Exp), k)
                b = 6 + p % 2
                PE.wait(ta, kv, free[b])
                for h in range(2):
                    hh = 2 * p + h
                    r = slice(HD * h, HD * h + HD)
                    PE.quiet(lambda e, h=h, r=r, hh=hh, b=b: e.matmul(ps[b][r, 0:S], V[:, 0, hh * HD:hh * HD + HD], zb[u][:, h, 0:S], start=True, stop=False))
                    t = PE.op(lambda e, h=h, r=r, hh=hh, b=b: e.matmul(ps[b][r, P:S], V[:, 1, hh * HD:hh * HD + HD], zb[u][:, h, S:384], start=False, stop=True))
                done_a[p] = t
                k = part(ps[b][:, 0:S], oh[:, p, :], ol[:, p, :], t)
                free[b] = [k]
                ko.append(k)

            for p in range(9):
                if p < 8:
                    score(p)
                if p >= 1:
                    attend(p - 1)
            k = by_tokens(lambda c: (oh[:, c, :], ol[:, c, :]), 8, [0, 1, 2, 3], ko, 8)
            DV.wait(t)
            return residual([0, 1, 2, 3], k, ALPHA, R)

        def head_norm(width, gain, scale, dst, banks, tbanks, work, toks):
            nh = width // HD
            ss, res = S_(NT, nh), []
            if scale != 1.0:
                g2 = S_(1)
                kg = DV.op(lambda e: e.tensor_scalar(g2, gain, float(scale), None, ALU.mult))
            else:
                g2, kg = gain, None
            for tt in range(NT):
                b = banks[tt]
                t = toks[tt]
                wk = work[tt]
                k = AC.op(lambda e, b=b, wk=wk: e.activation(wk[:, 0:width], ps[b][:, 0:width], ACT.Square), t, wfree.get(id(wk)))
                k = DV.op(lambda e, tt=tt, wk=wk: e.tensor_reduce(ss[:, tt, :], wk[:, 0:width].rearrange("p (h d) -> p h d", d=HD), AX.X, ALU.add), k)
                k = DV.op(lambda e, tt=tt: e.tensor_scalar(ss[:, tt, :], ss[:, tt, :], 1.0 / HD, RMS_EPS, ALU.mult, ALU.add), k)
                k = AC.op(lambda e, tt=tt: e.activation(ss[:, tt, :], ss[:, tt, :], ACT.Sqrt), k)
                k = DV.op(lambda e, tt=tt: e.reciprocal(ss[:, tt, :], ss[:, tt, :]), k)
                k = DV.op(lambda e, tt=tt, b=b, wk=wk: e.tensor_tensor(
                    wk[:, 0:width].rearrange("p (h d) -> p h d", d=HD), ps[b][:, 0:width].rearrange("p (h d) -> p h d", d=HD),
                    ss[:, tt, :].unsqueeze(2).to_broadcast([P, nh, HD]), ALU.mult), k)
                free[b] = [k]
                tb_ = tbanks[tt]
                for i in range(width // P):
                    fn = lambda e, i=i, tb_=tb_, wk=wk: e.transpose(ps[tb_][:, i * P:i * P + P], wk[:, i * P:i * P + P], ident)
                    t2 = PE.op(fn, k, free[tb_])
                wfree[id(wk)] = t2
                m = width // P
                o = dst[:, :, tt * P:tt * P + P]
                i_ = ps[tb_][:, 0:width].rearrange("p (i t) -> p i t", t=P)
                k = AC.op(lambda e, o=o, i_=i_: e.activation(o, i_, ACT.Copy, scale=g2), t2, kg)
                free[tb_] = [k]
                res.append(k)
            return res

        wfree = {}

        def copied(width, dst, banks, toks):
            res = []
            for tt in range(NT):
                b, o = banks[tt], dst(tt)
                k = DV.op(lambda e, b=b, o=o: e.tensor_copy(o, ps[b][:, 0:width]), toks[tt])
                free[b] = [k]
                res.append(k)
            return res

        def bias_loader(bias, db, heads, which):
            used = {}
            tok = {}

            def fetch(p):
                a, kind = heads(p), which(p)
                b = bias[p % 3]
                base = (kind * NH + a) * 384
                PL.wait(used.get(p - 3))
                for lo, n in ((0, P), (P, S)):
                    src = bass.AP(tv.tensor, base, [[1, P], [db * 384, 2], [1, n]])
                    tok[p] = PL.dma(lambda e, b=b, lo=lo, n=n, src=src: e.dma_start(b[:, :, lo:lo + n], src), c_bias[p % 3])
            return fetch, tok, used

        def soft_scores(qT, kT, p, kp, h, bank, bias_h, k_bias, toks, scr, stats, scr_free, gate=None):
            r = slice(HD * h, HD * h + HD)
            sbuf, mx, sm = scr, stats[0], stats[1]
            b = bank
            PE.quiet(lambda e: e.matmul(ps[b][:, S:384], qT[r, p, 0:P], kT[r, kp, 0:P], start=True, stop=True), free[b], toks)
            t = PE.op(lambda e: e.matmul(ps[b][:, 0:S], qT[r, p, P:S], kT[r, kp, :], start=True, stop=True))
            k = DV.op(lambda e: e.tensor_tensor(sbuf, ps[b][:, 0:384], bias_h[:, ::-1], ALU.add), t, k_bias, scr_free)
            free[b] = [k]
            used = k
            k1 = DV.op(lambda e: e.tensor_reduce(mx[:, 1:2], sbuf[:, 0:S], AX.X, ALU.max, negate=True), k)
            k0 = DV.op(lambda e: e.tensor_reduce(mx[:, 0:1], sbuf[:, S:384], AX.X, ALU.max, negate=True), k)
            a1 = AC.op(lambda e: e.activation(sbuf[:, 0:S], sbuf[:, 0:S], ACT.Exp, bias=mx[:, 1:2], accum_out=sm[:, 1:2]), k1)
            a0 = AC.op(lambda e: e.activation(sbuf[:, S:384], sbuf[:, S:384], ACT.Exp, bias=mx[:, 0:1], accum_out=sm[:, 0:1]), k0)
            k = DV.op(lambda e: e.reciprocal(sm, sm), a1, a0)
            if gate is not None:
                k = DV.op(lambda e: e.tensor_tensor(sm, sm, gate, ALU.mult), k)
            k1 = DV.op(lambda e: e.tensor_scalar(sbuf[:, 0:S], sbuf[:, 0:S], sm[:, 1:2], None, ALU.mult), k)
            k0 = DV.op(lambda e: e.tensor_scalar(sbuf[:, S:384], sbuf[:, S:384], sm[:, 0:1], None, ALU.mult), k)
            return used, [k1, k0]

        def soft_turn(sbuf, toks, bank, pT, pT_free):
            b = bank
            PE.wait(toks, free[b])
            PE.quiet(lambda e: e.transpose(ps[b][:, 0:P], sbuf[:, S:384], ident))
            PE.quiet(lambda e: e.transpose(ps[b][:, P:S], sbuf[:, 0:P], ident))
            t = PE.op(lambda e: e.transpose(ps[b][:, S:384], sbuf[:, P:S], ident))
            k = AC.op(lambda e: e.activation(pT, ps[b][:, 0:384], ACT.Copy), t, pT_free)
            free[b] = [k]
            return t, k

        def out_and_residual(oh, ol, toks):
            k = by_tokens(lambda c: (oh[:, c, :], ol[:, c, :]), 8, [0, 1, 2, 3], toks, 8)
            return residual([0, 1, 2, 3], k, 1.0, X)

        def mixer_ab(toks):
            A = stage()
            kr = rms_to(toks)
            kx = transposed(R, kr, gains[:, 0, :])
            qT, kT, oh, ol = A.take(8, S), A.take(8, S), A.take_r(8, S), A.take_r(8, S)
            V = R
            work = [A.take(512) for _ in range(2)]
            bias = [A.take(2, 384) for _ in range(3)]
            scr = [A.take(384) for _ in range(4)]
            pT = [A.take(384) for _ in range(4)]
            stats = [(S_(2), S_(2)) for _ in range(4)]
            fetch, k_bias, b_used = bias_loader(bias, 1, lambda p: 2 * p, lambda p: 0 if p < 4 else 1)
            for p in range(3):
                fetch(p)
            kq, kk, kv = {}, {}, {}
            for a in range(2):
                t, = by_token_cols([(0, 512, (4, 5))], kx)
                kq[a] = head_norm(512, hg[:, 2 * a:2 * a + 1], HD ** -0.5, qT[:, 4 * a:4 * a + 4, :], (4, 5), (6, 7), work, t)
                t, = by_token_cols([(0, 512, (0, 1))], kx)
                kk[a] = head_norm(512, hg[:, 2 * a + 1:2 * a + 2], 1.0, kT[:, 4 * a:4 * a + 4, :], (0, 1), (6, 7), work, t)
                t, = by_token_cols([(0, 512, (2, 3))], kx)
                kv[a] = copied(512, lambda tt, a=a: V[:, tt, 512 * a:512 * a + 512], (2, 3), t)
            ko = []
            pend = {}
            scr_free, pT_free, o_k = {}, {}, {}

            def first(h):
                p = h // 2
                used, k = soft_scores(qT, kT, p, p, h % 2, h % 4, bias[p % 3][:, h % 2, :], k_bias[p], kq[p // 4] + kk[p // 4],
                                      scr[h % 4], stats[h % 4], scr_free.get(h - 4))
                if h % 2:
                    b_used[p] = used
                    if p + 3 < 8:
                        fetch(p + 3)
                pend[h] = k

            def second(h):
                p = h // 2
                scr_free[h], k = soft_turn(scr[h % 4], pend[h], 4 + h % 2, pT[h % 4], pT_free.get(h - 4))
                b = 6 + p % 2
                r = slice(HD * (h % 2), HD * (h % 2) + HD)
                PE.wait(k, kv[p // 4], free[b] if h % 2 == 0 else None)
                PE.quiet(lambda e: e.matmul(ps[b][r, 0:S], V[:, 0, h * HD:h * HD + HD], pT[h % 4][:, 0:S], start=True, stop=False))
                t = PE.op(lambda e: e.matmul(ps[b][r, P:S], V[:, 1, h * HD:h * HD + HD], pT[h % 4][:, S:384], start=False, stop=True))
                pT_free[h] = t
                if h % 2:
                    k = part(ps[b][:, 0:S], oh[:, p, :], ol[:, p, :], t)
                    free[b] = [k]
                    ko.append(k)

            for h in range(NH + 2):
                if h < NH:
                    first(h)
                if h >= 2:
                    second(h - 2)
            return out_and_residual(oh, ol, ko)

        def mixer_nsa(toks):
            A = stage()
            kr = rms_to(toks)
            kx = transposed(R, kr, gains[:, 3, :])
            qT, oh, ol = A.take(8, S), A.take_r(8, S), A.take_r(8, S)
            kvc, ksT, kwT = A.take(4, S), A.take(2, S), A.take(2, S)
            Vs, Vw = A.take(NT, S), A.take(NT, S)
            bias = [A.take(2, 384) for _ in range(3)]
            work = [A.take(768) for _ in range(2)]
            scr = [work[i // 2][:, 384 * (i % 2):384 * (i % 2) + 384] for i in range(4)]
            pT = [A.take(384) for _ in range(4)]
            gw = A.take(DC, 48)
            cmp_ = A.take(227)
            w2, posT, cb = cmp_[:, 0:192], cmp_[:, 192:224], S_(8)
            b2b = A.take(HD)
            hidk, hidv = A.take(60), A.take(60)
            hidr = A.take(4, P)
            kcT = A.take(60)
            sq60, rs60 = A.take(60), A.take(60)
            vcr = A.take(4, HD)
            pc = GB[:, 0, :].rearrange("p (a b) -> p a b", b=32)
            cs = A.take(NT * NH, NCMP)
            pcT = GB[:, 1, :].rearrange("p (a b) -> p a b", b=S)
            gt = S_(NT, 48)
            stats = [(S_(2), S_(2)) for _ in range(4)]
            fetch, k_bias, b_used = bias_loader(bias, 4, lambda i: (i // 4) * 8 + i % 4, lambda i: 0)
            for p in range(3):
                fetch(p)
            PL.dma(lambda e: e.dma_start(gw, I["w_in_nsa_2"][0][:, 2560:2608].rearrange("(c p) n -> p c n", p=P)), c_sm)
            PL.dma(lambda e: e.dma_start(cmp_, I["cmp_small"]), c_sm)
            k_sm = PL.dma(lambda e: e.dma_start(b2b, I["cmp_v_b2_2"][0].partition_broadcast(P)), c_sm)

            kq = []
            for a in range(2):
                b = (4, 5) if a == 0 else (0, 1)
                t, = by_token_cols([(0, 512, b)], kx)
                kq.append(head_norm(512, hg[:, 4:5], HD ** -0.5, qT[:, 4 * a:4 * a + 4, :], b, (6, 7), work, t))
            k_kvc = []
            for j in range(2):
                ts = by_channels(2, (2, 3), kx)
                for h in range(2):
                    i = 2 * j + h
                    k = DV.op(lambda e, i=i, h=h: e.tensor_copy(kvc[:, i, :], ps[2 + h][:, 0:S]), ts[h])
                    free[2 + h] = [k]
                    k_kvc.append(k)
            t, tv_ = by_token_cols([(0, 256, (4, 5)), (256, 256, (0, 1))], kx)
            ks = head_norm(256, hg[:, 6:7], 1.0, ksT, (4, 5), (6, 7), work, t)
            kvs = copied(256, lambda tt: Vs[:, tt, :], (0, 1), tv_)
            t, tv_ = by_token_cols([(0, 256, (2, 3)), (256, 256, (0, 1))], kx)
            kw = head_norm(256, hg[:, 7:8], 1.0, kwT, (2, 3), (6, 7), work, t)
            kvw = copied(256, lambda tt: Vw[:, tt, :], (0, 1), tv_)
            k_cb = DV.op(lambda e: e.tensor_copy(cb[:, 0:3], cmp_[:, 224:227]), k_sm)
            gp_ = ps[2][:, 0:96].rearrange("p (t n) -> p t n", t=NT)
            for tt in range(NT):
                for c in range(DC):
                    for x in (XL, XH):
                        t = PE.op(lambda e, tt=tt, c=c, x=x: e.matmul(gp_[:, tt, :], x[:, c, tt * P:tt * P + P].bitcast(F32), gw[:, c, :],
                                                                      start=(c == 0 and x is XL), stop=(c == DC - 1 and x is XH)), free[2], k_sm)
            k_gt = AC.op(lambda e: e.activation(gt, gp_, ACT.Sigmoid), t)
            free[2] = [k_gt]
            hid_k = []
            for j in range(2):
                first_ = raw_slots(2)
                hb, bb = (((3, 4), 2), ((1, 5), 0))[j]
                bp_ = ps[bb][:, 128:129]
                r = slice(HD * j, HD * j + HD)
                w1 = lambda l, r, first_=first_: ring[r, first_[l // 16] % NRING, l % 16 * P:l % 16 * P + P]
                for l in range(32):
                    t = PE.op(lambda e, l=l, r=r, w1=w1, bp_=bp_: e.matmul(bp_, w1(l, r), posT[r, l:l + 1], start=(l == 0), stop=(l == 31)),
                              arrived(first_[l // 16]), free[bb], k_sm)
                kb = DV.op(lambda e, j=j, bp_=bp_: e.tensor_tensor(cb[:, 4 + j:5 + j], bp_, cb[:, j:j + 1], ALU.add), t, k_cb)
                hid, hk = (hidk, hidv)[j], []
                for par in range(2):
                    r, b = slice(HD * par, HD * par + HD), hb[par]
                    for l in range(32):
                        rhs = kvc[r, 2 * j:2 * j + 2, l:l + 225:16]
                        o = ps[b][:, 0:30].rearrange("p (a b) -> p a b", a=2)
                        fn = lambda e, l=l, r=r, w1=w1, rhs=rhs, o=o: e.matmul(o, w1(l, r), rhs, start=(l == 0), stop=(l == 31))
                        if l == 31:
                            t = PE.op(fn)
                        else:
                            PE.quiet(fn, k_kvc, free[b])
                    hk.append(AC.op(lambda e, j=j, b=b, hid=hid, par=par: e.activation(
                        hid[:, 30 * par:30 * par + 30], ps[b][:, 0:30], ACT.Gelu_apprx_tanh, bias=cb[:, 4 + j:5 + j]), t, kb))
                    free[b] = [hk[-1]]
                for n in first_:
                    loads[n]["released"] = t
                hid_k.append(hk)
                free[bb] = [kb]
            t = PE.op(lambda e: e.matmul(ps[0][:, 0:60], w2[:, 0:P], hidk, start=True, stop=True), hid_k[0], free[0], k_sm)
            t = kraw = AC.op(lambda e: e.activation(kcT, ps[0][:, 0:60], ACT.Identity, bias=cb[:, 2:3]), t)
            t = AC.op(lambda e: e.activation(sq60, kcT, ACT.Square), t)
            t = PE.op(lambda e: e.matmul(ps[0][:, 64:124], C("halves"), sq60, start=True, stop=True), t)
            t = DV.op(lambda e: e.tensor_scalar(rs60, ps[0][:, 64:124], 1.0 / HD, RMS_EPS, ALU.mult, ALU.add), t)
            t = AC.op(lambda e: e.activation(rs60, rs60, ACT.Sqrt), t)
            t = DV.op(lambda e: e.reciprocal(rs60, rs60), t)
            k_kc = DV.op(lambda e: e.scalar_tensor_tensor(kcT, kcT, hg[:, 5:6], rs60, ALU.mult, ALU.mult), t, kraw)
            free[0] = [t]
            t0 = DV.op(lambda e: e.memset(hidr, 0.0))
            h4 = hidr.rearrange("p g (i c) -> p g i c", i=4)[:, :, :, 0:NCMP]
            t = DV.op(lambda e: e.tensor_copy(h4, hidv.rearrange("p (g c) -> p g c", c=NCMP).unsqueeze(2).to_broadcast([P, 4, 4, NCMP])), t0, hid_k[1])
            vp = ps[1][:, 0:256].rearrange("p (g d) -> p g d", d=HD)
            for g in range(4):
                t2 = PE.op(lambda e, g=g: e.matmul(vp[:, g, :], hidr[:, g, :], w2[:, 128:192], start=True, stop=True), t, free[1])
            k_vc = DV.op(lambda e: e.tensor_tensor(vcr, vp, b2b.unsqueeze(1).to_broadcast([P, 4, HD]), ALU.add), t2, k_sm)
            free[1] = [k_vc]
            cp = [ps[2 + par][:, 0:NT * NH * NCMP].rearrange("p (a c) -> p a c", c=NCMP) for par in range(2)]
            for tt in range(NT):
                for h in range(NH):
                    g = h // 4
                    par, i, gi = g % 2, (g // 2) * 4 + h % 4, (g % 2) * 2 + g // 2
                    r = slice(HD * par, HD * par + HD)
                    t = PE.op(lambda e, tt=tt, h=h, par=par, r=r, i=i, gi=gi: e.matmul(
                        cp[par][:, tt * NH + h, :], qT[r, i, tt * P:tt * P + P], kcT[r, gi * NCMP:gi * NCMP + NCMP], start=True, stop=True),
                        free[2], free[3], k_kc, kq)
            cm, cl = S_(NT * NH), S_(NT * NH)
            b3 = lambda v: v.unsqueeze(2).to_broadcast([P, NT * NH, NCMP])
            k = []
            by_par = lambda v, tt, par: v[:, tt * NH:tt * NH + NH, :].rearrange("p (a b j) c -> p a b j c", b=2, j=4)[:, :, par, :, :]
            for tt in range(NT):
                for par in range(2):
                    bt = btab[:, tt, :, :].rearrange("p c (a b j) -> p a b j c", b=2, j=4)[:, :, par, :, :]
                    k.append(DV.op(lambda e, tt=tt, par=par, bt=bt: e.tensor_tensor(by_par(cs, tt, par), by_par(cp[par], tt, par), bt, ALU.add), t))
            free[2] = free[3] = k
            t = DV.op(lambda e: e.tensor_reduce(cm, cs, AX.X, ALU.max), k)
            t = DV.op(lambda e: e.tensor_scalar(cm, cm, NEG / 10, None, ALU.max), t)
            t = DV.op(lambda e: e.tensor_tensor(cs, cs, b3(cm), ALU.subtract), t)
            t = AC.op(lambda e: e.activation(cs, cs, ACT.Exp), t)
            t = DV.op(lambda e: e.tensor_reduce(cl, cs, AX.X, ALU.add), t)
            t = DV.op(lambda e: e.tensor_scalar(cl, cl, 1e-30, None, ALU.max), t)
            t = DV.op(lambda e: e.reciprocal(cl, cl), t)
            g3 = gt.rearrange("p t (h b) -> p t h b", b=3)
            t = DV.op(lambda e: e.tensor_tensor(cl.rearrange("p (t h) -> p t h", t=NT), cl.rearrange("p (t h) -> p t h", t=NT), g3[:, :, :, 0], ALU.mult), t, k_gt)
            t0 = DV.op(lambda e: e.memset(pc, 0.0))
            kpc = DV.op(lambda e: e.tensor_tensor(pc[:, :, 0:NCMP], cs, b3(cl), ALU.mult), t, t0)
            k_pc = []
            for g in range(4):
                b = g % 2
                for tt in range(NT):
                    i_ = pc[:, tt * NH + 4 * g:tt * NH + 4 * g + 4, :].rearrange("p a b -> p (a b)")
                    t = PE.op(lambda e, b=b, tt=tt, i_=i_: e.transpose(ps[b][:, tt * P:tt * P + P], i_, ident), kpc, free[b])
                k = DV.op(lambda e, b=b, g=g: e.tensor_copy(pcT[:, g, :], ps[b][:, 0:S]), t)
                free[b] = [k]
                k_pc.append(k)

            ko, pend = [], {}
            scr_free, pT_free = {}, {}
            jobs = [(i, par, br) for i in range(8) for par in range(2) for br in range(2)]

            def first(n):
                i, par, br = jobs[n]
                h = (i // 4) * 8 + par * 4 + i % 4
                kt, ktok = ((ksT, ks), (kwT, kw))[br]
                used, k = soft_scores(qT, kt, i, i // 4, par, n % 4, bias[i % 3][:, par, :], k_bias[i], kq[i // 4] + ktok,
                                      scr[n % 4], stats[n % 4], scr_free.get(n - 4), g3[:, :, h, 1 + br])
                if par and br:
                    b_used[i] = used
                    if i + 3 < 8:
                        fetch(i + 3)
                pend[n] = k

            def second(n):
                i, par, br = jobs[n]
                g = (i // 4) * 2 + par
                scr_free[n], k = soft_turn(scr[n % 4], pend[n], 4 + n % 2, pT[n % 4], pT_free.get(n - 4))
                b = 6 + i % 2
                r = slice(HD * par, HD * par + HD)
                vv, vt = ((Vs, kvs), (Vw, kvw))[br]
                PE.wait(vt, free[b] if par == 0 and br == 0 else None)
                if br == 0:
                    hi = i % 4
                    gi = par * 2 + i // 4
                    q = slice(32 * hi, 32 * hi + 32)
                    PE.quiet(lambda e: e.matmul(ps[b][r, 0:S], vcr[q, gi, :], pcT[q, g, :], start=True, stop=False), k_pc, k_vc)
                PE.quiet(lambda e: e.matmul(ps[b][r, 0:S], vv[:, 0, g * HD:g * HD + HD], pT[n % 4][:, 0:S], start=False, stop=False), k)
                t = PE.op(lambda e: e.matmul(ps[b][r, P:S], vv[:, 1, g * HD:g * HD + HD], pT[n % 4][:, S:384], start=False, stop=(br == 1)))
                pT_free[n] = t
                if par and br:
                    k = part(ps[b][:, 0:S], oh[:, i, :], ol[:, i, :], t)
                    free[b] = [k]
                    ko.append(k)

            for n in range(len(jobs) + 2):
                if n < len(jobs):
                    first(n)
                if n >= 2:
                    second(n - 2)
            return out_and_residual(oh, ol, ko)

        def swiglu(layer, toks):
            A = stage()
            kr = rms_to(toks)
            kx = transposed(R, kr, gains[:, 3 * layer + 1, :])
            hh, hl = [A.take_r(2, S) for _ in range(2)], [A.take_r(2, S) for _ in range(2)]
            sil = [A.take(2, S) for _ in range(2)]
            prod = [A.take(2, S) for _ in range(2)]
            kh, ka, used = {}, {}, [None, None]
            for j in range(FC // 2 + 1):
                i = j % 2
                if j < FC // 2:
                    tg = by_channels(2, (4, 5), kx)
                    tu = by_channels(2, (6, 7), kx)
                    a = []
                    for h in range(2):
                        a.append(AC.op(lambda e, i=i, h=h: e.activation(sil[i][:, h, :], ps[4 + h][:, 0:S], ACT.Silu), tg[h], ka.get(j - 2)))
                        free[4 + h] = [a[h]]
                    for h in range(2):
                        k = DV.op(lambda e, i=i, h=h: e.tensor_tensor(prod[i][:, h, :], sil[i][:, h, :], ps[6 + h][:, 0:S], ALU.mult), a[h], tu[h], kh.get(j - 2))
                        free[6 + h] = [k]
                    ka[j] = k
                if j >= 1:
                    o = 1 - i
                    k = by_tokens(lambda c: (hh[o][:, c % 2, :], hl[o][:, c % 2, :]), 2, [0, 1, 2, 3], kh[j - 1], FC, 2 * (j - 1))
                    used[o] = PE.last()
                if j < FC // 2:
                    kh[j] = part(prod[i], hh[i], hl[i], [ka[j], used[i]])
            return residual([0, 1, 2, 3], k, 1.0, X)

        def ple(layer, toks):
            A = stage()
            kr = rms_to(toks)
            kx = transposed(R, kr, gains[:, 3 * layer + 2, :])
            G = A.take(NT, D)
            pf, ph, pl_ = A.take(2, S), A.take_r(2, S), A.take_r(2, S)
            kp = PL.dma(lambda e: e.dma_start(pf, I["p_2"][layer].rearrange("(c p) n -> p c n", p=P)), c_sm)
            kp = part(pf, ph, pl_, kp)
            k = by_tokens(lambda c: (XH[:, c, :], XL[:, c, :]), 8, [4, 5, 6, 7], kx, 8)
            ka = []
            for tt in range(NT):
                for h in range(2):
                    b = 4 + 2 * tt + h
                    ka.append(AC.op(lambda e, tt=tt, h=h, b=b: e.activation(G[:, tt, h * 512:h * 512 + 512], ps[b][:, :], ACT.Sigmoid), k[2 * tt + h]))
                    free[b] = [ka[-1]]
            k = by_tokens(lambda c: (ph[:, c, :], pl_[:, c, :]), 2, [0, 1, 2, 3], [kp], 2)
            r = []
            for tt in range(NT):
                for h in range(2):
                    b = 2 * tt + h
                    sl = slice(h * 512, h * 512 + 512)
                    t = DV.op(lambda e, tt=tt, b=b, sl=sl: e.tensor_tensor(G[:, tt, sl], G[:, tt, sl], ps[b][:, :], ALU.mult), ka[b], k[b])
                    free[b] = [t]
                    r.append(DV.op(lambda e, tt=tt, sl=sl: e.tensor_tensor(X[:, tt, sl], X[:, tt, sl], G[:, tt, sl], ALU.add), t))
            return r

        gb = load_ln(I["ln_mix_g"][0], I["ln_mix_b"][0])
        t = conv_mixer()
        t = layer_norm(t, gb)
        gb = load_ln(I["ln_ffn_g"][0], I["ln_ffn_b"][0])
        t = moe(0, t)
        t = layer_norm(t, gb)
        gb = load_ln(I["ln_mix_g"][1], I["ln_mix_b"][1])
        t = stick(t)
        t = layer_norm(t, gb)
        gb = load_ln(I["ln_ffn_g"][1], I["ln_ffn_b"][1])
        t = moe(1, t)
        t = layer_norm(t, gb)
        for layer in range(DEPTH):
            t = mixer_ab(t) if layer == 0 else mixer_nsa(t)
            t = swiglu(layer, t)
            t = ple(layer, t)
        assert taken[0] == len(pieces) and next_raw[0] == len(raw)

        for n, l in enumerate(loads):
            for layer in range(DEPTH):
                if n == moe_end[layer]:
                    put_branch(SP, sp_branch[layer])
            i = n % NRING
            if n >= NRING:
                SP.wait(loads[n - NRING]["released"])
            for view, src in l["parts"]:
                view = view(ring[:, i, :])
                SP.items.append(("inc", lambda e, view=view, src=src: e.dma_start(view, src), c_ring[i].sem, 16))
        SP.dma(lambda e: e.dma_start(out[0].rearrange("(t p) d -> p t d", p=P), X[:, :, :]), c_out, t)
        SP.wait((c_out.sem, 16))

        block = ctx.enter_context(nc.Block())
        block.sync(lambda e: SP.play(e))
        block.scalar(lambda e: AC.play(e))
        block.vector(lambda e: DV.play(e))
        block.gpsimd(lambda e: PL.play(e))
        block.tensor(lambda e: PE.play(e))


def put_branch(q, what):
    ready, cond, body = what
    q.wait(ready)
    q.items.append(("if", cond, body))


_PLAIN = ["x", "even_w_in", "even_w_out", "odd_w_qkv", "odd_w_o", "ln_mix_g", "ln_mix_b", "ln_ffn_g", "ln_ffn_b",
          "expert_w_up", "expert_w_down", "rel_bias_2",
          "w_ffn_gate_2", "w_ffn_up_2", "w_ffn_down_2", "w_ple_proj_2", "w_ple_gate_2", "w_in_ab_2", "w_out_ab_2",
          "cmp_k_w1_2", "cmp_v_w1_2", "cmp_v_b2_2"]
_HEAD_GAINS = ["qn_moba_2", "kn_moba_2", "qn_dil_2", "kn_dil_2", "qn_nsa_2", "kn_cmp_2", "kn_slc_2", "kn_win_2"]


def kernel(**inputs):
    import numpy as _np
    import concourse.bacc as _bacc
    from concourse import mybir as _mybir
    from concourse.bass_utils import run_bass_kernel_spmd as _run

    a = {n: _np.ascontiguousarray(inputs[n]) for n in _PLAIN}
    asis = {n: _np.asarray(inputs[n]) for n in inputs}
    chan = lambda v: _np.asarray(v).reshape(-1, 128).T
    twice = lambda v: _np.concatenate([v, v], axis=0)
    a["conv_taps"] = _np.ascontiguousarray(_np.concatenate(
        [asis["even_conv_b_w"][0].reshape(31, 4, 128).transpose(2, 1, 0), asis["even_conv_a"][0].reshape(3, 4, 128).transpose(2, 1, 0)]
        + [chan(asis[n][0])[:, :, None] for n in ("even_conv_b_bias", "even_norm_b_g", "even_norm_b_b")], axis=2))
    a["gains"] = _np.ascontiguousarray(_np.stack(
        [chan(asis[n][i]) for i in range(2) for n in ("norm_mix_2", "norm_ffn_2", "norm_ple_2")], axis=1))
    a["head_gains"] = _np.ascontiguousarray(_np.stack([twice(asis[n][0]) for n in _HEAD_GAINS], axis=1))
    a["cmp_small"] = _np.ascontiguousarray(_np.concatenate(
        [asis["cmp_k_w2_2"][0], asis["cmp_k_w2_2"][0], asis["cmp_v_w2_2"][0],
         _np.concatenate([asis["cmp_k_pos_2"][0].T, asis["cmp_v_pos_2"][0].T], axis=0),
         asis["cmp_k_b1_2"][0][:, None], asis["cmp_v_b1_2"][0][:, None], twice(asis["cmp_k_b2_2"][0])[:, None]], axis=1))
    a["router_w"] = _np.concatenate([asis["router_group_w"], asis["router_expert_w"]], axis=2)
    a["router_b"] = _np.concatenate([asis["router_group_b"], asis["router_expert_b"]], axis=1)
    a["p_2"] = _np.ascontiguousarray(asis["p_2"][:, 0].transpose(0, 2, 1))
    w = asis["w_in_nsa_2"]
    q = w[:, :, :1024].reshape(1, 1024, 2, 2, 4, 64).transpose(0, 1, 2, 4, 3, 5).reshape(1, 1024, 1024)
    a["w_in_nsa_2"] = _np.concatenate([q, w[:, :, 1024:]], axis=2)
    a["w_out_nsa_2"] = _np.ascontiguousarray(
        asis["w_out_nsa_2"].reshape(1, 2, 2, 4, 64, 1024).transpose(0, 1, 3, 2, 4, 5).reshape(1, 1024, 1024))
    a["consts"] = CONSTS
    a["bias_tables"] = BIAS_TABLES

    nc = _bacc.Bacc("TRN2", target_bir_lowering=False, num_devices=1)
    arrays, aps = {}, {}
    for n, v in a.items():
        arrays[f"in_{n}"] = v
        aps[n] = nc.dram_tensor(f"in_{n}", v.shape, _mybir.dt.from_np(v.dtype), kind="ExternalInput").ap()
    out = nc.dram_tensor("out_0", (1, 256, 1024), _mybir.dt.float32, kind="ExternalOutput").ap()
    bass_two_blocks_kernel(nc, aps, out)
    r = _run(nc, [arrays], core_ids=[0])
    return r.results[0]["out_0"]
```

```python
from contextlib import ExitStack

import numpy as np

import concourse.bass as bass
from concourse import mybir

F32 = mybir.dt.float32
I32 = mybir.dt.int32
U32 = mybir.dt.uint32
F32R = mybir.dt.float32r
ALU = mybir.AluOpType
ACT = mybir.ActivationFunctionType
AX = mybir.AxisListType

P = 128
S = 256
D = 1024
DC = D // P
NT = S // P
DEPTH = 2
NE = 32
NG = 4
F_E = 512
NH = 16
HD = 64
FFN = 2816
FC = FFN // P
NCMP = 15
ALPHA = (2 * DEPTH) ** 0.25
LN_EPS = 1e-5
RMS_EPS = 1e-6
NEG = -1e30
BIG = 3e38

WIN = 32
W2 = 2 * WIN
NOV = S * 2 // WIN - 1
SLOTS = 2 * S
YR = NE * WIN
NRING = 6
RW = 2048
NB = 4
PC = 1024

CONST_COLS = {}


def host_constants():
    p = np.arange(P)[:, None]
    j = np.arange(P)[None, :]
    parts = [
        ("ident", p == j),
        ("ones", np.ones((P, P))),
        ("before", p < j),
        ("suffix", p >= j),
        ("halves", (p // HD) == (j // HD)),
        ("fold36", (p % 36) == np.arange(36)[None, :]),
        ("fold48", (p % 48) == np.arange(48)[None, :]),
        ("fold", (p % WIN) == np.arange(WIN)[None, :]),
        ("strict", np.concatenate([np.where(p < j, 0.0, NEG), np.zeros((P, P)), np.where(p < j, 0.0, NEG)], 1)),
        ("slot", np.broadcast_to(np.arange(SLOTS), (P, SLOTS))),
        ("io32m", np.broadcast_to(np.arange(NE) - 64, (P, NE))),
        ("io32", np.broadcast_to(np.arange(NE), (P, NE))),
        ("io4m", np.broadcast_to(np.arange(NG) - 64, (P, NG))),
        ("windows", np.broadcast_to(np.arange(NOV), (P, NOV))),
    ]
    at = 0
    for name, a in parts:
        CONST_COLS[name] = (at, at + a.shape[1])
        at += a.shape[1]
    return np.concatenate([np.asarray(a, np.float32) for _, a in parts], 1)


def bucket_of(n):
    n = max(int(n), 0)
    if n < 16:
        return n
    return min(16 + int(np.log(np.float32(n / 16)) / np.log(2048 / 16) * 16), 31)


def host_bias_tables():
    W = 384
    a = np.zeros((33, 2, W), np.float32)
    for col in range(W - 1):
        d = col - 127
        if d < 0:
            a[32, :, col] = NEG
            continue
        a[bucket_of(d), :, col] = 1.0
        count = (d <= 128) + (d % 4 == 0) + (d % 16 == 0)
        a[32, 1, col] = np.log(count) if count else NEG
    c = np.zeros((33, NCMP, S), np.float32)
    for k in range(NCMP):
        for t in range(S):
            d = t - (16 * k + 31)
            if d >= 0:
                c[bucket_of(d), k, t] = 1.0
            else:
                c[32, k, t] = NEG
    return np.concatenate([a.reshape(33, -1), c.reshape(33, -1)], 1)


CONSTS = host_constants()
BIAS_TABLES = host_bias_tables()


class Queue:

    def __init__(self, sem):
        self.sem, self.n, self.items, self.seen = sem, 0, [], {}

    def wait(self, *toks):
        for t in toks:
            if t is None:
                continue
            if isinstance(t, list):
                self.wait(*t)
                continue
            sem, v = t
            if self.seen.get(sem.name, 0) < v:
                self.seen[sem.name] = v
                self.items.append(("wait", sem, v))

    def op(self, fn, *toks):
        self.wait(*toks)
        self.n += 1
        self.items.append(("inc", fn, self.sem, 1))
        return self.sem, self.n

    def quiet(self, fn, *toks):
        self.wait(*toks)
        self.items.append(("plain", fn))

    def dma(self, fn, counter, *toks):
        self.wait(*toks)
        self.items.append(("inc", fn, counter.sem, 16))
        return counter.next(16)

    def last(self):
        return (self.sem, self.n) if self.n else None

    def branch(self, cond):
        q = Queue(None)
        q.seen = dict(self.seen)
        self.items.append(("if", cond, q))
        return q

    def bump(self, fn, counter, *toks):
        self.wait(*toks)
        self.items.append(("inc", fn, counter.sem, 1))
        return counter.next(1)

    def play(self, e):
        for it in self.items:
            if it[0] == "wait":
                e.wait_ge(it[1], it[2])
            elif it[0] == "inc":
                it[1](e).then_inc(it[2], it[3])
            elif it[0] == "plain":
                it[1](e)
            else:
                with e.If(it[1](e)):
                    it[2].play(e)


class Counter:
    def __init__(self, sem):
        self.sem, self.n = sem, 0

    def next(self, by):
        self.n += by
        return self.sem, self.n


def bass_two_blocks_kernel(nc, I, out):
    ctx = ExitStack()
    with ctx:
        def sb(name, shape, dt=F32):
            return ctx.enter_context(nc.sbuf_tensor(name, shape, dt))

        def sem(name):
            return ctx.enter_context(nc.semaphore(name))

        CW = CONSTS.shape[1]
        cst = sb("cst", [P, CW])
        X = sb("X", [P, NT, D])
        XHL = sb("XHL", [P, 2, DC, S], F32R)
        XH, XL = XHL[:, 0, :, :], XHL[:, 1, :, :]
        R = sb("R", [P, NT, D])
        GB = sb("GB", [P, 2, D])
        ring = sb("ring", [P, NRING, RW])
        whi = sb("whi", [P, NB, PC], F32R)
        wlo = sb("wlo", [P, NB, PC], F32R)
        AW = 12480
        arena = sb("arena", [P, AW])
        ARW = 5120
        arena_r = sb("arena_r", [P, ARW], F32R)
        small = sb("small", [P, 1100])
        oi = sb("oi", [1, 64], I32)
        yi = sb("yi", [P, 2 * NT], U32)
        ps = [ctx.enter_context(nc.psum_tensor(f"ps{i}", [P, 512], F32)) for i in range(8)]

        ys = nc.dram_tensor("ys", [YR + SLOTS + WIN, D], F32, kind="Internal").ap()
        tv = nc.dram_tensor("tv", [2, NH, 384], F32, kind="Internal").ap()

        PE, DV, AC, PL = (Queue(sem(n)) for n in ("s_pe", "s_dve", "s_act", "s_pool"))
        SP = Queue(sem("s_sp"))
        c_in = Counter(sem("s_in"))
        c_ring = [Counter(sem(f"s_ring{i}")) for i in range(NRING)]
        c_gb = Counter(sem("s_gb"))
        c_rw = Counter(sem("s_rw"))
        c_yl = Counter(sem("s_yl"))
        c_y = [Counter(sem(f"s_y{i}")) for i in range(2)]
        c_yg = [Counter(sem(f"s_yg{i}")) for i in range(NT)]
        c_tv = Counter(sem("s_tv"))
        c_bias = [Counter(sem(f"s_bias{i}")) for i in range(3)]
        c_sm = Counter(sem("s_sm"))
        c_out = Counter(sem("s_out"))
        c_ov = [{n: Counter(sem(f"s_ov_{n}{l}")) for n in ("dma", "pe", "act", "dve", "pool", "y")} for l in range(DEPTH)]

        def C(name, rows=P):
            a, b = CONST_COLS[name]
            return cst[0:rows, a:b]

        ident, ones = C("ident"), C("ones")

        def shaped(v, shape):
            if len(shape) == 2:
                return v.rearrange("p (a b) -> p a b", b=shape[1])
            if len(shape) == 3:
                return v.rearrange("p (a b c) -> p a b c", b=shape[1], c=shape[2])
            return v

        class Area:

            def __init__(self):
                self.at = self.at_r = 0

            def take(self, *shape):
                v = arena[:, self.at:self.at + int(np.prod(shape))]
                self.at += int(np.prod(shape))
                assert self.at <= AW, self.at
                return shaped(v, shape)

            def take_r(self, *shape):
                v = arena_r[:, self.at_r:self.at_r + int(np.prod(shape))]
                self.at_r += int(np.prod(shape))
                assert self.at_r <= ARW, self.at_r
                return shaped(v, shape)

        sm_at = [0]

        def S_(*shape):
            n = int(np.prod(shape))
            v = small[:, sm_at[0]:sm_at[0] + n]
            sm_at[0] += n
            assert sm_at[0] <= 1100
            return shaped(v, shape)

        def stage():
            toks = [q.last() for q in (PE, DV, AC, PL)]
            for q in (PE, DV, AC, PL):
                q.wait(toks)
            for i in range(8):
                free[i] = None
            sm_at[0] = 0
            return Area()

        free = [None] * 8

        loads = []

        pieces = []

        def load(*parts, split=True):
            n = len(loads)
            loads.append({"parts": parts, "released": None, "arrived": [c_ring[n % NRING].next(16) for _ in parts][-1]})
            if split:
                pieces.extend((n, h) for h in range(RW // PC))
            else:
                raw.append(n)

        taken, prepared, next_raw = [0], [0], [0]
        piece_free = {}

        def arrived(n):
            return loads[n]["arrived"]

        def prepare(k):
            n, h = pieces[k]
            src = ring[:, n % NRING, h * PC:h * PC + PC]
            hi, lo = whi[:, k % NB, :], wlo[:, k % NB, :]
            t = AC.op(lambda e: e.activation(hi, src, ACT.Copy), arrived(n), piece_free.get(k - NB))
            t = DV.op(lambda e: e.tensor_tensor(lo, src, hi.bitcast(F32), ALU.subtract), t)
            loads[n]["released"] = t
            ready[k] = t

        ready = {}

        raw = []

        def raw_slots(n):
            next_raw[0] += n
            return raw[next_raw[0] - n:next_raw[0]]

        def next_piece():
            k = taken[0]
            taken[0] += 1
            while prepared[0] < min(k + NB, len(pieces)):
                prepare(prepared[0])
                prepared[0] += 1
            return whi[:, k % NB, :], wlo[:, k % NB, :], ready[k], k

        def rows2(w, r0):
            return lambda s: s.rearrange("p (c n) -> p c n", c=2), w[r0:r0 + 256, :].rearrange("(c p) n -> p c n", p=P)

        def rows(w, r0, n):
            for r in range(r0, r0 + n, 256):
                load(rows2(w, r))

        def cols(w, c0):
            for r in (0, 512):
                load((lambda s: s.rearrange("p (c n) -> p c n", c=4), w[r:r + 512, c0:c0 + 512].rearrange("(c p) n -> p c n", p=P)))

        def cols256(w, c0):
            load((lambda s: s.rearrange("p (c n) -> p c n", c=8), w[:, c0:c0 + 256].rearrange("(c p) n -> p c n", p=P)))

        def plan_loads():
            w = I["even_w_in"][0]
            for i in range(2):
                cols256(w, 1536 + 256 * i)
                cols256(w, 2048 + 256 * i)
            for c0 in (512, 1024, 0):
                for i in range(2):
                    cols256(w, c0 + 256 * i)
            rows(I["even_w_out"][0], 0, 1024)
            moe_loads(0)
            w = I["odd_w_qkv"][0]
            for c0 in range(0, 2048, 256):
                cols256(w, c0)
            rows(w[:, 2048:3072], 0, 1024)
            rows(I["odd_w_o"][0], 0, 1024)
            moe_loads(1)
            for i in range(DEPTH):
                if i == 0:
                    for c0 in range(0, 3072, 512):
                        cols(I["w_in_ab_2"][0], c0)
                    wo = I["w_out_ab_2"][0]
                else:
                    w = I["w_in_nsa_2"][0]
                    for c0 in (1024, 1280):
                        cols256(w, c0)
                    cols(w, 0)
                    for name in ("cmp_k_w1_2", "cmp_v_w1_2"):
                        src = I[name][0].rearrange("(l d) c -> d l c", d=HD)
                        load(*((lambda s, h=h: s[HD * h:HD * h + HD, :].rearrange("p (l c) -> p l c", c=P), src[:, 16 * h:16 * h + 16, :])
                               for h in range(2)), split=False)
                    for c0 in (512, 1536, 2048):
                        cols(w, c0)
                    wo = I["w_out_nsa_2"][0]
                rows(wo, 0, 1024)
                for j in range(FC // 2 + 1):
                    if j < FC // 2:
                        cols256(I["w_ffn_gate_2"][i], 256 * j)
                        cols256(I["w_ffn_up_2"][i], 256 * j)
                    if j:
                        rows(I["w_ffn_down_2"][i], 256 * (j - 1), 256)
                rows(I["w_ple_gate_2"][i], 0, 1024)
                rows(I["w_ple_proj_2"][i], 0, 256)

        def moe_loads(layer):
            for e in range(NE + 1):
                if e < NE:
                    rows(I["expert_w_up"][layer, e], 0, 1024)
                if e:
                    rows(I["expert_w_down"][layer, e - 1], 0, 512)

        plan_loads()

        def of_tile(toks, tt):
            n = len(toks) // NT
            return toks[n * tt:n * tt + n]

        def transposed(src, toks):
            done = []
            for tt in range(NT):
                for h in range(2):
                    b = 2 * tt + h
                    bank = ps[b]
                    for q in range(4):
                        o, i = bank[:, q * P:q * P + P], src[:, tt, (4 * h + q) * P:(4 * h + q) * P + P]
                        fn = lambda e, o=o, i=i: e.transpose(o, i, ident)
                        if q < 3:
                            PE.quiet(fn, free[b], of_tile(toks, tt), k_cst)
                        else:
                            t = PE.op(fn)
                    i = bank[:, :].rearrange("p (a b) -> p a b", b=P)
                    oh, ol = (v[:, 4 * h:4 * h + 4, tt * P:tt * P + P] for v in (XH, XL))
                    k = AC.op(lambda e, oh=oh, i=i: e.activation(oh, i, ACT.Copy), t)
                    k = DV.op(lambda e, oh=oh, ol=ol, i=i: e.tensor_tensor(ol, i, oh.bitcast(F32), ALU.subtract), k)
                    free[b] = [k]
                    done.append(k)
            return done

        def part(src, hi, lo, toks):
            t = AC.op(lambda e: e.activation(hi, src, ACT.Copy), toks)
            return DV.op(lambda e: e.tensor_tensor(lo, src, hi.bitcast(F32), ALU.subtract), t)

        def by_tokens(lhs, n_chunks, banks, toks, chunks, c0=0):
            for c in range(c0, c0 + n_chunks):
                wh, wl, tok, k = next_piece()
                PE.wait(tok, toks(c) if callable(toks) else toks)
                lh, ll = lhs(c)
                for tt in range(NT):
                    for l, w, first, last in ((lh, wl, True, False), (lh, wh, False, False), (ll, wh, False, True)):
                        for h in range(2):
                            b = banks[2 * tt + h]
                            if c == 0:
                                PE.wait(free[b])
                            fn = lambda e, b=b, l=l[:, tt * P:tt * P + P], w=w[:, h * 512:h * 512 + 512], a=c == 0 and first, z=c == chunks - 1 and last: e.matmul(
                                ps[b][:, :], l, w, start=a, stop=z)
                            if last and ((tt == 1 and h == 1) or c == chunks - 1):
                                t = done[b] = PE.op(fn)
                            else:
                                PE.quiet(fn)
                piece_free[k] = t
            return [done[b] for b in banks]

        def small_product(w, n, bank, out, toks, dst):
            PE.wait(toks, free[bank])
            for c in range(DC):
                fn = lambda e, c=c: e.matmul(ps[bank][0:2 * n, :], w[:, c, :], XHL[:, :, c, :], start=(c == 0), stop=(c == DC - 1))
                if c < DC - 1:
                    PE.quiet(fn)
                else:
                    t = PE.op(fn)
            t = AC.op(lambda e: e.activation(dst[0:2 * n, :], ps[bank][0:2 * n, :], ACT.Copy), t)
            free[bank] = [t]
            for tt in range(NT):
                for h in (1, 0):
                    at = h * S + tt * P
                    fn = lambda e, tt=tt, h=h, at=at: e.matmul(out[:, tt, :], dst[0:2 * n, at:at + P], C(f"fold{n}", 2 * n), start=(h == 1), stop=(h == 0))
                    if tt and not h:
                        return PE.op(fn)
                    PE.quiet(fn, t)

        def by_channels(n_out, banks, toks, first=()):
            for hf in range(2):
                wh, wl, tok, k = next_piece()
                PE.wait(tok, toks)
                wh, wl = (v.rearrange("p (c n) -> p c n", c=4) for v in (wh, wl))
                for i in range(n_out):
                    PE.wait(free[banks[i]])
                    o, cs_ = ps[banks[i]][:, 0:S], slice(i * P, i * P + P)
                    for c in range(4):
                        x = 4 * hf + c
                        PE.quiet(lambda e, o=o, cs_=cs_, c=c, x=x, wl=wl: e.matmul(o, wl[:, c, cs_], XH[:, x, :], start=(x == 0), stop=False))
                        PE.quiet(lambda e, o=o, cs_=cs_, c=c, x=x, wh=wh: e.matmul(o, wh[:, c, cs_], XL[:, x, :], start=False, stop=False))
                        fn = lambda e, o=o, cs_=cs_, c=c, x=x, wh=wh: e.matmul(o, wh[:, c, cs_], XH[:, x, :], start=False, stop=(x == 7))
                        if c == 3:
                            t = PE.op(fn)
                        else:
                            PE.quiet(fn)
                        if x == 7:
                            done[banks[i]] = t
                piece_free[k] = t
            return [done[b] for b in banks]

        def by_token_cols(groups, toks):
            for q in range(4):
                wh, wl, tok, k = next_piece()
                PE.wait(tok, toks)
                wh, wl = (v.rearrange("p (c n) -> p c n", c=2) for v in (wh, wl))
                for tt in range(NT):
                    for c0, n, banks in groups:
                        PE.wait(free[banks[tt]] if q == 0 else None)
                    for c in range(2):
                        x, rows_ = 2 * q + c, slice(tt * P, tt * P + P)
                        for l, w, first, last in ((XH, wl, True, False), (XH, wh, False, False), (XL, wh, False, True)):
                            for c0, n, banks in groups:
                                b = banks[tt]
                                fn = lambda e, b=b, l=l[:, x, rows_], w=w[:, c, c0:c0 + n], n=n, a=x == 0 and first, z=x == 7 and last: e.matmul(
                                    ps[b][:, 0:n], l, w, start=a, stop=z)
                                if last and (c == 1):
                                    t = done[b] = PE.op(fn)
                                else:
                                    PE.quiet(fn)
                piece_free[k] = t
            return [[done[b] for b in banks] for _, _, banks in groups]

        done = [None] * 8

        def residual(banks, toks, scale, dst):
            r = []
            for tt in range(NT):
                for h in range(2):
                    b = banks[2 * tt + h]
                    sl = slice(h * 512, h * 512 + 512)
                    k = DV.op(lambda e, b=b, tt=tt, sl=sl: e.scalar_tensor_tensor(
                        dst[:, tt, sl], X[:, tt, sl], float(scale), ps[b][:, :], ALU.mult, ALU.add), toks[2 * tt + h])
                    free[b] = [k]
                    r.append(k)
            return r

        nst, nag, nrs = sb("nst", [P, 2 * NT, 6]), sb("nag", [P, NT, 2]), sb("nrs", [P, NT])
        gb_free, gb_n = [None], [0]

        def load_rows(*rows):
            for i, v in enumerate(rows):
                k = PL.dma(lambda e, i=i, v=v: e.dma_start(GB[:, i, :], v.partition_broadcast(P)), c_gb, gb_free[0])
            return k

        def layer_norm(toks, gb):
            ks, res = {}, []
            for tt in range(NT):
                k = [DV.op(lambda e, tt=tt, h=h: e.bn_stats(nst[:, 2 * tt + h, :], R[:, tt, h * 512:h * 512 + 512]), of_tile(toks, tt), res) for h in range(2)]
                km = DV.op(lambda e, tt=tt: e.bn_aggr(nag[:, tt, :], nst[:, 2 * tt:2 * tt + 2, :]), k)
                k = DV.op(lambda e, tt=tt: e.tensor_scalar(nrs[:, tt:tt + 1], nag[:, tt, 1:2], LN_EPS, None, ALU.add), km)
                k = AC.op(lambda e, tt=tt: e.activation(nrs[:, tt:tt + 1], nrs[:, tt:tt + 1], ACT.Sqrt), k)
                ks[tt] = km, k
                if tt == 1:
                    normalise(0, ks, res, gb)
            normalise(1, ks, res, gb)
            gb_free[0] = res[-1]
            return res

        def normalise(tt, ks, res, gb):
            km, k = ks[tt]
            k0 = DV.op(lambda e: e.scalar_tensor_tensor(R[:, tt, :], R[:, tt, :], nag[:, tt, 0:1], GB[:, 0, :], ALU.subtract, ALU.mult), km, gb)
            k = DV.op(lambda e: e.reciprocal(nrs[:, tt:tt + 1], nrs[:, tt:tt + 1]), k)
            res.append(DV.op(lambda e: e.scalar_tensor_tensor(X[:, tt, :], R[:, tt, :], nrs[:, tt:tt + 1], GB[:, 1, :], ALU.mult, ALU.add), k0, k))

        def rms_to(toks, g, after=None):
            gb = load_rows(g)
            res = []
            ss = nst[:, 0, 0:NT]
            ks = [AC.op(lambda e, tt=tt: e.activation(R[:, tt, :], X[:, tt, :], ACT.Square, accum_out=ss[:, tt:tt + 1]), of_tile(toks, tt), after)
                  for tt in range(NT)]
            for tt in range(NT):
                k = DV.op(lambda e, tt=tt: e.tensor_scalar(nrs[:, tt:tt + 1], ss[:, tt:tt + 1], 1.0 / D, RMS_EPS, ALU.mult, ALU.add), ks[tt])
                k = AC.op(lambda e, tt=tt: e.activation(nrs[:, tt:tt + 1], nrs[:, tt:tt + 1], ACT.Sqrt), k)
                k = DV.op(lambda e, tt=tt: e.reciprocal(nrs[:, tt:tt + 1], nrs[:, tt:tt + 1]), k)
                res.append(DV.op(lambda e, tt=tt: e.scalar_tensor_tensor(R[:, tt, :], X[:, tt, :], nrs[:, tt:tt + 1], GB[:, 0, :], ALU.mult, ALU.mult), k, gb))
            gb_free[0] = res[-1]
            return res

        c_x, c_cst, c_tab = Counter(sem("s_x")), Counter(sem("s_cst")), Counter(sem("s_tab"))
        c_id = Counter(sem("s_id"))
        k_x = [SP.dma(lambda e, tt=tt: e.dma_start(X[:, tt, :], I["x"][0, tt * P:tt * P + P, :]), c_x) for tt in range(NT)][-1:]
        k_cst = SP.dma(lambda e: e.dma_start(cst[:, 0:P], I["consts"][:, 0:P]), c_id)
        k_rest = AC.dma(lambda e: e.dma_start(cst[:, P:], I["consts"][:, P:]), c_cst, k_cst)
        hg = sb("hg", [P, 8])
        cw = sb("cw", [P, 4, 37])
        rbt = sb("rbt", [P, DEPTH, 36])
        rwt = GB[:, 1, 0:DEPTH * DC * 36].rearrange("p (c n) -> p c n", n=36)
        rwhl = sb("rwhl", [P, DEPTH * DC, 72], F32R)
        rel = sb("rel", [33, NH])
        k_cw = SP.dma(lambda e: e.dma_start(cw[:], I["conv_taps"]), Counter(sem("s_cw")))
        AC.dma(lambda e: e.dma_start(hg[:], I["head_gains"]), c_in)
        AC.dma(lambda e: e.dma_start(rwt, I["router_w"].rearrange("p l c n -> p (l c) n")), c_in)
        k_in = AC.dma(lambda e: e.dma_start(rbt[:].rearrange("p l n -> p (l n)"), I["router_b"].rearrange("l n -> (l n)").partition_broadcast(P)), c_in)
        btab = sb("btab", [P, NT, NCMP, NH])
        tables = arena[0:33, AW - 768 - NCMP * S:AW]
        t = DV.op(lambda e: e.memset(rel[:, :], 1.0))
        AC.dma(lambda e: e.dma_start(rel[0:32, :], I["rel_bias_2"]), c_tab, t)
        k_tab = AC.dma(lambda e: e.dma_start(tables, I["bias_tables"]), c_tab)
        dummy = sb("spare", [P, 2])
        k_dummy = DV.op(lambda e: e.memset(dummy[:, :], 1.0))

        def table_of(func):
            AC.op(lambda e: e.activation(dummy[:, 1:2], dummy[:, 0:1], func), k_dummy, AC.last())

        def clear_rows():
            zeros = R[:, 1, 0:512]
            t = PL.op(lambda e: e.memset(zeros, 0.0), DV.last())
            rest = ys[YR:, :].rearrange("r (h c) -> (r h) c", c=512)
            for r in range(0, 2 * (SLOTS + WIN), P):
                n = min(P, 2 * (SLOTS + WIN) - r)
                PL.dma(lambda e, r=r, n=n: e.dma_start(rest[r:r + n, :], zeros[0:n, :]), c_tv, t)

        def bias_rows():
            tvs = R[0:NH, 0, 0:768].rearrange("p (a b) -> p a b", a=2)
            for a in range(2):
                t = PE.op(lambda e, a=a: e.matmul(ps[a][0:NH, 0:384], rel[:, :], tables[:, 384 * a:384 * a + 384], start=True, stop=True), k_tab, free[a])
                k = DV.op(lambda e, a=a: e.tensor_copy(tvs[:, a, :], ps[a][0:NH, 0:384]), t)
                free[a] = [k]
            PL.dma(lambda e: e.dma_start(tv.rearrange("a h c -> h a c"), tvs), c_tv, k)
            for tt in range(NT):
                for c in range(NCMP):
                    at = 768 + c * S + tt * P
                    t = PE.op(lambda e, tt=tt, c=c, at=at: e.matmul(ps[2][:, (tt * NCMP + c) * NH:(tt * NCMP + c) * NH + NH],
                                                                    tables[:, at:at + P], rel[:, :], start=True, stop=True), free[2])
            k = DV.op(lambda e: e.tensor_copy(btab[:, :, :, :].rearrange("p a b c -> p (a b c)"), ps[2][:, 0:NT * NCMP * NH]), t)
            free[2] = [k]


        k_rwhl = []

        def conv_mixer():
            kx = transposed(X, k_x * 2)
            A = stage()
            gp = A.take(4, 286)
            ap_ = A.take(4, 258)
            ac, ab, gc, sg, sq = A.take(4, S), A.take(4, S), A.take(4, S), A.take(4, S), A.take(4, S)
            ya, yb = sg, sq
            yh, yl = A.take_r(8, S), A.take_r(8, S)
            mean, var = A.take(S), A.take(S)
            z = [DV.op(lambda e: e.memset(gp[:, :, 0:30], 0.0)), DV.op(lambda e: e.memset(ap_[:, :, 0:2], 0.0))]

            kg = []
            for j in range(2):
                tv_ = by_channels(2, (4, 5), kx)
                tg = by_channels(2, (6, 7), kx)
                for h in range(2):
                    i = 2 * j + h
                    t = AC.op(lambda e, i=i, h=h: e.activation(sg[:, i, :], ps[6 + h][:, 0:S], ACT.Sigmoid), tg[h])
                    free[6 + h] = [t]
                    t = DV.op(lambda e, i=i, h=h: e.tensor_tensor(gp[:, i, 30:286], ps[4 + h][:, 0:S], sg[:, i, :], ALU.mult), t, tv_[h])
                    free[4 + h] = [t]
                    kg.append(t)

            def conv_b(i, Q):
                t = Q.op(lambda e: e.tensor_scalar(gc[:, i, :], gp[:, i, 0:S], cw[:, i, 0:1], cw[:, i, 34:35], ALU.mult, ALU.add), kg[i], z, k_cw)
                yield t
                for k in range(1, 31):
                    t = Q.op(lambda e, k=k: e.scalar_tensor_tensor(gc[:, i, :], gp[:, i, k:k + S], cw[:, i, k:k + 1], gc[:, i, :],
                                                                   ALU.mult, ALU.add), t)
                    yield t

            taps = zip(*(conv_b(i, DV) for i in range(3)))

            def some_taps(n):
                for _, three in zip(range(n), taps):
                    ends[0:3] = list(three)

            ends = [None] * 4
            diag = [R[:, 1, 512 + P * k:640 + P * k] for k in range(4)]
            diag_free = {}

            def diagonals(k0, k1):
                for k in range(k0, k1):
                    t = AC.op(lambda e, k=k: e.activation(diag[k % 4], ident, ACT.Copy, scale=cw[:, 3, k:k + 1]), diag_free.get(k - 4), kg[3], z, k_cw)
                    diag_free[k] = PE.op(lambda e, k=k: e.matmul(ps[7][:, 0:S], diag[k % 4], gp[:, 3, k:k + S], start=(k == 0), stop=(k == 30)), t, free[7])
                if k1 == 31:
                    ends[3] = AC.op(lambda e: e.activation(gc[:, 3, :], ps[7][:, 0:S], ACT.Identity, bias=cw[:, 3, 34:35]), diag_free[30])
                    free[7] = [ends[3]]

            kc_, kb_, ka = [], [], []
            some_taps(5)
            for j in range(2):
                t = by_channels(2, (2 * j, 2 * j + 1), kx)
                for h in range(2):
                    i = 2 * j + h
                    k = AC.op(lambda e, i=i: e.activation(ac[:, i, :], ps[i][:, 0:S], ACT.Copy), t[h])
                    free[i] = [k]
                    kc_.append(k)
                some_taps(6)
                diagonals(8 * j, 8 * j + 8)
            for j in range(2):
                t = by_channels(2, (4, 5), kx)
                for h in range(2):
                    i = 2 * j + h
                    k = DV.op(lambda e, i=i, h=h: e.tensor_tensor(ap_[:, i, 2:258], ps[4 + h][:, 0:S], ac[:, i, :], ALU.mult), t[h], kc_[i])
                    free[4 + h] = [k]
                    ka.append(k)
                some_taps(6)
                diagonals(16 + 8 * j, min(24 + 8 * j, 31))
            for j in range(2):
                t = by_channels(2, (2 * j, 2 * j + 1), kx)
                for h in range(2):
                    i = 2 * j + h
                    k = AC.op(lambda e, i=i: e.activation(ab[:, i, :], ps[i][:, 0:S], ACT.Copy), t[h])
                    free[i] = [k]
                    kb_.append(k)
                some_taps(5)
            clear_rows()
            bias_rows()
            for q in (PE, DV, AC, PL):
                q.wait(k_in, k_rest)
            k_rwhl.append(part(rwt, rwhl[:, :, 0:36], rwhl[:, :, 36:72], k_in))
            gb_free[0] = k_rwhl[0]
            some_taps(31)
            t = ka
            for tap in range(3):
                t2 = []
                for i in range(4):
                    if tap == 0:
                        t2.append(DV.op(lambda e, i=i: e.tensor_scalar(ya[:, i, :], ap_[:, i, 0:S], cw[:, i, 31:32], None, ALU.mult), ka[i], z))
                    else:
                        t2.append(DV.op(lambda e, i=i, tap=tap: e.scalar_tensor_tensor(
                            ya[:, i, :], ap_[:, i, tap:tap + S], cw[:, i, 31 + tap:32 + tap], ya[:, i, :], ALU.mult, ALU.add), t[i]))
                t = t2
            ky = DV.op(lambda e: e.tensor_tensor(ya, ya, ab, ALU.mult), t, kb_)
            ky = part(ya, yh[:, 0:4, :], yl[:, 0:4, :], ky)

            def sums(src, toks, bank):
                PE.wait(toks, free[bank])
                for i in range(4):
                    fn = lambda e, i=i: e.matmul(ps[bank][:, 0:S], ones, src[:, i, :], start=(i == 0), stop=(i == 3))
                    if i < 3:
                        PE.quiet(fn)
                    else:
                        return PE.op(fn)

            t = sums(gc, ends, 4)
            t = DV.op(lambda e: e.tensor_scalar(mean, ps[4][:, 0:S], 1.0 / 512, None, ALU.mult), t)
            t = DV.op(lambda e: e.tensor_tensor(gc, gc, mean.unsqueeze(1).to_broadcast([P, 4, S]), ALU.subtract), t)
            kd = t
            t = AC.op(lambda e: e.activation(sq, gc, ACT.Square), t)
            t = sums(sq, [t], 5)
            t = DV.op(lambda e: e.tensor_scalar(var, ps[5][:, 0:S], 1.0 / 512, LN_EPS, ALU.mult, ALU.add), t)
            t = AC.op(lambda e: e.activation(var, var, ACT.Sqrt), t)
            t = DV.op(lambda e: e.reciprocal(var, var), t)
            t = DV.op(lambda e: e.tensor_tensor(gc, gc, var.unsqueeze(1).to_broadcast([P, 4, S]), ALU.mult), t, kd)
            ks = [AC.op(lambda e, i=i: e.activation(yb[:, i, :], gc[:, i, :], ACT.Silu, scale=cw[:, i, 35:36], bias=cw[:, i, 36:37]), t)
                  for i in range(4)]
            free[4], free[5] = [kd], [t]
            ks = part(yb, yh[:, 4:8, :], yl[:, 4:8, :], ks)
            k = by_tokens(lambda c: (yh[:, c, :], yl[:, c, :]), 8, [0, 1, 2, 3], lambda c: ky if c < 4 else ks, 8)
            DV.wait((c_tv.sem, c_tv.n))
            return residual([0, 1, 2, 3], k, ALPHA, R)

        def moe(layer, toks):
            kx = transposed(X, toks)
            A = stage()
            rb = rbt[:, layer, :]
            XsT = A.take(DC, SLOTS + WIN)
            Yg = XsT.rearrange("p c s -> p (c s)")[:, 0:2 * NT * D].rearrange("p (a b) -> p a b", b=D)
            xh, xl = A.take_r(NT, D), A.take_r(NT, D)
            Pm = A.take_r(NT, SLOTS)
            r_ = lambda at, *shape: shaped(arena_r[:, at:at + int(np.prod(shape))], shape)
            xe = [r_(1024 * i, DC, W2) for i in range(2)]
            hT = [r_(2048 + 512 * i, 4, W2) for i in range(2)]
            usb = [A.take(2 * F_E) for _ in range(2)]
            sil = [A.take(4, WIN) for _ in range(2)]
            hh = [A.take(4, WIN) for _ in range(2)]
            low = [A.take(512) for _ in range(2)]
            ysb = [A.take(D) for _ in range(2)]
            wov = A.take(D)
            kxh = AC.op(lambda e: e.activation(xh, X[:, :, :], ACT.Copy), toks)
            kxl = PL.op(lambda e: e.tensor_tensor(xl, X[:, :, :], xh.bitcast(F32), ALU.subtract), kxh)
            kz = DV.op(lambda e: e.memset(XsT[:, :, SLOTS:SLOTS + WIN], 0.0))

            lp = ps[4][:, 0:72].rearrange("p (a b) -> p a b", b=36)
            t = small_product(rwhl[:, layer * DC:layer * DC + DC, :], 36, 5, lp, [kx, k_rwhl, k_rest], usb[0][:, 0:512])
            lg = S_(NT, 36)
            bc = lambda v, *s: v.to_broadcast([P, *s])
            k_lg = t = DV.op(lambda e: e.tensor_tensor(lg, lp, bc(rb.unsqueeze(1), NT, 36), ALU.add), t, k_in)

            def V(fn, *toks):
                return DV.op(fn, *toks)

            gm, gd, ge, gs = S_(NT), S_(NT, NG), S_(NT, NG), S_(NT)
            goh, gt, gi = S_(NT, NG), S_(NT, NG), S_(NT)
            gl = lg[:, :, 0:NG]
            t = V(lambda e: e.tensor_reduce(gm, gl, AX.X, ALU.max), t)
            t = kgd = V(lambda e: e.tensor_tensor(gd, gl, bc(gm.unsqueeze(2), NT, NG), ALU.subtract), t)
            ka = AC.op(lambda e: e.activation(ge, gd, ACT.Exp), t)
            t = V(lambda e: e.tensor_tensor(gt, gl, bc(gm.unsqueeze(2), NT, NG), ALU.is_equal), t)
            t = V(lambda e: e.tensor_tensor(gt, gt, bc(C("io4m").unsqueeze(1), NT, NG), ALU.mult), t)
            t = V(lambda e: e.tensor_reduce(gi, gt, AX.X, ALU.min), t)
            t = V(lambda e: e.tensor_tensor(goh, bc(C("io4m").unsqueeze(1), NT, NG), bc(gi.unsqueeze(2), NT, NG), ALU.is_equal), t)
            mneg, ml = S_(NT, NG), S_(NT, NE)
            ml4 = ml.rearrange("p t (g e) -> p t g e", g=NG)
            el4 = lg[:, :, NG:36].rearrange("p t (g e) -> p t g e", g=NG)
            t1 = V(lambda e: e.tensor_scalar(mneg, goh, -1.0, BIG, ALU.add, ALU.mult), t)
            t = V(lambda e: e.tensor_tensor(ml4, el4, bc(goh.unsqueeze(3), NT, NG, 8), ALU.mult), t)
            t = V(lambda e: e.tensor_tensor(ml4, ml4, bc(mneg.unsqueeze(3), NT, NG, 8), ALU.add), t, t1)
            oh = [S_(NT, NE) for _ in range(2)]
            mx = [S_(NT) for _ in range(2)]
            ix = [S_(NT) for _ in range(2)]
            eq = S_(NT, NE)
            io = bc(C("io32m").unsqueeze(1), NT, NE)
            for k in range(2):
                t = V(lambda e, k=k: e.tensor_reduce(mx[k], ml, AX.X, ALU.max), t)
                t = V(lambda e, k=k: e.tensor_tensor(eq, ml, bc(mx[k].unsqueeze(2), NT, NE), ALU.is_equal), t)
                t = V(lambda e, k=k: e.tensor_tensor(eq, eq, io, ALU.mult), t)
                t = V(lambda e, k=k: e.tensor_reduce(ix[k], eq, AX.X, ALU.min), t)
                t = V(lambda e, k=k: e.tensor_tensor(oh[k], io, bc(ix[k].unsqueeze(2), NT, NE), ALU.is_equal), t)
                if k == 0:
                    t = V(lambda e: e.scalar_tensor_tensor(ml, oh[0], -BIG, ml, ALU.mult, ALU.add), t)
            M = S_(NT, NE)
            t = kM = V(lambda e: e.tensor_tensor(M, oh[0], oh[1], ALU.add), t)
            before = C("before")
            rk, sz, szT = ps[5][:, 0:64], ps[5][:, 64:96], ps[6][0:NE, 0:P]
            PE.wait(kM)
            for tt in range(NT):
                fn = lambda e, tt=tt: e.matmul(szT, M[:, tt, :], ones, start=(tt == 0), stop=(tt == 1))
                if tt:
                    ksT = PE.op(fn)
                else:
                    PE.quiet(fn)
            PE.quiet(lambda e: e.matmul(rk[:, 0:NE], before, M[:, 0, :], start=True, stop=True))
            PE.quiet(lambda e: e.matmul(rk[:, NE:64], ones, M[:, 0, :], start=True, stop=False))
            PE.quiet(lambda e: e.matmul(rk[:, NE:64], before, M[:, 1, :], start=False, stop=True))
            for tt in range(NT):
                kr = PE.op(lambda e, tt=tt: e.matmul(sz, ones, M[:, tt, :], start=(tt == 0), stop=(tt == 1)))
            szs, exT, st, cx, size, ext = S_(P), S_(P), S_(NE), S_(NE), S_(NE), S_(NE)
            szs, exT = szs[0:NE, :], exT[0:NE, :]
            t = ksz = V(lambda e: e.tensor_copy(szs, szT), ksT)
            kp = PE.op(lambda e: e.matmul(ps[6][:, 128:160], szs, before[0:NE, 0:NE], start=True, stop=True), ksz)
            rank, pos, pk, rr, far = S_(NT, NE), S_(NT, NE), S_(2, NT), S_(2, NT), S_(2, NT)
            t = k_rk = V(lambda e: e.tensor_copy(rank, rk.rearrange("p (t e) -> p t e", t=NT)), kr)
            t0 = V(lambda e: e.tensor_copy(size, sz), kr)
            k_st = V(lambda e: e.tensor_copy(st, ps[6][:, 128:160]), kp)
            tp = V(lambda e: e.tensor_tensor(pos, rank, bc(st.unsqueeze(1), NT, NE), ALU.add), t, k_st)
            tq = []
            for k in range(2):
                a = V(lambda e, k=k: e.tensor_tensor(eq, oh[k], pos, ALU.mult), tp, tq[-1:])
                b = V(lambda e, k=k: e.tensor_reduce(pk[:, k, :], eq, AX.X, ALU.add), a)
                tq.append(b)
            k_pm = []
            for tt in range(NT):
                a = V(lambda e, tt=tt: e.tensor_scalar(Pm[:, tt, :], C("slot"), pk[:, 0, tt:tt + 1], None, ALU.is_equal), tq)
                k_pm.append(V(lambda e, tt=tt: e.scalar_tensor_tensor(Pm[:, tt, :], C("slot"), pk[:, 1, tt:tt + 1], Pm[:, tt, :].bitcast(F32),
                                                                      ALU.is_equal, ALU.add), a))
            k_xs = []
            for c in range(DC):
                b = c % 4
                PE.wait(free[b], k_pm, kxh, kxl)
                for i, (x, tt) in enumerate(((xl, 0), (xl, 1), (xh, 0), (xh, 1))):
                    fn = lambda e, b=b, c=c, x=x, tt=tt, i=i: e.matmul(ps[b][:, :], x[:, tt, c * P:c * P + P], Pm[:, tt, :], start=(i == 0), stop=(i == 3))
                    if i < 3:
                        PE.quiet(fn)
                    else:
                        t = PE.op(fn)
                if c % 2:
                    k = AC.op(lambda e, b=b, c=c: e.activation(XsT[:, c, 0:SLOTS], ps[b][:, :], ACT.Copy), t)
                else:
                    k = DV.op(lambda e, b=b, c=c: e.tensor_copy(XsT[:, c, 0:SLOTS], ps[b][:, :]), t)
                free[b] = [k]
                k_xs.append(k)
            k_oi = V(lambda e: e.tensor_copy(oi[:, 0:NE], st[0:1, :]), k_st)

            w2, wt = S_(NT), S_(2, NT)

            def rest_of_routing():
                t = V(lambda e: e.tensor_tensor(w2, mx[1], mx[0], ALU.subtract))
                ka2 = AC.op(lambda e: e.activation(w2, w2, ACT.Exp), t)
                t = V(lambda e: e.tensor_reduce(gs, ge, AX.X, ALU.add), ka)
                t2 = V(lambda e: e.tensor_scalar(wt[:, 0, :], w2, 1.0, None, ALU.add), ka2)
                yield
                t = V(lambda e: e.tensor_tensor(gs, gs, wt[:, 0, :], ALU.mult), t, t2)
                t = V(lambda e: e.reciprocal(wt[:, 0, :], gs), t)
                k_wt = V(lambda e: e.tensor_tensor(wt[:, 1, :], wt[:, 0, :], w2, ALU.mult), t)
                yield
                def windows(o, i, toks):
                    t = V(lambda e: e.tensor_scalar(o, i, float(WIN), None, ALU.is_gt), toks)
                    for j in range(2, S // WIN):
                        t = V(lambda e, j=j: e.scalar_tensor_tensor(o, i, float(WIN * j), o, ALU.is_gt, ALU.add), t)
                    return t

                t = windows(exT, szs, ksz)
                kp = PE.op(lambda e: e.matmul(ps[TB][:, 448:480], exT, before[0:NE, 0:NE], start=True, stop=True), t, free[TB])
                k_ext = windows(ext, size, t0)
                k_cx = V(lambda e: e.tensor_copy(cx, ps[TB][:, 448:480]), kp)
                free[TB] = [k_cx]
                for k in range(2):
                    a = V(lambda e, k=k: e.tensor_tensor(eq, oh[k], rank, ALU.mult), k_rk, tq[-1:])
                    tq.append(V(lambda e, k=k: e.tensor_reduce(rr[:, k, :], eq, AX.X, ALU.add), a))
                er = S_(2, NT)
                for k in range(2):
                    a = V(lambda e, k=k: e.tensor_scalar(er[:, k, :], ix[k], 64.0, float(WIN), ALU.add, ALU.mult))
                    tq.append(a)
                a = V(lambda e: e.tensor_tensor(er, er, rr, ALU.add), tq)
                b = V(lambda e: e.tensor_scalar(far, rr, float(WIN), None, ALU.is_ge), tq)
                yield
                c_ = V(lambda e: e.tensor_tensor(pk, pk, er, ALU.subtract), a, k_pm)
                c_ = V(lambda e: e.tensor_scalar(pk, pk, float(YR), None, ALU.add), c_)
                c_ = V(lambda e: e.tensor_tensor(pk, pk, far, ALU.mult), c_, b)
                yield
                c_ = V(lambda e: e.tensor_tensor(er, er, pk, ALU.add), c_)
                k_yi = V(lambda e: e.tensor_copy(yi[:, :].rearrange("p (a b) -> p a b", b=NT), er), c_)
                o1, o2, o3 = A.take(NOV, NE), A.take(NOV, NE), A.take(NOV, NE)
                o1, o2, o3 = o1[0:1, :, :], o2[0:1, :, :], o3[0:1, :, :]
                ofl = S_(2 * NOV + 1)[0:1, :]
                b1 = lambda v: v.to_broadcast([1, NOV, NE])
                a = V(lambda e: e.tensor_tensor(o1, b1(C("windows", 1).unsqueeze(2)), b1(cx[0:1, :].unsqueeze(1)), ALU.subtract), k_cx)
                yield
                b = V(lambda e: e.tensor_tensor(o2, o1, b1(ext[0:1, :].unsqueeze(1)), ALU.is_lt), a, k_ext)
                a = V(lambda e: e.scalar_tensor_tensor(o2, o1, 0.0, o2, ALU.is_ge, ALU.mult), b)
                b = V(lambda e: e.scalar_tensor_tensor(o1, o1, float(WIN), b1(st[0:1, :].unsqueeze(1)), ALU.mult, ALU.add), a)
                yield
                b = V(lambda e: e.tensor_scalar(o1, o1, float(WIN - SLOTS), None, ALU.add), b)
                b = V(lambda e: e.tensor_tensor(o1, o1, o2, ALU.mult), b)
                b = V(lambda e: e.tensor_reduce(ofl[:, 0:NOV], o1, AX.X, ALU.add), b)
                yield
                b = V(lambda e: e.tensor_scalar(ofl[:, 0:NOV], ofl[:, 0:NOV], float(SLOTS), None, ALU.add), b)
                a = V(lambda e: e.tensor_tensor(o3, o2, b1(C("io32", 1).unsqueeze(1)), ALU.mult), a)
                a = V(lambda e: e.tensor_reduce(ofl[:, NOV:2 * NOV], o3, AX.X, ALU.add), a)
                yield
                c_ = V(lambda e: e.tensor_reduce(ofl[:, 2 * NOV:2 * NOV + 1], ext[0:1, :], AX.X, ALU.add), k_ext)
                k_ofl = V(lambda e: e.tensor_copy(oi[:, NE:NE + 2 * NOV + 1], ofl), a, b, c_, k_oi)
                k_al = [AC.op(lambda e, tt=tt: e.activation(R[:, tt, :], X[:, tt, :], ACT.Copy, scale=float(ALPHA))) for tt in range(NT)]
                yield k_wt, k_yi, k_ofl, k_al

            U = [[0, 1], [2, 3]]
            TB, YB = 4, [5, 6]
            PE.wait(k_st)
            up_done = {}
            y_done = [None, None]
            xe_done = {}

            def gather(e_):
                ap = oi[0:1, e_:e_ + 1]
                PL.wait(k_oi, k_xs, kz, up_done.get(e_ - 2))
                hi, lo = xe[e_ % 2][:, :, 0:WIN], xe[e_ % 2][:, :, WIN:W2]

                def fn(e):
                    r = e.value_load(ap, min_val=0, max_val=SLOTS)
                    return e.tensor_copy(hi, XsT[:, :, bass.ds(r, WIN)])

                def fn2(e):
                    r = e.value_load(ap, min_val=0, max_val=SLOTS)
                    return e.tensor_tensor(lo, XsT[:, :, bass.ds(r, WIN)], hi.bitcast(F32), ALU.subtract)
                t = PL.op(fn)
                xe_done[e_] = PL.op(fn2, t)

            def up(e_, chunks):
                u = U[e_ % 2]
                PE.wait(xe_done[e_])
                for c in chunks:
                    wh, wl, tok, k = next_piece()
                    PE.wait(tok)
                    if c == 0:
                        PE.wait(free[u[0]], free[u[1]])
                    for w, last in ((wl, False), (wh, True)):
                        for h in range(2):
                            fn = lambda e, c=c, h=h, w=w, last=last: e.matmul(ps[u[h]][0:W2, :], xe[e_ % 2][:, c, :], w[:, h * 512:h * 512 + 512],
                                                                              start=(c == 0 and not last), stop=(c == DC - 1 and last))
                            if last and h:
                                piece_free[k] = up_done[e_] = PE.op(fn)
                            else:
                                PE.quiet(fn)

            def up_out(e_):
                for h in range(2):
                    u = U[e_ % 2][h]
                    t = usb_done[e_] = AC.op(lambda e, u=u, h=h: e.activation(usb[e_ % 2][0:W2, h * F_E:h * F_E + F_E], ps[u][0:W2, :], ACT.Copy), up_done[e_], turned.get(e_ - 2))
                    free[u] = [t]

            usb_done, turned, split_done, sil_done, down_done = {}, {}, {}, {}, {}

            def turn(e_):
                i = e_ % 2
                tb = ps[TB][:, 0:8 * WIN].rearrange("p (m c n) -> p m c n", m=2, c=4)
                PE.wait(usb_done[e_], free[TB])
                for m in range(2):
                    for f in range(4):
                        at = m * F_E + f * P
                        fn = lambda e, m=m, f=f, at=at: e.matmul(tb[:, m, f, :], usb[i][0:W2, at:at + P], C("fold", W2), start=True, stop=True)
                        if m and f == 3:
                            turned[e_] = PE.op(fn)
                        else:
                            PE.quiet(fn)
                t = AC.op(lambda e: e.activation(sil[i], tb[:, 0, :, :], ACT.Silu), turned[e_], sil_done.get(e_ - 2))
                t = sil_done[e_] = DV.op(lambda e: e.tensor_tensor(hh[i], sil[i], tb[:, 1, :, :], ALU.mult), t, split_done.get(e_ - 2))
                free[TB] = [t]
                split_done[e_] = part(hh[i], hT[i][:, :, 0:WIN], hT[i][:, :, WIN:W2], [t, down_done.get(e_ - 2)])

            def down(e_):
                i = e_ % 2
                PE.wait(split_done[e_])
                for f in range(4):
                    wh, wl, tok, k = next_piece()
                    PE.wait(tok)
                    if f == 0:
                        PE.wait(free[YB[0]], free[YB[1]])
                    for w, last in ((wl, False), (wh, True)):
                        for h in range(2):
                            fn = lambda e, f=f, h=h, w=w, last=last: e.matmul(ps[YB[h]][0:W2, :], hT[i][:, f, :], w[:, h * 512:h * 512 + 512],
                                                                              start=(f == 0 and not last), stop=(f == 3 and last))
                            if last and h:
                                piece_free[k] = t = PE.op(fn)
                            else:
                                PE.quiet(fn)
                down_done[e_] = t
                ks = []
                for h in range(2):
                    k = AC.op(lambda e, h=h: e.activation(low[h][0:WIN, :], ps[YB[h]][WIN:W2, :], ACT.Copy), t, low_free[h])
                    k = low_free[h] = DV.op(lambda e, h=h: e.tensor_tensor(ysb[i][0:WIN, h * 512:h * 512 + 512], low[h][0:WIN, :], ps[YB[h]][0:WIN, :], ALU.add), k, y_done[i])
                    free[YB[h]] = [k]
                    ks.append(k)
                if e_ < NE - 1:
                    y_done[i] = PL.dma(lambda e: e.dma_start(ys[e_ * WIN:e_ * WIN + WIN, :], ysb[i][0:WIN, :]), c_y[i], ks)
                else:
                    for h, k in enumerate(ks):
                        sl = slice(h * 512, h * 512 + 512)
                        y_done[i] = AC.dma(lambda e, sl=sl: e.dma_start(ys[e_ * WIN:e_ * WIN + WIN, sl], ysb[i][0:WIN, sl]), c_yl, k)

            low_free = [None, None]
            free[TB] = [k_lg]
            free[5] = free[6] = [k_st, t0, tp]
            slices, late = rest_of_routing(), None
            gather(0)
            for e_ in range(NE + 1):
                if e_ + 1 < NE:
                    gather(e_ + 1)
                if e_ < NE:
                    up(e_, range(0, 4))
                if e_ >= 1:
                    late = next(slices, late)
                if e_ >= 1:
                    turn(e_ - 1)
                if e_ < NE:
                    up(e_, range(4, 8))
                    up_out(e_)
                if e_ >= 1:
                    down(e_ - 1)

            assert next(slices, None) is None
            k_wt, k_yi, k_ofl, k_al = late

            ov = c_ov[layer]
            n_ap = oi[0:1, NE + 2 * NOV:NE + 2 * NOV + 1]
            some = lambda e: e.value_load(n_ap, min_val=0, max_val=NOV) > 0
            for q in (PE, AC, DV, PL):
                q.wait(k_ofl)
            bp, ba, bv, bg = (q.branch(some) for q in (PE, AC, DV, PL))
            bs = Queue(None)
            xo, so = usb[0][:, 0:DC * WIN].rearrange("p (c n) -> p c n", c=DC), usb[0][:, 512:1024]
            ho, to, yo = usb[1][:, 0:512], usb[1][:, 512:512 + 4 * WIN].rearrange("p (c n) -> p c n", c=4), ysb[0]
            first = [q.last() for q in (PE, AC, DV, PL)] + [t for t in y_done]
            for q in (bp, ba, bv, bg, bs):
                q.wait(first, k_ofl)
            t_y = t_dn = None
            t_pe = None
            for k in range(NOV):
                sap, eap = oi[0:1, NE + k:NE + k + 1], oi[0:1, NE + NOV + k:NE + NOV + k + 1]

                def pick(e, sap=sap):
                    r = e.value_load(sap, min_val=0, max_val=SLOTS)
                    return e.tensor_copy(xo, XsT[:, :, bass.ds(r, WIN)])
                tx = bg.bump(pick, ov["pool"], t_pe)

                def piece(c, t_free):
                    def fn(e, c=c, eap=eap):
                        r = e.value_load(eap, min_val=0, max_val=NE - 1)
                        w = I["expert_w_up"][layer] if c < DC else I["expert_w_down"][layer]
                        r0 = (c if c < DC else c - DC) * P
                        src = w[bass.ds(r, 1), r0:r0 + P, :].rearrange("o p n -> p (o n)")
                        return e.dma_start(wov, src)
                    return bs.dma(fn, ov["dma"], t_free)

                for c in range(DC):
                    td = piece(c, t_pe)
                    for h in range(2):
                        fn = lambda e, c=c, h=h: e.matmul(ps[h][0:WIN, :], xo[:, c, :], wov[:, h * 512:h * 512 + 512], start=(c == 0), stop=(c == DC - 1))
                        t_pe = bp.bump(fn, ov["pe"], td, tx)
                ta = ba.bump(lambda e: e.activation(so[0:WIN, :], ps[0][0:WIN, :], ACT.Silu), ov["act"], t_pe)
                tm = bv.bump(lambda e: e.tensor_tensor(ho[0:WIN, :], so[0:WIN, :], ps[1][0:WIN, :], ALU.mult), ov["dve"], ta)
                tb = ps[TB][:, 0:4 * WIN].rearrange("p (c n) -> p c n", c=4)
                for f in range(4):
                    tt_ = bp.bump(lambda e, f=f: e.transpose(tb[:, f, :], ho[0:WIN, f * P:f * P + P], ident[0:WIN, 0:WIN]), ov["pe"], tm)
                tc = bv.bump(lambda e: e.tensor_copy(to, tb), ov["dve"], tt_)
                for f in range(4):
                    td = piece(DC + f, t_pe)
                    for h in range(2):
                        fn = lambda e, f=f, h=h: e.matmul(ps[YB[h]][0:WIN, :], to[:, f, :], wov[:, h * 512:h * 512 + 512], start=(f == 0), stop=(f == 3))
                        t_pe = bp.bump(fn, ov["pe"], td, tc)
                for h in range(2):
                    te = ba.bump(lambda e, h=h: e.activation(yo[0:WIN, h * 512:h * 512 + 512], ps[YB[h]][0:WIN, :], ACT.Copy), ov["act"], t_pe, t_y)

                def put(e, sap=sap):
                    r = e.value_load(sap, min_val=0, max_val=SLOTS)
                    return e.dma_start(ys[bass.ds(r + YR, WIN), :], yo[0:WIN, :])
                t_y = ba.dma(put, ov["y"], te)
                bp.wait(te)
            for q in (bp, ba, bv, bg):
                q.wait(t_y)

            at, rows_in = pieces[prepared[0] - 1][0] + 1, []
            r, before_ = [], [k_yi, y_done, PE.last(), DV.last(), AC.last()]
            for tt in range(NT):
                for k in range(2):
                    j = k * NT + tt
                    k_yg = PL.dma(lambda e, j=j: e.indirect_dma_start(
                        Yg[:, j, :], None, ys, bass.IndirectOffsetOnAxis(ap=yi[:, j:j + 1], axis=0)), c_yg[tt], before_)
                rows_in.append(k_yg)
                t = DV.op(lambda e, tt=tt: e.scalar_tensor_tensor(R[:, tt, :], Yg[:, tt, :], wt[:, 0, tt:tt + 1], R[:, tt, :], ALU.mult, ALU.add),
                          k_yg, k_wt, k_al)
                r.append(DV.op(lambda e, tt=tt: e.scalar_tensor_tensor(R[:, tt, :], Yg[:, NT + tt, :], wt[:, 1, tt:tt + 1], R[:, tt, :],
                                                                       ALU.mult, ALU.add), t))
            sp_branch[at] = (k_ofl, some, bs), rows_in
            return r

        sp_branch = {}

        def stick(toks):
            kx = transposed(X, toks)
            A = stage()
            qT, kT, oh, ol = A.take(8, S), A.take(8, S), A.take_r(8, S), A.take_r(8, S)
            zb = [A.take(2, 384) for _ in range(5)]
            tb = [A.take(2, 384) for _ in range(5)]
            V = R
            k_q = {}
            for j in range(8):
                b = (4 + 2 * (j % 2), 5 + 2 * (j % 2))
                ts = by_channels(2, b, kx)
                for h in range(2):
                    i = 2 * (j % 4) + h
                    o = ps[b[h]][:, 0:S]
                    if j < 4:
                        k = AC.op(lambda e, i=i, o=o: e.activation(qT[:, i, :], o, ACT.Copy, scale=float(HD ** -0.5)), ts[h])
                    else:
                        k = DV.op(lambda e, i=i, o=o: e.tensor_copy(kT[:, i, :], o), ts[h])
                    free[b[h]] = [k]
                    k_q[j // 4, i] = k
            k = by_tokens(lambda c: (XH[:, c, :], XL[:, c, :]), 8, [0, 1, 2, 3], [], 8)
            k = dict(zip(range(4), k))
            kv = []
            for tt in range(NT):
                for h in range(2):
                    b = 2 * tt + h
                    o = V[:, tt, h * 512:h * 512 + 512]
                    if h:
                        t = AC.op(lambda e, b=b, o=o: e.activation(o, ps[b][:, :], ACT.Copy), k[b])
                    else:
                        t = DV.op(lambda e, b=b, o=o: e.tensor_copy(o, ps[b][:, :]), k[b])
                    free[b] = [t]
                    kv.append(t)
            strict, suffix = C("strict"), C("suffix")
            zk, done_a, sp, ta, ko = {}, {}, {}, {}, []

            def score(p):
                u, k = p % 5, []
                for h in range(2):
                    b, r = 2 * (p % 2) + h, slice(HD * h, HD * h + HD)
                    PE.wait(free[b], k_q[0, p], k_q[1, p])
                    PE.quiet(lambda e, b=b, r=r: e.matmul(ps[b][:, 0:S], kT[r, p, 0:P], qT[r, p, :], start=True, stop=True))
                    t = PE.op(lambda e, b=b, r=r: e.matmul(ps[b][:, S:384], kT[r, p, P:S], qT[r, p, P:S], start=True, stop=True))
                    k.append(DV.op(lambda e, b=b, u=u, h=h: e.tensor_tensor(zb[u][:, h, :], ps[b][:, 0:384], strict, ALU.add), t, done_a.get(p - 5)))
                    free[b] = k[-1:]
                t = AC.op(lambda e: e.activation(tb[u], zb[u], ACT.Abs), k)
                t = AC.op(lambda e: e.activation(tb[u], tb[u], ACT.Exp, scale=-1.0), t)
                zk[p] = AC.op(lambda e: e.activation(tb[u], tb[u], ACT.Ln, bias=1.0), t)

            def softplus(p):
                u = p % 5
                sp[p] = DV.op(lambda e: e.scalar_tensor_tensor(tb[u], zb[u], 0.0, tb[u], ALU.max, ALU.add), zk[p])

            def attend(p):
                u, k = p % 5, []
                for h in range(2):
                    b = 4 + h
                    PE.wait(sp[p], free[b])
                    PE.quiet(lambda e, b=b, h=h: e.matmul(ps[b][:, 0:384], suffix, tb[u][:, h, :], start=True, stop=False))
                    t = PE.op(lambda e, b=b, h=h: e.matmul(ps[b][:, P:S], ones, tb[u][:, h, S:384], start=False, stop=True))
                    k.append(DV.op(lambda e, b=b, h=h: e.tensor_tensor(zb[u][:, h, :], zb[u][:, h, :], ps[b][:, 0:384], ALU.subtract), t))
                    free[b] = k[-1:]
                ta[p] = AC.op(lambda e: e.activation(zb[u], zb[u], ACT.Exp), k)

            def weigh(p):
                u, b = p % 5, 6 + p % 2
                PE.wait(ta[p], kv, free[b])
                for h in range(2):
                    hh = 2 * p + h
                    r = slice(HD * h, HD * h + HD)
                    PE.quiet(lambda e, h=h, r=r, hh=hh, b=b: e.matmul(ps[b][r, 0:S], V[:, 0, hh * HD:hh * HD + HD], zb[u][:, h, 0:S], start=True, stop=False))
                    t = PE.op(lambda e, h=h, r=r, hh=hh, b=b: e.matmul(ps[b][r, P:S], V[:, 1, hh * HD:hh * HD + HD], zb[u][:, h, S:384], start=False, stop=True))
                done_a[p] = t
                k = part(ps[b][:, 0:S], oh[:, p, :], ol[:, p, :], t)
                free[b] = [k]
                ko.append(k)

            for n in range(8 + 4):
                if n >= 4:
                    weigh(n - 4)
                if 3 <= n < 11:
                    attend(n - 3)
                if 1 <= n < 9:
                    softplus(n - 1)
                if n < 8:
                    score(n)
            k = by_tokens(lambda c: (oh[:, c, :], ol[:, c, :]), 8, [0, 1, 2, 3], ko, 8)
            DV.wait(t)
            return residual([0, 1, 2, 3], k, ALPHA, R)

        def head_norm(width, gain, scale, dst, banks, tbanks, work, toks):
            nh = width // HD
            ss, res = S_(NT, nh), []
            if scale != 1.0:
                g2 = S_(1)
                kg = DV.op(lambda e: e.tensor_scalar(g2, gain, float(scale), None, ALU.mult))
            else:
                g2, kg = gain, None
            heads = lambda v: v[:, 0:width].rearrange("p (h d) -> p h d", d=HD)
            two = range(NT)
            k = [AC.op(lambda e, tt=tt: e.activation(work[tt][:, 0:width], ps[banks[tt]][:, 0:width], ACT.Square), toks[tt], wfree.get(id(work[tt]))) for tt in two]
            k = [DV.op(lambda e, tt=tt: e.tensor_reduce(ss[:, tt, :], heads(work[tt]), AX.X, ALU.add), k[tt]) for tt in two]
            k = [DV.op(lambda e, tt=tt: e.tensor_scalar(ss[:, tt, :], ss[:, tt, :], 1.0 / HD, RMS_EPS, ALU.mult, ALU.add), k[tt]) for tt in two]
            k = [AC.op(lambda e, tt=tt: e.activation(ss[:, tt, :], ss[:, tt, :], ACT.Sqrt), k[tt]) for tt in two]
            k = [DV.op(lambda e, tt=tt: e.reciprocal(ss[:, tt, :], ss[:, tt, :]), k[tt]) for tt in two]
            k = [DV.op(lambda e, tt=tt: e.tensor_tensor(heads(work[tt]), heads(ps[banks[tt]]), ss[:, tt, :].unsqueeze(2).to_broadcast([P, nh, HD]), ALU.mult), k[tt])
                 for tt in two]
            for tt in two:
                free[banks[tt]] = [k[tt]]

            def turn():
                for tt in two:
                    b, wk = tbanks[tt], work[tt]
                    for i in range(width // P):
                        t = PE.op(lambda e, i=i, b=b, wk=wk: e.transpose(ps[b][:, i * P:i * P + P], wk[:, i * P:i * P + P], ident), k[tt], free[b])
                    wfree[id(wk)] = t
                    o = dst[:, :, tt * P:tt * P + P]
                    i_ = ps[b][:, 0:width].rearrange("p (i t) -> p i t", t=P)
                    kt = AC.op(lambda e, o=o, i_=i_: e.activation(o, i_, ACT.Copy, scale=g2), t, kg)
                    free[b] = [kt]
                    res.append(kt)
            return res, turn

        wfree = {}

        def copied(width, dst, banks, toks):
            res = []
            for tt in range(NT):
                b, o = banks[tt], dst(tt)
                k = DV.op(lambda e, b=b, o=o: e.tensor_copy(o, ps[b][:, 0:width]), toks[tt])
                free[b] = [k]
                res.append(k)
            return res

        def bias_loader(bias, db, heads, which):
            used = {}
            tok = {}

            def fetch(p):
                a, kind = heads(p), which(p)
                b = bias[p % 3]
                base = (kind * NH + a) * 384
                PL.wait(used.get(p - 3))
                for lo, n in ((0, P), (P, S)):
                    src = bass.AP(tv.tensor, base, [[1, P], [db * 384, 2], [1, n]])
                    tok[p] = PL.dma(lambda e, b=b, lo=lo, n=n, src=src: e.dma_start(b[:, :, lo:lo + n], src), c_bias[p % 3])
            return fetch, tok, used

        def softmaxes(n_jobs, job, turned_to, scr, pT, stats):
            work, scr_free, pT_free = {}, {}, {}

            def scores(n):
                j = job(n)
                s_, b, (mx, sm) = scr[n % 4], n % 4, stats[n % 4]
                PE.quiet(lambda e: e.matmul(ps[b][:, S:384], j["q"][:, 0:P], j["k"][:, 0:P], start=True, stop=True), free[b], j["ready"])
                t = PE.op(lambda e: e.matmul(ps[b][:, 0:S], j["q"][:, P:S], j["k"], start=True, stop=True))
                k = DV.op(lambda e: e.tensor_tensor(s_, ps[b][:, 0:384], j["bias"][:, ::-1], ALU.add), t, j["biased"], scr_free.get(n - 4))
                free[b] = [k]
                j["done"](k)
                w = work[n] = {"sum": sm}
                if n >= 1:
                    inverse(n - 1)
                k1 = DV.op(lambda e: e.tensor_reduce(mx[:, 1:2], s_[:, 0:S], AX.X, ALU.max, negate=True), k)
                if n >= 1:
                    scale(n - 1, 0)
                k0 = DV.op(lambda e: e.tensor_reduce(mx[:, 0:1], s_[:, S:384], AX.X, ALU.max, negate=True), k)
                if n >= 1:
                    scale(n - 1, 1)
                w["exp"] = [AC.op(lambda e: e.activation(s_[:, 0:S], s_[:, 0:S], ACT.Exp, bias=mx[:, 1:2], accum_out=sm[:, 1:2]), k1),
                            AC.op(lambda e: e.activation(s_[:, S:384], s_[:, S:384], ACT.Exp, bias=mx[:, 0:1], accum_out=sm[:, 0:1]), k0)]
                w["gate"], w["scr"] = j["gate"], s_

            def inverse(n):
                w = work[n]
                sm = w["sum"]
                k = DV.op(lambda e: e.reciprocal(sm, sm), w["exp"])
                if w["gate"] is not None:
                    k = DV.op(lambda e: e.tensor_tensor(sm, sm, w["gate"], ALU.mult), k)
                w["inv"], w["scaled"] = k, []

            def scale(n, tile):
                w = work[n]
                part_ = w["scr"][:, 0:S] if tile == 0 else w["scr"][:, S:384]
                sm = w["sum"][:, 1 - tile:2 - tile]
                w["scaled"].append(DV.op(lambda e: e.tensor_scalar(part_, part_, sm, None, ALU.mult), w["inv"]))

            def turn(n):
                w, b = work[n], 4 + n % 2
                s_ = w["scr"]
                PE.wait(w["scaled"], free[b])
                PE.quiet(lambda e: e.transpose(ps[b][:, 0:P], s_[:, S:384], ident))
                PE.quiet(lambda e: e.transpose(ps[b][:, P:S], s_[:, 0:P], ident))
                t = scr_free[n] = PE.op(lambda e: e.transpose(ps[b][:, S:384], s_[:, P:S], ident))
                w["turned"] = AC.op(lambda e: e.activation(pT[n % 4], ps[b][:, 0:384], ACT.Copy), t, pT_free.get(n - 4))
                free[b] = [w["turned"]]

            for n in range(n_jobs + 5):
                if n >= 5:
                    pT_free[n - 5] = turned_to(n - 5, pT[(n - 5) % 4], work[n - 5]["turned"])
                if 3 <= n < n_jobs + 3:
                    turn(n - 3)
                if n < n_jobs:
                    scores(n)
                elif n == n_jobs:
                    inverse(n - 1)
                    scale(n - 1, 0)
                    scale(n - 1, 1)

        def out_and_residual(oh, ol, toks):
            k = by_tokens(lambda c: (oh[:, c, :], ol[:, c, :]), 8, [0, 1, 2, 3], toks, 8)
            return residual([0, 1, 2, 3], k, 1.0, X)

        def mixer_ab(toks):
            kr = rms_to(toks, I["norm_mix_2"][0])
            kx = transposed(R, kr)
            A = stage()
            qT, kT, oh, ol = A.take(8, S), A.take(8, S), A.take_r(8, S), A.take_r(8, S)
            V = R
            work = [A.take(512) for _ in range(4)]
            bias = [A.take(2, 384) for _ in range(3)]
            scr = [A.take(384) for _ in range(4)]
            pT = [A.take(384) for _ in range(4)]
            stats = [(S_(2), S_(2)) for _ in range(4)]
            fetch, k_bias, b_used = bias_loader(bias, 1, lambda p: 2 * p, lambda p: 0 if p < 4 else 1)
            for p in range(3):
                fetch(p)
            kq, kk, kv = {}, {}, {}
            turn = None
            for a in range(2):
                t, = by_token_cols([(0, 512, (4, 5))], kx)
                if turn:
                    turn()
                kq[a], turn = head_norm(512, hg[:, 2 * a:2 * a + 1], HD ** -0.5, qT[:, 4 * a:4 * a + 4, :], (4, 5), (6, 7), work[0:2], t)
                t, = by_token_cols([(0, 512, (0, 1))], kx)
                turn()
                kk[a], turn = head_norm(512, hg[:, 2 * a + 1:2 * a + 2], 1.0, kT[:, 4 * a:4 * a + 4, :], (0, 1), (6, 7), work[2:4], t)
                t, = by_token_cols([(0, 512, (2, 3))], kx)
                kv[a] = copied(512, lambda tt, a=a: V[:, tt, 512 * a:512 * a + 512], (2, 3), t)
            turn()
            table_of(ACT.Exp)
            ko = []

            def job(n):
                p, h = n // 2, n % 2
                r = slice(HD * h, HD * h + HD)

                def done_(k):
                    if h:
                        b_used[p] = k
                        if p + 3 < 8:
                            fetch(p + 3)
                return {"q": qT[r, p, :], "k": kT[r, p, :], "ready": kq[p // 4] + kk[p // 4], "bias": bias[p % 3][:, h, :],
                        "biased": k_bias[p], "done": done_, "gate": None}

            def weigh(n, pT_, k):
                p, h = n // 2, n % 2
                b = 6 + p % 2
                r = slice(HD * h, HD * h + HD)
                PE.wait(k, kv[p // 4], free[b] if h == 0 else None)
                PE.quiet(lambda e: e.matmul(ps[b][r, 0:S], V[:, 0, n * HD:n * HD + HD], pT_[:, 0:S], start=True, stop=False))
                t = PE.op(lambda e: e.matmul(ps[b][r, P:S], V[:, 1, n * HD:n * HD + HD], pT_[:, S:384], start=False, stop=True))
                if h:
                    k = part(ps[b][:, 0:S], oh[:, p, :], ol[:, p, :], t)
                    free[b] = [k]
                    ko.append(k)
                return t

            softmaxes(NH, job, weigh, scr, pT, stats)
            return out_and_residual(oh, ol, ko)

        def mixer_nsa(toks):
            kr = rms_to(toks, I["norm_mix_2"][1])
            kx = transposed(R, kr)
            A = stage()
            qT, oh, ol = A.take(8, S), A.take_r(8, S), A.take_r(8, S)
            early, ksT, kwT = A.take(2 * 5 * S), A.take(2, S), A.take(2, S)
            kvs_ = [shaped(early[:, 5 * S * j:5 * S * j + 5 * S], (5, S)) for j in range(2)]
            Vs, Vw = A.take(NT, S), A.take(NT, S)
            bias = [A.take(2, 384) for _ in range(3)]
            work = [A.take(768) for _ in range(2)]
            scr = [work[i // 2][:, 384 * (i % 2):384 * (i % 2) + 384] for i in range(4)]
            pT = [early[:, 384 * i:384 * i + 384] for i in range(4)]
            gw = A.take(DC, 48)
            gwhl, gsb = A.take_r(DC, 96), work[0][:, 0:512]
            cmp_ = A.take(227)
            w2, posT, cb = cmp_[:, 0:192], cmp_[:, 192:224], S_(8)
            b2b = A.take(HD)
            hidk, hidv = A.take(60), A.take(60)
            hidr = shaped(early[:, 2016:2528], (4, P))
            kcT = A.take(60)
            sq60, rs60 = A.take(60), A.take(60)
            vcr = A.take(4, HD)
            pc = R[:, 0, :].rearrange("p (a b) -> p a b", b=32)
            cs = shaped(early[:, 1536:2016], (NT * NH, NCMP))
            pcT = R[:, 1, :].rearrange("p (a b) -> p a b", b=S)
            gt = S_(NT, 48)
            stats = [(S_(2), S_(2)) for _ in range(4)]
            fetch, k_bias, b_used = bias_loader(bias, 4, lambda i: (i // 4) * 8 + i % 4, lambda i: 0)
            for p in range(3):
                fetch(p)
            PL.dma(lambda e: e.dma_start(gw, I["w_in_nsa_2"][0][:, 2560:2608].rearrange("(c p) n -> p c n", p=P)), c_sm)
            PL.dma(lambda e: e.dma_start(cmp_, I["cmp_small"]), c_sm)
            k_sm = PL.dma(lambda e: e.dma_start(b2b, I["cmp_v_b2_2"][0].partition_broadcast(P)), c_sm)

            k_cb = DV.op(lambda e: e.tensor_copy(cb[:, 0:3], cmp_[:, 224:227]), k_sm)
            kg = part(gw, gwhl[:, :, 0:48], gwhl[:, :, 48:96], k_sm)
            work2 = [R[:, tt, 0:512] for tt in range(NT)]
            k_kvc = [[], []]
            for j in range(2):
                v = kvs_[j]
                z = PL.op(lambda e, v=v: e.memset(v[:, 4, :], 0.0), PL.last())
                z2 = PL.op(lambda e, v=v: e.memset(v[HD:P, 0:4, S - 16:S], 0.0), z, k_kvc[j - 1][-1:])
                k_kvc[j] += [z2, PL.op(lambda e, v=v, j=j: e.tensor_copy(v[:, 4, 0:16], posT[:, 16 * j:16 * j + 16]), z2, k_sm)]
                ts = by_channels(2, (2, 3), kx)
                for h in range(2):
                    bank = ps[2 + h]
                    for gg in range(2):
                        g, r = 2 * h + gg, slice(HD * gg, HD * gg + HD)
                        a = AC.op(lambda e, v=v, g=g, r=r, bank=bank: e.activation(v[0:HD, g, :], bank[r, 0:S], ACT.Copy), ts[h])
                        k = DV.op(lambda e, v=v, g=g, r=r, bank=bank: e.tensor_copy(v[HD:P, g, 0:S - 16], bank[r, 16:S]), a)
                    free[2 + h] = [k]
                    k_kvc[j].append(k)
            t, = by_token_cols([(0, 512, (4, 5))], kx)
            kq0, turn = head_norm(512, hg[:, 4:5], HD ** -0.5, qT[:, 0:4, :], (4, 5), (6, 7), work, t)
            hid_k = []
            for j in range(2):
                n, = raw_slots(1)
                b = 3 - j
                w1 = ring[:, n % NRING, :].rearrange("p (l c) -> p l c", c=P)
                o = ps[b][:, 0:75].rearrange("p (g c) -> p g c", c=NCMP)
                for l in range(16):
                    rhs = kvs_[j][:, :, l:l + 225:16]
                    t = PE.op(lambda e, l=l, w1=w1, rhs=rhs, o=o: e.matmul(o, w1[:, l, :], rhs, start=(l == 0), stop=(l == 15)),
                              arrived(n), k_kvc[j], free[b])
                loads[n]["released"] = t
                kb = DV.op(lambda e, j=j, b=b: e.tensor_tensor(cb[:, 4 + j:5 + j], ps[b][:, 60:61], cb[:, j:j + 1], ALU.add), t, k_cb)
                hid = (hidk, hidv)[j]
                hid_k.append(AC.op(lambda e, j=j, b=b, hid=hid: e.activation(hid, ps[b][:, 0:60], ACT.Gelu_apprx_tanh, bias=cb[:, 4 + j:5 + j]), kb))
                free[b] = [hid_k[-1]]
            t, = by_token_cols([(0, 512, (0, 1))], kx)
            turn()
            kq1, turn = head_norm(512, hg[:, 4:5], HD ** -0.5, qT[:, 4:8, :], (0, 1), (6, 7), work2, t)
            t = PE.op(lambda e: e.matmul(ps[2][:, 0:60], w2[:, 0:P], hidk, start=True, stop=True), hid_k[0], free[2], k_sm)
            t = kraw = AC.op(lambda e: e.activation(kcT, ps[2][:, 0:60], ACT.Identity, bias=cb[:, 2:3]), t)
            k_sq = AC.op(lambda e: e.activation(sq60, kcT, ACT.Square), t)
            t0 = DV.op(lambda e: e.memset(hidr, 0.0), hid_k[1])
            h4 = hidr.rearrange("p g (i c) -> p g i c", i=4)[:, :, :, 0:NCMP]
            k_hr = DV.op(lambda e: e.tensor_copy(h4, hidv.rearrange("p (g c) -> p g c", c=NCMP).unsqueeze(2).to_broadcast([P, 4, 4, NCMP])), t0, hid_k[1])
            gp_ = ps[5][:, 0:96].rearrange("p (t n) -> p t n", t=NT)
            t = small_product(gwhl, 48, 3, gp_, [kx, kg, free[5]], gsb)
            k_gt = AC.op(lambda e: e.activation(gt, gp_, ACT.Sigmoid), t)
            free[5] = [k_gt]
            t, tv_ = by_token_cols([(0, 256, (4, 5)), (256, 256, (0, 1))], kx)
            turn()
            ks, turn = head_norm(256, hg[:, 6:7], 1.0, ksT, (4, 5), (6, 7), work, t)
            kvs = copied(256, lambda tt: Vs[:, tt, :], (0, 1), tv_)
            t = PE.op(lambda e: e.matmul(ps[2][:, 64:124], C("halves"), sq60, start=True, stop=True), k_sq)
            t = DV.op(lambda e: e.tensor_scalar(rs60, ps[2][:, 64:124], 1.0 / HD, RMS_EPS, ALU.mult, ALU.add), t)
            free[2] = [t]
            t = AC.op(lambda e: e.activation(rs60, rs60, ACT.Sqrt), t)
            t = DV.op(lambda e: e.reciprocal(rs60, rs60), t)
            k_kc = DV.op(lambda e: e.scalar_tensor_tensor(kcT, kcT, hg[:, 5:6], rs60, ALU.mult, ALU.mult), t, kraw)
            vp = ps[3][:, 0:256].rearrange("p (g d) -> p g d", d=HD)
            for g in range(4):
                t2 = PE.op(lambda e, g=g: e.matmul(vp[:, g, :], hidr[:, g, :], w2[:, 128:192], start=True, stop=True), k_hr, free[3])
            k_vc = DV.op(lambda e: e.tensor_tensor(vcr, vp, b2b.unsqueeze(1).to_broadcast([P, 4, HD]), ALU.add), t2, k_sm)
            free[3] = [k_vc]
            t, tv_ = by_token_cols([(0, 256, (4, 5)), (256, 256, (0, 1))], kx)
            turn()
            kw, turn = head_norm(256, hg[:, 7:8], 1.0, kwT, (4, 5), (6, 7), work, t)
            kvw = copied(256, lambda tt: Vw[:, tt, :], (0, 1), tv_)
            kq = [kq0, kq1]
            cp = [ps[2 + par][:, 0:NT * NH * NCMP].rearrange("p (a c) -> p a c", c=NCMP) for par in range(2)]
            for tt in range(NT):
                for h in range(NH):
                    g = h // 4
                    par, i, gi = g % 2, (g // 2) * 4 + h % 4, g
                    r = slice(HD * par, HD * par + HD)
                    t = PE.op(lambda e, tt=tt, h=h, par=par, r=r, i=i, gi=gi: e.matmul(
                        cp[par][:, tt * NH + h, :], qT[r, i, tt * P:tt * P + P], kcT[r, gi * NCMP:gi * NCMP + NCMP], start=True, stop=True),
                        free[2], free[3], k_kc, kq0, kq1)
            cm, cl = S_(NT * NH), S_(NT * NH)
            b3 = lambda v: v.unsqueeze(2).to_broadcast([P, NT * NH, NCMP])
            k = []
            by_par = lambda v, tt, par: v[:, tt * NH:tt * NH + NH, :].rearrange("p (a b j) c -> p a b j c", b=2, j=4)[:, :, par, :, :]
            for tt in range(NT):
                for par in range(2):
                    bt = btab[:, tt, :, :].rearrange("p c (a b j) -> p a b j c", b=2, j=4)[:, :, par, :, :]
                    k.append(DV.op(lambda e, tt=tt, par=par, bt=bt: e.tensor_tensor(by_par(cs, tt, par), by_par(cp[par], tt, par), bt, ALU.add), t))
            free[2] = free[3] = k
            t = DV.op(lambda e: e.tensor_reduce(cm, cs, AX.X, ALU.max), k)
            t = DV.op(lambda e: e.tensor_scalar(cm, cm, NEG / 10, None, ALU.max), t)
            t = DV.op(lambda e: e.tensor_tensor(cs, cs, b3(cm), ALU.subtract), t)
            t = AC.op(lambda e: e.activation(cs, cs, ACT.Exp), t)
            t = DV.op(lambda e: e.tensor_reduce(cl, cs, AX.X, ALU.add), t)
            t = DV.op(lambda e: e.tensor_scalar(cl, cl, 1e-30, None, ALU.max), t)
            t = DV.op(lambda e: e.reciprocal(cl, cl), t)
            g3 = gt.rearrange("p t (h b) -> p t h b", b=3)
            t = DV.op(lambda e: e.tensor_tensor(cl.rearrange("p (t h) -> p t h", t=NT), cl.rearrange("p (t h) -> p t h", t=NT), g3[:, :, :, 0], ALU.mult), t, k_gt)
            t0 = DV.op(lambda e: e.memset(pc, 0.0))
            kpc = DV.op(lambda e: e.tensor_tensor(pc[:, :, 0:NCMP], cs, b3(cl), ALU.mult), t, t0)
            turn()
            k_pc = []

            def turn_compressed():
                for g in range(4):
                    b = 6 + g % 2
                    for tt in range(NT):
                        i_ = pc[:, tt * NH + 4 * g:tt * NH + 4 * g + 4, :].rearrange("p a b -> p (a b)")
                        t = PE.op(lambda e, b=b, tt=tt, i_=i_: e.transpose(ps[b][:, tt * P:tt * P + P], i_, ident), kpc, free[b])
                    k = DV.op(lambda e, b=b, g=g: e.tensor_copy(pcT[:, g, :], ps[b][:, 0:S]), t)
                    free[b] = [k]
                    k_pc.append(k)

            ko = []

            def job(n):
                i, par, br = n // 4, n // 2 % 2, n % 2
                r = slice(HD * par, HD * par + HD)
                h = (i // 4) * 8 + par * 4 + i % 4
                kt, ktok = ((ksT, ks), (kwT, kw))[br]

                def done_(k):
                    if par and br:
                        b_used[i] = k
                        if i + 3 < 8:
                            fetch(i + 3)
                return {"q": qT[r, i, :], "k": kt[r, i // 4, :], "ready": kq[i // 4] + ktok, "bias": bias[i % 3][:, par, :],
                        "biased": k_bias[i], "done": done_, "gate": g3[:, :, h, 1 + br]}

            def weigh(n, pT_, k):
                i, par, br = n // 4, n // 2 % 2, n % 2
                g = (i // 4) * 2 + par
                b = 6 + i % 2
                r = slice(HD * par, HD * par + HD)
                vv, vt = ((Vs, kvs), (Vw, kvw))[br]
                if n == 0:
                    turn_compressed()
                PE.wait(k, vt, free[b] if par == 0 and br == 0 else None)
                if br == 0:
                    hi = i % 4
                    q = slice(32 * hi, 32 * hi + 32)
                    PE.quiet(lambda e: e.matmul(ps[b][r, 0:S], vcr[q, g, :], pcT[q, g, :], start=True, stop=False), k_pc, k_vc)
                PE.quiet(lambda e: e.matmul(ps[b][r, 0:S], vv[:, 0, g * HD:g * HD + HD], pT_[:, 0:S], start=False, stop=False))
                t = PE.op(lambda e: e.matmul(ps[b][r, P:S], vv[:, 1, g * HD:g * HD + HD], pT_[:, S:384], start=False, stop=(br == 1)))
                if par and br:
                    k = part(ps[b][:, 0:S], oh[:, i, :], ol[:, i, :], t)
                    free[b] = [k]
                    ko.append(k)
                return t

            softmaxes(32, job, weigh, scr, pT, stats)
            return out_and_residual(oh, ol, ko)

        def swiglu(layer, toks):
            kr = rms_to(toks, I["norm_ffn_2"][layer])
            kx = transposed(R, kr)
            A = stage()
            hh, hl = [A.take_r(2, S) for _ in range(2)], [A.take_r(2, S) for _ in range(2)]
            sil = [A.take(2, S) for _ in range(2)]
            prod = [A.take(2, S) for _ in range(2)]
            kh, ka, used = {}, {}, [None, None]
            for j in range(FC // 2 + 1):
                i = j % 2
                if j < FC // 2:
                    tg = by_channels(2, (4, 5), kx)
                    tu = by_channels(2, (6, 7), kx)
                    a = []
                    for h in range(2):
                        a.append(AC.op(lambda e, i=i, h=h: e.activation(sil[i][:, h, :], ps[4 + h][:, 0:S], ACT.Silu), tg[h], ka.get(j - 2)))
                        free[4 + h] = [a[h]]
                    for h in range(2):
                        k = DV.op(lambda e, i=i, h=h: e.tensor_tensor(prod[i][:, h, :], sil[i][:, h, :], ps[6 + h][:, 0:S], ALU.mult), a[h], tu[h], kh.get(j - 2))
                        free[6 + h] = [k]
                    ka[j] = k
                if j >= 1:
                    o = 1 - i
                    k = by_tokens(lambda c: (hh[o][:, c % 2, :], hl[o][:, c % 2, :]), 2, [0, 1, 2, 3], kh[j - 1], FC, 2 * (j - 1))
                    used[o] = PE.last()
                if j < FC // 2:
                    kh[j] = part(prod[i], hh[i], hl[i], [ka[j], used[i]])
            return residual([0, 1, 2, 3], k, 1.0, X)

        def ple(layer, toks):
            kr = rms_to(toks, I["norm_ple_2"][layer])
            kx = transposed(R, kr)
            A = stage()
            G = A.take(NT, D)
            pf, ph, pl_ = A.take(2, S), A.take_r(2, S), A.take_r(2, S)
            kp = PL.dma(lambda e: e.dma_start(pf, I["p_2"][layer].rearrange("(c p) n -> p c n", p=P)), c_sm)
            kp = part(pf, ph, pl_, kp)
            k = by_tokens(lambda c: (XH[:, c, :], XL[:, c, :]), 8, [4, 5, 6, 7], kx, 8)
            ka = []
            for tt in range(NT):
                for h in range(2):
                    b = 4 + 2 * tt + h
                    ka.append(AC.op(lambda e, tt=tt, h=h, b=b: e.activation(G[:, tt, h * 512:h * 512 + 512], ps[b][:, :], ACT.Sigmoid), k[2 * tt + h]))
                    free[b] = [ka[-1]]
            k = by_tokens(lambda c: (ph[:, c, :], pl_[:, c, :]), 2, [0, 1, 2, 3], [kp], 2)
            r = []
            for tt in range(NT):
                for h in range(2):
                    b = 2 * tt + h
                    sl = slice(h * 512, h * 512 + 512)
                    t = DV.op(lambda e, tt=tt, b=b, sl=sl: e.tensor_tensor(G[:, tt, sl], G[:, tt, sl], ps[b][:, :], ALU.mult), ka[b], k[b])
                    free[b] = [t]
                    r.append(DV.op(lambda e, tt=tt, sl=sl: e.tensor_tensor(X[:, tt, sl], X[:, tt, sl], G[:, tt, sl], ALU.add), t))
            return r

        t = conv_mixer()
        gb = load_rows(I["ln_mix_g"][0], I["ln_mix_b"][0])
        t = layer_norm(t, gb)
        gb = load_rows(I["ln_ffn_g"][0], I["ln_ffn_b"][0])
        t = moe(0, t)
        t = layer_norm(t, gb)
        gb = load_rows(I["ln_mix_g"][1], I["ln_mix_b"][1])
        t = stick(t)
        t = layer_norm(t, gb)
        gb = load_rows(I["ln_ffn_g"][1], I["ln_ffn_b"][1])
        t = moe(1, t)
        t = layer_norm(t, gb)
        for layer in range(DEPTH):
            t = mixer_ab(t) if layer == 0 else mixer_nsa(t)
            t = swiglu(layer, t)
            t = ple(layer, t)
        assert taken[0] == len(pieces) and next_raw[0] == len(raw)

        for n, l in enumerate(loads):
            if n in sp_branch:
                branch, rows_in = sp_branch[n]
                put_branch(SP, branch)
                SP.wait(rows_in)
            i = n % NRING
            if n >= NRING:
                SP.wait(loads[n - NRING]["released"])
            for view, src in l["parts"]:
                view = view(ring[:, i, :])
                SP.items.append(("inc", lambda e, view=view, src=src: e.dma_start(view, src), c_ring[i].sem, 16))
        SP.dma(lambda e: e.dma_start(out[0].rearrange("(t p) d -> p t d", p=P), X[:, :, :]), c_out, t)
        SP.wait((c_out.sem, 16))

        block = ctx.enter_context(nc.Block())
        block.sync(lambda e: SP.play(e))
        block.scalar(lambda e: AC.play(e))
        block.vector(lambda e: DV.play(e))
        block.gpsimd(lambda e: PL.play(e))
        block.tensor(lambda e: PE.play(e))


def put_branch(q, what):
    ready, cond, body = what
    q.wait(ready)
    q.items.append(("if", cond, body))


_PLAIN = ["x", "even_w_in", "even_w_out", "odd_w_qkv", "odd_w_o", "ln_mix_g", "ln_mix_b", "ln_ffn_g", "ln_ffn_b",
          "expert_w_up", "expert_w_down", "rel_bias_2",
          "w_ffn_gate_2", "w_ffn_up_2", "w_ffn_down_2", "w_ple_proj_2", "w_ple_gate_2", "w_in_ab_2", "w_out_ab_2",
          "cmp_k_w1_2", "cmp_v_w1_2", "cmp_v_b2_2", "norm_mix_2", "norm_ffn_2", "norm_ple_2"]
_HEAD_GAINS = ["qn_moba_2", "kn_moba_2", "qn_dil_2", "kn_dil_2", "qn_nsa_2", "kn_cmp_2", "kn_slc_2", "kn_win_2"]


def kernel(**inputs):
    import numpy as _np
    import concourse.bacc as _bacc
    from concourse import mybir as _mybir
    from concourse.bass_utils import run_bass_kernel_spmd as _run

    a = {n: _np.ascontiguousarray(inputs[n]) for n in _PLAIN}
    asis = {n: _np.asarray(inputs[n]) for n in inputs}
    chan = lambda v: _np.asarray(v).reshape(-1, 128).T
    twice = lambda v: _np.concatenate([v, v], axis=0)
    a["conv_taps"] = _np.ascontiguousarray(_np.concatenate(
        [asis["even_conv_b_w"][0].reshape(31, 4, 128).transpose(2, 1, 0), asis["even_conv_a"][0].reshape(3, 4, 128).transpose(2, 1, 0)]
        + [chan(asis[n][0])[:, :, None] for n in ("even_conv_b_bias", "even_norm_b_g", "even_norm_b_b")], axis=2))
    a["head_gains"] = _np.ascontiguousarray(_np.stack([twice(asis[n][0]) for n in _HEAD_GAINS], axis=1))
    a["cmp_small"] = _np.ascontiguousarray(_np.concatenate(
        [asis["cmp_k_w2_2"][0], asis["cmp_k_w2_2"][0], asis["cmp_v_w2_2"][0],
        ] + [asis[n][0].reshape(2, 16, 64).transpose(0, 2, 1).reshape(128, 16) for n in ("cmp_k_pos_2", "cmp_v_pos_2")] + [
         asis["cmp_k_b1_2"][0][:, None], asis["cmp_v_b1_2"][0][:, None], twice(asis["cmp_k_b2_2"][0])[:, None]], axis=1))
    a["router_w"] = _np.ascontiguousarray(
        _np.concatenate([asis["router_group_w"], asis["router_expert_w"]], axis=2).reshape(2, 8, 128, 36).transpose(2, 0, 1, 3))
    a["router_b"] = _np.concatenate([asis["router_group_b"], asis["router_expert_b"]], axis=1)
    a["p_2"] = _np.ascontiguousarray(asis["p_2"][:, 0].transpose(0, 2, 1))
    w = asis["w_in_nsa_2"]
    q = w[:, :, :1024].reshape(1, 1024, 2, 2, 4, 64).transpose(0, 1, 2, 4, 3, 5).reshape(1, 1024, 1024)
    a["w_in_nsa_2"] = _np.concatenate([q, w[:, :, 1024:]], axis=2)
    a["w_out_nsa_2"] = _np.ascontiguousarray(
        asis["w_out_nsa_2"].reshape(1, 2, 2, 4, 64, 1024).transpose(0, 1, 3, 2, 4, 5).reshape(1, 1024, 1024))
    a["consts"] = CONSTS
    a["bias_tables"] = BIAS_TABLES

    nc = _bacc.Bacc("TRN2", target_bir_lowering=False, num_devices=1)
    arrays, aps = {}, {}
    for n, v in a.items():
        arrays[f"in_{n}"] = v
        aps[n] = nc.dram_tensor(f"in_{n}", v.shape, _mybir.dt.from_np(v.dtype), kind="ExternalInput").ap()
    out = nc.dram_tensor("out_0", (1, 256, 1024), _mybir.dt.float32, kind="ExternalOutput").ap()
    bass_two_blocks_kernel(nc, aps, out)
    r = _run(nc, [arrays], core_ids=[0])
    return r.results[0]["out_0"]
```
